# Optimizing a Trainium2 kernel written in Bass

```python
import jax, jax.numpy as jnp
from jax import lax
import numpy as np

D_MODEL = 1024
BATCH = 1
SEQ = 256
DEPTH = 1

CHUNK = 64
MEM_LEN = 256
FOX_HEADS = 8
FOX_HEAD_DIM = 64
FOX_WIDTH = FOX_HEADS * FOX_HEAD_DIM
POOL_WIDTH = D_MODEL - FOX_WIDTH
POOL_WINDOWS = (2, 4, 8, 16)
POOL_GROUPS = len(POOL_WINDOWS)
POOL_GROUP_DIM = POOL_WIDTH // POOL_GROUPS
IN_COLS = 3 * FOX_WIDTH + POOL_WIDTH + FOX_HEADS
MEM_HEADS = 4
MEM_HEAD_DIM = 128
MEM_WIDTH = MEM_HEADS * MEM_HEAD_DIM
D_FF = ((-(-8 * D_MODEL // 3) + 255) // 256) * 256
Q_BLOCK = 128
EPS = 1e-6


def rmsnorm(x, g):
    xf = x.astype(jnp.float32)
    y = xf * lax.rsqrt(jnp.mean(xf * xf, axis=-1, keepdims=True) + EPS)
    return (y * g.astype(jnp.float32)).astype(x.dtype)

def forgetting_attention(q, k, v, f_logit):
    c = jnp.cumsum(jax.nn.log_sigmoid(f_logit.astype(jnp.float32)), axis=-1)
    scale = FOX_HEAD_DIM ** -0.5
    S = q.shape[2]
    outs = []
    for start in range(0, S, Q_BLOCK):
        end = start + Q_BLOCK
        qb = q[:, :, start:end]
        kb = k[:, :, :end]
        vb = v[:, :, :end]
        s = jnp.einsum('bhqd,bhkd->bhqk', qb, kb, preferred_element_type=jnp.float32) * scale
        s = s + c[:, :, start:end, None] - c[:, :, None, :end]
        qpos = start + jnp.arange(Q_BLOCK)
        kpos = jnp.arange(end)
        s = jnp.where(kpos[None, :] <= qpos[:, None], s, -jnp.inf)
        p = jax.nn.softmax(s, axis=-1)
        outs.append(jnp.einsum('bhqk,bhkd->bhqd', p.astype(vb.dtype), vb))
    return jnp.concatenate(outs, axis=2)

def multiscale_pool(p, w_pool, pool_scale):
    B, S, _ = p.shape
    pf = p.astype(jnp.float32).reshape(B, S, POOL_GROUPS, POOL_GROUP_DIM)
    cs = jnp.concatenate([jnp.zeros((B, 1, POOL_GROUPS, POOL_GROUP_DIM), jnp.float32),
                          jnp.cumsum(pf, axis=1)], axis=1)
    t = jnp.arange(S)
    outs = []
    for g, w in enumerate(POOL_WINDOWS):
        csg = cs[:, :, g]
        lower = jnp.pad(csg, ((0, 0), (w - 1, 0), (0, 0)))[:, :S]
        cnt = jnp.minimum(t + 1, w).astype(jnp.float32)[None, :, None]
        mixed = (csg[:, 1:] - lower) / cnt - pf[:, :, g]
        outs.append(jnp.einsum('bsc,cd->bsd', mixed, w_pool[g].astype(jnp.float32)))
    y = jnp.concatenate(outs, axis=-1) * pool_scale.astype(jnp.float32)
    return y.astype(p.dtype)

def head_split(t, n_heads, head_dim):
    B, S, _ = t.shape
    return t.reshape(B, S, n_heads, head_dim)

def first_inputs(seed: int = 0) -> dict:
    key = jax.random.key(seed)
    ks = jax.random.split(key, 24)
    f32 = jnp.float32
    D = D_MODEL

    def nrm(k, shape, fan_in):
        return jax.random.normal(k, shape, f32) * (fan_in ** -0.5)

    def gain(k, shape):
        return 1.0 + 0.05 * jax.random.normal(k, shape, f32)

    return {
        "x": jax.random.normal(ks[0], (BATCH, SEQ, D), f32),
        "mem": jax.random.normal(ks[1], (BATCH, MEM_LEN, D), f32),
        "g_mix": gain(ks[2], (DEPTH, D)),
        "w_in": nrm(ks[3], (DEPTH, D, IN_COLS), D),
        "b_forget": 3.0 + 0.5 * jax.random.normal(ks[4], (DEPTH, FOX_HEADS), f32),
        "g_q_fox": gain(ks[5], (DEPTH, FOX_HEAD_DIM)),
        "g_k_fox": gain(ks[6], (DEPTH, FOX_HEAD_DIM)),
        "w_pool": nrm(ks[7], (DEPTH, POOL_GROUPS, POOL_GROUP_DIM, POOL_GROUP_DIM), POOL_GROUP_DIM),
        "pool_scale": gain(ks[8], (DEPTH, POOL_WIDTH)),
        "w_out": nrm(ks[9], (DEPTH, D, D), D),
        "g_mem_q": gain(ks[10], (DEPTH, D)),
        "g_mem_kv": gain(ks[11], (DEPTH, D)),
        "w_mem_q": nrm(ks[12], (DEPTH, D, MEM_WIDTH), D),
        "w_mem_kv": nrm(ks[13], (DEPTH, D, 2 * MEM_WIDTH), D),
        "g_q_mem": gain(ks[14], (DEPTH, MEM_HEAD_DIM)),
        "g_k_mem": gain(ks[15], (DEPTH, MEM_HEAD_DIM)),
        "w_mem_out": nrm(ks[16], (DEPTH, MEM_WIDTH, D), MEM_WIDTH),
        "g_ffn": gain(ks[17], (DEPTH, D)),
        "w_gate_up": nrm(ks[18], (DEPTH, D, 2 * D_FF), D),
        "w_down": nrm(ks[19], (DEPTH, D_FF, D), D_FF),
    }

def first_block(x, mem, g_mix, w_in, b_forget, g_q_fox, g_k_fox, w_pool, pool_scale, w_out,
              g_mem_q, g_mem_kv, w_mem_q, w_mem_kv, g_q_mem, g_k_mem, w_mem_out,
              g_ffn, w_gate_up, w_down):
    B, S, _ = x.shape
    h = x
    for l in range(DEPTH):
        xn = rmsnorm(h, g_mix[l])
        z = jnp.einsum('bsd,dc->bsc', xn, w_in[l])
        q = z[..., :FOX_WIDTH]
        k = z[..., FOX_WIDTH:2 * FOX_WIDTH]
        v = z[..., 2 * FOX_WIDTH:3 * FOX_WIDTH]
        p_in = z[..., 3 * FOX_WIDTH:3 * FOX_WIDTH + POOL_WIDTH]
        f_logit = z[..., 3 * FOX_WIDTH + POOL_WIDTH:] + b_forget[l]
        q = rmsnorm(head_split(q, FOX_HEADS, FOX_HEAD_DIM), g_q_fox[l]).transpose(0, 2, 1, 3)
        k = rmsnorm(head_split(k, FOX_HEADS, FOX_HEAD_DIM), g_k_fox[l]).transpose(0, 2, 1, 3)
        v = head_split(v, FOX_HEADS, FOX_HEAD_DIM).transpose(0, 2, 1, 3)
        fox = forgetting_attention(q, k, v, f_logit.transpose(0, 2, 1))
        fox = fox.transpose(0, 2, 1, 3).reshape(B, S, FOX_WIDTH)
        pool = multiscale_pool(p_in, w_pool[l], pool_scale[l])
        h = h + jnp.einsum('bsc,cd->bsd', jnp.concatenate([fox, pool], axis=-1), w_out[l])

        hn = rmsnorm(h, g_mem_q[l])
        mn = rmsnorm(mem, g_mem_kv[l])
        mq = rmsnorm(head_split(jnp.einsum('bsd,dc->bsc', hn, w_mem_q[l]), MEM_HEADS, MEM_HEAD_DIM), g_q_mem[l])
        mkv = jnp.einsum('bmd,dc->bmc', mn, w_mem_kv[l])
        mk = rmsnorm(head_split(mkv[..., :MEM_WIDTH], MEM_HEADS, MEM_HEAD_DIM), g_k_mem[l])
        mv = head_split(mkv[..., MEM_WIDTH:], MEM_HEADS, MEM_HEAD_DIM)
        sc = jnp.einsum('bshd,bmhd->bhsm', mq, mk, preferred_element_type=jnp.float32) * (MEM_HEAD_DIM ** -0.5)
        pm = jax.nn.softmax(sc, axis=-1).astype(mv.dtype)
        mo = jnp.einsum('bhsm,bmhd->bshd', pm, mv).reshape(B, S, MEM_WIDTH)
        h = h + jnp.einsum('bsc,cd->bsd', mo, w_mem_out[l])

        hn = rmsnorm(h, g_ffn[l])
        gu = jnp.einsum('bsd,df->bsf', hn, w_gate_up[l])
        act = jax.nn.silu(gu[..., :D_FF]) * gu[..., D_FF:]
        h = h + jnp.einsum('bsf,fd->bsd', act, w_down[l])
    return h


SB_WIDTH = D_MODEL // 2
SB_HEAD_DIM = 64
SB_HEADS = SB_WIDTH // SB_HEAD_DIM
ML_WIDTH = D_MODEL - SB_WIDTH
ML_HEADS = 4
ML_HEAD_DIM = ML_WIDTH // ML_HEADS
MIX_WIDTH = SB_WIDTH + ML_WIDTH
CONV_WIDTH = 4
IN_SIZES = (SB_WIDTH, SB_WIDTH, SB_WIDTH, 2 * ML_WIDTH, ML_WIDTH, ML_WIDTH, ML_HEADS, ML_HEADS)
IN_WIDTH = 3 * SB_WIDTH + 4 * ML_WIDTH + 2 * ML_HEADS
PEER_HEADS = 8
PEER_NKEYS = 128
PEER_EXPERTS = PEER_NKEYS * PEER_NKEYS
PEER_TOPK = 16
PEER_QDIM = 256
PEER_HALF = PEER_QDIM // 2
PEER_TOKEN_BLOCK = 128
N_MOD = 6


def rms_norm(x, g):
    x32 = x.astype(jnp.float32)
    y = x32 * lax.rsqrt(jnp.mean(x32 * x32, axis=-1, keepdims=True) + EPS)
    return (y * g.astype(jnp.float32)).astype(x.dtype)

def causal_depthwise_conv(x, w):
    return lax.conv_general_dilated(
        x, w[:, None, :].astype(x.dtype), window_strides=(1,),
        padding=[(CONV_WIDTH - 1, 0)], dimension_numbers=('NWC', 'WIO', 'NWC'),
        feature_group_count=x.shape[-1])

def stick_breaking(q, k, v):
    s_len, d = q.shape[2], q.shape[-1]
    scale = d ** -0.5
    outs = []
    for t0 in range(0, s_len, Q_BLOCK):
        t1 = t0 + Q_BLOCK
        z = jnp.einsum('bhtd,bhsd->bhts', q[:, :, t0:t1], k[:, :, :t1]).astype(jnp.float32) * scale
        visible = jnp.arange(t1)[None, :] < jnp.arange(t0, t1)[:, None]
        log_keep = jnp.where(visible, jax.nn.log_sigmoid(-z), 0.0)
        log_between = lax.cumsum(log_keep, axis=3, reverse=True) - log_keep
        w = jnp.where(visible, jnp.exp(jax.nn.log_sigmoid(z) + log_between), 0.0)
        outs.append(jnp.einsum('bhts,bhsd->bhtd', w, v[:, :, :t1].astype(jnp.float32)))
    return jnp.concatenate(outs, axis=2).astype(v.dtype)

def mlstm(q, k, v, i_pre, f_pre):
    b, nh, s_len, d = q.shape
    nc = s_len // CHUNK
    f32 = jnp.float32

    def to_chunks(t):
        t = t.reshape((b, nh, nc, CHUNK) + t.shape[3:])
        return jnp.moveaxis(t, 2, 0)

    qc = to_chunks(q.astype(f32))
    kc = to_chunks(k.astype(f32) * (d ** -0.5))
    vc = to_chunks(v.astype(f32))
    a = jnp.cumsum(to_chunks(jax.nn.log_sigmoid(f_pre.astype(f32))), axis=-1)
    li = to_chunks(i_pre.astype(f32))
    causal = jnp.tril(jnp.ones((CHUNK, CHUNK), dtype=bool))

    def step(carry, inp):
        c_state, n_state, m_state = carry
        q_c, k_c, v_c, a_c, i_c = inp
        log_d = jnp.where(causal, a_c[..., :, None] - a_c[..., None, :] + i_c[..., None, :], -jnp.inf)
        log_inter = a_c + m_state[..., None]
        m_row = jnp.maximum(jnp.max(log_d, axis=-1), log_inter)
        w_intra = jnp.exp(log_d - m_row[..., None])
        w_inter = jnp.exp(log_inter - m_row)
        s_qk = jnp.einsum('bhtk,bhsk->bhts', q_c, k_c) * w_intra
        num = (jnp.einsum('bhts,bhsv->bhtv', s_qk, v_c)
               + w_inter[..., None] * jnp.einsum('bhvk,bhtk->bhtv', c_state, q_c))
        den = jnp.sum(s_qk, axis=-1) + w_inter * jnp.einsum('bhk,bhtk->bht', n_state, q_c)
        h = num / jnp.maximum(jnp.abs(den), jnp.exp(-m_row))[..., None]
        a_end = a_c[..., -1]
        log_w = a_end[..., None] - a_c + i_c
        m_new = jnp.maximum(a_end + m_state, jnp.max(log_w, axis=-1))
        w_s = jnp.exp(log_w - m_new[..., None])
        decay = jnp.exp(a_end + m_state - m_new)
        c_new = decay[..., None, None] * c_state + jnp.einsum('bhs,bhsv,bhsk->bhvk', w_s, v_c, k_c)
        n_new = decay[..., None] * n_state + jnp.einsum('bhs,bhsk->bhk', w_s, k_c)
        return (c_new, n_new, m_new), h

    init = (jnp.zeros((b, nh, d, d), f32), jnp.zeros((b, nh, d), f32), jnp.zeros((b, nh), f32))
    _, h = lax.scan(step, init, (qc, kc, vc, a, li))
    h = jnp.moveaxis(h, 0, 2).reshape(b, nh, s_len, d)
    return h.astype(v.dtype)

def peer(h, w_q, sub_keys, expert_u, expert_v):
    b, s_len, d = h.shape
    q = jnp.einsum('bsd,dq->bsq', h, w_q).reshape(b, s_len, PEER_HEADS, 2, PEER_HALF)
    scores = jnp.einsum('bshpc,hpnc->bshpn', q, sub_keys).astype(jnp.float32)
    top_s, top_i = lax.top_k(scores, PEER_TOPK)
    cand_s = (top_s[..., 0, :, None] + top_s[..., 1, None, :]).reshape(b, s_len, PEER_HEADS, PEER_TOPK * PEER_TOPK)
    cand_i = (top_i[..., 0, :, None] * PEER_NKEYS + top_i[..., 1, None, :]).reshape(b, s_len, PEER_HEADS, PEER_TOPK * PEER_TOPK)
    best_s, best_pos = lax.top_k(cand_s, PEER_TOPK)
    best_i = jnp.take_along_axis(cand_i, best_pos, axis=-1)
    gate = jax.nn.softmax(best_s, axis=-1)
    n_sel = PEER_HEADS * PEER_TOPK
    nb = (b * s_len) // PEER_TOKEN_BLOCK
    xs = h.reshape(nb, PEER_TOKEN_BLOCK, d)
    idx = best_i.reshape(nb, PEER_TOKEN_BLOCK, n_sel)
    gs = gate.reshape(nb, PEER_TOKEN_BLOCK, n_sel)

    def token_block(args):
        xb, ib, gb = args
        u = jnp.take(expert_u, ib, axis=0)
        act = jax.nn.gelu(jnp.einsum('td,tkd->tk', xb, u).astype(jnp.float32), approximate=False)
        vv = jnp.take(expert_v, ib, axis=0)
        return jnp.einsum('tk,tkd->td', (gb * act).astype(h.dtype), vv)

    y = lax.map(token_block, (xs, idx, gs))
    return y.reshape(b, s_len, d)

def second_inputs(seed: int = 0) -> dict:
    key = jax.random.key(seed)
    ks = jax.random.split(key, 20)
    nrm = jax.random.normal
    D = D_MODEL
    return {
        "x": nrm(ks[0], (BATCH, SEQ, D), jnp.float32),
        "c": nrm(ks[1], (BATCH, D), jnp.float32),
        "w_ada": nrm(ks[2], (DEPTH, D, N_MOD * D), jnp.float32) * (0.5 * D ** -0.5),
        "b_ada": nrm(ks[3], (DEPTH, N_MOD * D), jnp.float32) * 0.02,
        "g_norm1": 1.0 + 0.02 * nrm(ks[4], (DEPTH, D), jnp.float32),
        "w_in": nrm(ks[5], (DEPTH, D, IN_WIDTH), jnp.float32) * D ** -0.5,
        "b_igate": 0.1 * nrm(ks[6], (DEPTH, ML_HEADS), jnp.float32),
        "b_fgate": 3.0 + 3.0 * jax.random.uniform(ks[7], (DEPTH, ML_HEADS), jnp.float32),
        "conv_w": nrm(ks[8], (DEPTH, CONV_WIDTH, 2 * ML_WIDTH), jnp.float32) * CONV_WIDTH ** -0.5,
        "g_q_sb": 1.0 + 0.02 * nrm(ks[9], (DEPTH, SB_HEAD_DIM), jnp.float32),
        "g_k_sb": 1.0 + 0.02 * nrm(ks[10], (DEPTH, SB_HEAD_DIM), jnp.float32),
        "g_out_sb": 1.0 + 0.02 * nrm(ks[11], (DEPTH, SB_HEADS, SB_HEAD_DIM), jnp.float32),
        "g_out_ml": 1.0 + 0.02 * nrm(ks[12], (DEPTH, ML_HEADS, ML_HEAD_DIM), jnp.float32),
        "w_out": nrm(ks[13], (DEPTH, MIX_WIDTH, D), jnp.float32) * MIX_WIDTH ** -0.5,
        "g_norm2": 1.0 + 0.02 * nrm(ks[14], (DEPTH, D), jnp.float32),
        "w_q_peer": nrm(ks[15], (DEPTH, D, PEER_HEADS * PEER_QDIM), jnp.float32) * D ** -0.5,
        "sub_keys": nrm(ks[16], (DEPTH, PEER_HEADS, 2, PEER_NKEYS, PEER_HALF), jnp.float32) * PEER_HALF ** -0.5,
        "expert_u": nrm(ks[17], (DEPTH, PEER_EXPERTS, D), jnp.float32) * D ** -0.5,
        "expert_v": nrm(ks[18], (DEPTH, PEER_EXPERTS, D), jnp.float32),
    }

def second_block(x, c, w_ada, b_ada, g_norm1, w_in, b_igate, b_fgate, conv_w, g_q_sb, g_k_sb,
              g_out_sb, g_out_ml, w_out, g_norm2, w_q_peer, sub_keys, expert_u, expert_v):
    b, s_len, _ = x.shape
    cuts = []
    acc = 0
    for size in IN_SIZES[:-1]:
        acc += size
        cuts.append(acc)

    def to_heads(t, n):
        return t.reshape(b, s_len, n, -1).transpose(0, 2, 1, 3)

    for l in range(DEPTH):
        mod = jnp.einsum('bd,dm->bm', jax.nn.silu(c), w_ada[l]) + b_ada[l]
        shift1, scale1, gate1, shift2, scale2, gate2 = jnp.split(mod[:, None, :], N_MOD, axis=-1)

        h = rms_norm(x, g_norm1[l]) * (1 + scale1) + shift1
        proj = jnp.einsum('bsd,dn->bsn', h, w_in[l])
        q_sb, k_sb, v_sb, qk_ml, v_ml, o_ml, i_ml, f_ml = jnp.split(proj, cuts, axis=-1)

        q_sb = rms_norm(to_heads(q_sb, SB_HEADS), g_q_sb[l])
        k_sb = rms_norm(to_heads(k_sb, SB_HEADS), g_k_sb[l])
        y_sb = stick_breaking(q_sb, k_sb, to_heads(v_sb, SB_HEADS)).transpose(0, 2, 1, 3)
        y_sb = rms_norm(y_sb, g_out_sb[l])

        qk_ml = jax.nn.silu(causal_depthwise_conv(qk_ml, conv_w[l]))
        q_ml, k_ml = jnp.split(qk_ml, 2, axis=-1)
        i_pre = (i_ml + b_igate[l]).transpose(0, 2, 1)
        f_pre = (f_ml + b_fgate[l]).transpose(0, 2, 1)
        y_ml = mlstm(to_heads(q_ml, ML_HEADS), to_heads(k_ml, ML_HEADS), to_heads(v_ml, ML_HEADS), i_pre, f_pre)
        y_ml = rms_norm(y_ml.transpose(0, 2, 1, 3), g_out_ml[l]) * jax.nn.sigmoid(o_ml).reshape(b, s_len, ML_HEADS, ML_HEAD_DIM)

        mixed = jnp.concatenate([y_sb.reshape(b, s_len, SB_WIDTH), y_ml.reshape(b, s_len, ML_WIDTH)], axis=-1)
        x = x + gate1 * jnp.einsum('bsm,md->bsd', mixed, w_out[l])

        h2 = rms_norm(x, g_norm2[l]) * (1 + scale2) + shift2
        x = x + gate2 * peer(h2, w_q_peer[l], sub_keys[l], expert_u[l], expert_v[l])
    return x


def setup_inputs(seed=0):
    out = dict(first_inputs(seed))
    for name, value in second_inputs(seed + 1).items():
        if name != "x":
            out[name + "_2"] = value
    return out


def reference(
    x, mem, g_mix, w_in, b_forget, g_q_fox, g_k_fox, w_pool, pool_scale, w_out, g_mem_q,
    g_mem_kv, w_mem_q, w_mem_kv, g_q_mem, g_k_mem, w_mem_out, g_ffn, w_gate_up, w_down, c_2,
    w_ada_2, b_ada_2, g_norm1_2, w_in_2, b_igate_2, b_fgate_2, conv_w_2, g_q_sb_2, g_k_sb_2,
    g_out_sb_2, g_out_ml_2, w_out_2, g_norm2_2, w_q_peer_2, sub_keys_2, expert_u_2, expert_v_2,
):
    x = first_block(
        x, mem, g_mix, w_in, b_forget, g_q_fox, g_k_fox, w_pool, pool_scale, w_out, g_mem_q,
        g_mem_kv, w_mem_q, w_mem_kv, g_q_mem, g_k_mem, w_mem_out, g_ffn, w_gate_up, w_down,
    )
    return second_block(
        x, c_2, w_ada_2, b_ada_2, g_norm1_2, w_in_2, b_igate_2, b_fgate_2, conv_w_2, g_q_sb_2,
        g_k_sb_2, g_out_sb_2, g_out_ml_2, w_out_2, g_norm2_2, w_q_peer_2, sub_keys_2,
        expert_u_2, expert_v_2,
    )


_drawn_inputs = setup_inputs


def setup_inputs(seed=0):
    import zlib

    import numpy as np

    out = dict(_drawn_inputs(seed))
    spreads = {}
    factors = {'g_q_fox': 3.58,
     'g_k_fox': 3.631,
     'g_mem_q': 6.003,
     'g_mem_kv': 4.35,
     'g_q_mem': 5.512,
     'g_k_mem': 5.226,
     'g_norm1_2': 6.336,
     'b_igate_2': 64.0,
     'g_q_sb_2': 8.0,
     'g_k_sb_2': 23.821,
     'g_out_sb_2': 47.427,
     'g_out_ml_2': 64.0,
     'g_norm2_2': 14.076}
    for name, (base, spread) in spreads.items():
        noise = np.random.default_rng([zlib.crc32(name.encode()), seed]).standard_normal(out[name].shape)
        drawn = base * np.exp(spread * noise) if base else spread * noise
        out[name] = __import__('jax').numpy.asarray(drawn.astype(out[name].dtype))
    for name, factor in factors.items():
        out[name] = (out[name] * factor).astype(out[name].dtype)
    return out
```

```python
import numpy as np
from contextlib import ExitStack, contextmanager

import concourse.bass as bass
from concourse import mybir

P = 128
S = 256
TB = S // P
D = 1024
KT = D // P
SLAB = 2048
FOX_H, FOX_D = 8, 64
FOX_A = FOX_D + 2
POOL_WINDOWS = (2, 4, 8, 16)
MEM_H, MEM_D = 4, 128
D_FF = 2816
FF_C = 256
FF_N = D_FF // FF_C
SB_H, SB_D = 8, 64
ML_H, ML_D = 4, 128
CONV = 4
PEER_H, NKEYS, TOPK = 8, 128, 16
SEL = PEER_H * TOPK
EX_A = 4
EX_N = NKEYS // EX_A
HALF_A = NKEYS // 2
EPS = 1e-6
BIG = 1e30
N_MOD = 6


def constants():
    i = np.arange(P)
    row, col = i[:, None], i[None, :]
    bands = np.zeros((TB, P, len(POOL_WINDOWS), S), np.float32)
    t, s = np.arange(S)[None, :], np.arange(S)[:, None]
    for g, w in enumerate(POOL_WINDOWS):
        inside = (s <= t) & (s > t - w)
        bands[:, :, g] = (inside / np.minimum(t + 1, w) - (s == t)).reshape(TB, P, S)
    parts = {
        "ident": (row == col), "ones": np.ones((P, P)), "iota": np.broadcast_to(col, (P, P)),
        "fox_mask": np.where(col <= row, 0, -BIG),
        "ml_mask": np.where(row <= col, 0, -BIG),
        "sb_keep": (row < col),
        "sb_mask": np.where(row < col, 0, BIG),
        "upto": (row <= col),
        "after": (row > col),
        "bands": bands.transpose(1, 0, 2, 3).reshape(P, -1),
    }
    return {k: np.ascontiguousarray(v, dtype=np.float32) for k, v in parts.items()}


class Count:

    def __init__(self, nc, ctx, name):
        self.sem = ctx.enter_context(nc.semaphore(name))
        self.base, self.k = 0, 0

    @property
    def now(self):
        return self, self.base + self.k

    def add(self, ins, by=1):
        ins.then_inc(self.sem, by)
        self.k += by
        return self.now


def wait(eng, *tokens):
    for t in tokens:
        if t is not None and not (isinstance(t[1], int) and t[1] <= 0):
            eng.wait_ge(t[0].sem, t[1])


@contextmanager
def loop(nc, n, steps):
    before = {c: c.base + c.k for c in steps}
    with nc.Fori(0, n) as i:
        for c, d in steps.items():
            c.base, c.k = before[c] + i * d, 0
        yield i
        for c, d in steps.items():
            assert c.k == d, (c.sem, c.k, d)
    for c, d in steps.items():
        c.base, c.k = before[c] + n * d, 0


def program(nc, a, out, stage="all"):
    f32, f32r, bf16, u32 = mybir.dt.float32, mybir.dt.float32r, mybir.dt.bfloat16, mybir.dt.uint32
    ALU, ACT, AX = mybir.AluOpType, mybir.ActivationFunctionType, mybir.AxisListType
    PE, DVE, ACTE, POOL, SP = nc.tensor, nc.vector, nc.scalar, nc.gpsimd, nc.sync
    ctx = ExitStack()
    with ctx:
        def sb(name, shape, dt=f32):
            return ctx.enter_context(nc.sbuf_tensor(name, shape, dt))

        NSLOT = 4
        raw = sb("slab_raw", [P, NSLOT, SLAB])
        slab_hi = sb("slab_hi", [P, NSLOT, SLAB], f32r)
        slab_lo = sb("slab_lo", [P, NSLOT, SLAB], f32r)
        h = sb("residual", [P, TB, D])
        xh = sb("x_hi", [P, KT, S], f32r)
        xl = sb("x_lo", [P, KT, S], f32r)
        zs = sb("hidden", [P, 1024])
        wf = sb("weighted", [P, 1024])
        wh = sb("weighted_hi", [P, EX_A, S], f32r)
        wl = sb("weighted_lo", [P, EX_A, S], f32r)
        arena = sb("arena", [P, HALF_A * S])
        ident = sb("ident", [P, P])
        ones = sb("ones", [P, P])
        iota = sb("iota", [P, P])
        sel_a = sb("selected_first_keys", [P, S], bf16)
        sel_b = sb("selected_second_keys", [P, S], bf16)
        gate_parts = sb("selected_gates_in_parts", [P, 3, S], bf16)
        key4 = sb("key_numbers_by_4", [P, NKEYS, 4], bf16)
        cols = sb("columns", [P, 256])
        stat = sb("statistics", [P, 64])
        wsm_h = sb("small_weight_hi", [P, KT, 8], f32r)
        wsm_l = sb("small_weight_lo", [P, KT, 8], f32r)
        ps = ctx.enter_context(nc.psum_tensor("psum", [P, 8, 512], f32))

        def carve(at, *shape, parts=P):
            n = int(np.prod(shape))
            assert at + n <= HALF_A * S
            v = arena[0:parts, at:at + n]
            names = "abcd"[:len(shape)]
            if len(shape) > 1:
                v = v.rearrange(f"p ({' '.join(names)}) -> p {' '.join(names)}",
                                **{names[i]: shape[i] for i in range(len(shape))})
            return v

        def banks(b, n):
            return ps[:, b:b + n, :].rearrange("p b n -> p (b n)")

        pe, dve, act, pool = (Count(nc, ctx, n) for n in ("pe_done", "dve_done", "act_done", "pool_done"))
        z_read = Count(nc, ctx, "hidden_banks_read")
        load = [Count(nc, ctx, f"raw_loaded{s}") for s in range(NSLOT)]
        split_hi = [Count(nc, ctx, f"slab_hi_ready{s}") for s in range(NSLOT)]
        split_lo = [Count(nc, ctx, f"slab_lo_ready{s}") for s in range(NSLOT)]
        used = [Count(nc, ctx, f"slab_used{s}") for s in range(NSLOT)]

        def v(fn, *args, w=(), **kw):
            wait(DVE, *w)
            return dve.add(dve_ops[fn](*args, **kw))

        dve_ops = {"tt": DVE.tensor_tensor, "ts": DVE.tensor_scalar, "stt": DVE.scalar_tensor_tensor,
                        "copy": DVE.tensor_copy, "red": DVE.tensor_reduce, "recip": DVE.reciprocal,
                        "scan": DVE.tensor_tensor_scan, "max": DVE.max, "idx": DVE.max_index,
                        "repl": DVE.match_replace, "set": DVE.memset}

        def s(out, in_, func, w=(), **kw):
            wait(ACTE, *w)
            return act.add(ACTE.activation(out, in_, func, **kw))

        def mm(out, lhsT, rhs, start=True, stop=True):
            return PE.matmul(out, lhsT, rhs, start=start, stop=stop)

        def tr(out, in_):
            return PE.transpose(out, in_, ident[0:in_.shape[0], 0:in_.shape[0]])

        def done(ins):
            return pe.add(ins)

        def mm3(out, ah, al, bh, bl, start, stop):
            mm(out, ah, bh, start, False)
            mm(out, ah, bl, False, False)
            return mm(out, al, bh, False, stop)

        def everything():
            return pe.now, *(c.now for c in used), z_read.now, dve.now, act.now, pool.now

        def others():
            return dve.now, act.now, pool.now, z_read.now

        def fetch(name, pairs, w=()):
            c = Count(nc, ctx, name)
            wait(SP, *w)
            for dst, src in pairs:
                c.add(SP.dma_start(dst, src), 16)
            return c.now

        plan = []
        at = {"load": 0, "split": 0, "use": 0}

        def queue(entries):
            plan.extend(entries)

        def cyc(name, n):
            first = len(plan)
            queue([(name, j, (first + j) % NSLOT) for j in range(n)])

        def emit_load(name, j, slot):
            wait(SP, split_hi[slot].now, split_lo[slot].now)
            src = a[name].rearrange("n p m -> (n p) m")[bass.ds(j * P, P), :]
            load[slot].add(SP.dma_start(raw[:, slot, :], src), 16)

        def emit_split(slot):
            wait(ACTE, load[slot].now, used[slot].now)
            split_hi[slot].add(ACTE.activation(slab_hi[:, slot, :], raw[:, slot, :], ACT.Copy))
            wait(DVE, split_hi[slot].now)
            split_lo[slot].add(DVE.tensor_tensor(slab_lo[:, slot, :], raw[:, slot, :],
                                                 slab_hi[:, slot, :].bitcast(f32), ALU.subtract))

        def last_of(slot, before):
            return max((n for n in range(before) if plan[n][2] == slot), default=-1)

        def pump_loads():
            while at["load"] < len(plan) and last_of(plan[at["load"]][2], at["load"]) < at["split"]:
                emit_load(*plan[at["load"]])
                at["load"] += 1

        def pump(n=99):
            pump_loads()
            while n and at["split"] < at["load"] and last_of(plan[at["split"]][2], at["split"]) < at["use"]:
                emit_split(plan[at["split"]][2])
                at["split"] += 1
                n -= 1
                pump_loads()

        def pump_to(n):
            pump(max(0, n - (at["split"] - at["use"])))

        def take():
            while at["split"] <= at["use"]:
                pump(1)
            slot = plan[at["use"]][2]
            at["use"] += 1
            wait(PE, split_hi[slot].now, split_lo[slot].now)
            return slot

        def parts(slot, k, n):
            shape = dict(k=k, n=n)
            return tuple(t[:, slot, :].rearrange("p (k n) -> p k n", **shape) for t in (slab_hi, slab_lo))

        def gemm_tok(bank, half, slot, k0, nk=4, last=True, first=True):
            bh, bl = parts(slot, 4, 512)
            for tb in range(TB):
                tok = slice(tb * P, tb * P + P)
                for k in range(nk):
                    ins = mm3(ps[:, bank + tb, :], xh[:, k0 + k, tok], xl[:, k0 + k, tok], bh[:, k], bl[:, k],
                              first and k == 0, last and k == nk - 1)
            return ins

        def gemm_chunk(bank, free=()):
            wait(PE, *free)
            for half in range(2):
                slot = take()
                ins = gemm_tok(bank, half, slot, 4 * half, first=half == 0, last=half == 1)
                if half == 0:
                    used[slot].add(ins)
                    pump_to(3)
            return used[slot].add(ins)

        cyc("w_mem_kv", 4)
        cyc("w_in", 8)
        cyc("w_out", 4)
        cyc("w_mem_q", 2)
        cyc("w_mem_out", 2)
        ff = [("w_gu", 0, 0), ("w_gu", 1, 1)]
        for c in range(1, FF_N):
            ff += [("w_gu", 2 * c, 0), ("w_gu", 2 * c + 1, 1), ("w_down", c - 1, 2)]
        queue(ff + [("w_down", FF_N - 1, 2)])
        cyc("w_in_2", 14)
        cyc("w_out_2", 4)
        cyc("w_q_peer", 8)
        ex = [("ex_u", 0, 0), ("ex_u", 1, 1)]
        for c in range(1, EX_N):
            columns = [("ex_u", 2 * c, 0), ("ex_u", 2 * c + 1, 1)]
            rows = [("ex_v", 2 * c - 2, 2), ("ex_v", 2 * c - 1, 3)]
            ex += rows + columns if c == EX_N // 2 else columns + rows
        queue(ex + [("ex_v", 2 * EX_N - 2, 2), ("ex_v", 2 * EX_N - 1, 3)])

        gm = arena[:, 14336:16384].rearrange("p (b n) -> p b n", b=TB)
        t_mem = fetch("mem_loaded", [(gm, a["mem"])])
        CM, CKV, CQ, CF = 0, 8, 16, 24
        C_FOXQ, C_FOXK, C_MEMQ, C_MEMK, C_PS, C_EPS = 32, 33, 34, 35, 36, 40
        C_CT, C_SC, C_N1, C_N2, C_ADA, C_SBQ, C_SBK, C_CONV = 41, 49, 57, 65, 73, 121, 122, 124
        C_G1, C_G2, C_BG = 156, 164, 172
        t_col = fetch("columns_loaded", [(cols[:, 0:192], a["cols"]), (ident[:], a["ident"]), (ones[:], a["ones"]),
                                         (iota[:], a["iota"])])
        pump_loads()
        t_x = fetch("x_loaded", [(h[:], a["x"])])
        nc.scalar.preload_act_table_set("natural_log_exp_and_others")

        def rstd(n, width, at0, w):
            wait(POOL, *w)
            t = pool.add(POOL.tensor_scalar(stat[:, at0:at0 + n], stat[:, at0:at0 + n], 1.0 / width, EPS,
                                            ALU.mult, ALU.add))
            wait(POOL, t)
            return pool.add(POOL.tensor_tensor(stat[:, at0:at0 + n], stat[:, at0:at0 + n],
                                               minus_half[:, 0:n], ALU.pow))

        minus_half = sb("minus_half", [P, 16])
        t_mh = pool.add(POOL.memset(minus_half[:], -0.5))

        def split(dst_h, dst_l, full, w):
            wait(DVE, *w)
            t = s(dst_h, full, ACT.Copy, w=w)
            return v("tt", dst_l, full, dst_h.bitcast(f32), ALU.subtract, w=[t])

        def norm_to_x(src, gain, t_src, shift=None, scr=0, bank=0):
            free = everything()
            sq, xs = carve(scr, D), carve(scr, TB, D)
            full = carve(scr + TB * D, KT, S)
            for tb in range(TB):
                s(xs[:, tb, :], src[:, tb, :], ACT.Square, w=[*t_src, *free], accum_out=stat[:, tb:tb + 1])
            t = rstd(TB, D, 0, [act.now, t_mh])
            pump_to(1)
            for tb in range(TB):
                t = v("ts", xs[:, tb, :], src[:, tb, :], stat[:, tb:tb + 1], None, ALU.mult, w=[*free, t, act.now])
            for b in range(4):
                wait(PE, *free, t, *last_use())
                for k in (2 * b, 2 * b + 1):
                    for tb in range(TB):
                        ins = tr(ps[:, bank + b, (k % 2) * S + tb * P:(k % 2) * S + tb * P + P],
                                 xs[:, tb, k * P:k * P + P])
                tp = done(ins)
                two = slice(2 * b, 2 * b + 2)
                src_p = ps[:, bank + b, :].rearrange("p (k n) -> p k n", k=2)
                tf = v("tt", full[:, two], src_p, gain[:, two].unsqueeze(2).to_broadcast([P, 2, S]), ALU.mult, w=[tp])
                if shift is not None:
                    tf = v("tt", full[:, two], full[:, two], shift[:, two].unsqueeze(2).to_broadcast([P, 2, S]),
                           ALU.add, w=[tf])
                tl = split(xh[:, two], xl[:, two], full[:, two], [tf, *last_use()])
                if b == 1:
                    pump_to(2)
            return act.now, tl

        def last_use():
            return [c.now for c in used]

        def head_norm(src, dst, n_heads, d, at0, w, scratch):
            t = s(scratch, src, ACT.Square, w=w)
            t = v("red", stat[:, at0:at0 + n_heads], scratch, AX.X, ALU.add, w=[t])
            t = rstd(n_heads, d, at0, [t])
            return v("tt", dst, src, stat[:, at0:at0 + n_heads].unsqueeze(2).to_broadcast([P, n_heads, d]),
                     ALU.mult, w=[t, *w])

        return_stage = []

        A_MKT, A_MV, A_V, A_PIN, A_QT, A_KT, A_P, A_PT, A_MIX = 0, 1024, 2048, 3072, 4096, 6144, 8192, 12288, 15360
        t_xm = norm_to_x(gm, cols[:, CKV:CKV + 8], [t_mem, t_col], scr=4096, bank=0)
        wait(PE, *t_xm)
        t_k = gemm_chunk(4)
        t_v = gemm_chunk(6)
        mkn = carve(A_QT, 8, MEM_D)
        mksq = carve(A_KT, 8, MEM_D)
        t = head_norm(banks(4, 2).rearrange("p (h d) -> p h d", d=MEM_D), mkn, 8, MEM_D, 8, [t_k], mksq)
        mv = carve(A_MV, TB, 512)
        t_mv = s(mv, ps[:, 6:8, :], ACT.Copy, w=[t_v])
        mkT = carve(A_MKT, MEM_H, S)

        def head_transposes(dst, srcs, bank, n_rows, gain, w):
            for b in range(len(srcs) // 2):
                wait(PE, *w)
                for j in range(2):
                    for tb in range(TB):
                        o = j * S + tb * P
                        ins = tr(ps[0:n_rows, bank + b, o:o + P], srcs[2 * b + j][tb])
                tp = done(ins)
                t = s(dst[:, 2 * b:2 * b + 2, :], ps[0:n_rows, bank + b, :].rearrange("p (h n) -> p h n", h=2),
                      ACT.Copy, w=[tp, *w], scale=gain)
            return t

        t_cs = v("ts", cols[:, C_MEMQ:C_MEMQ + 1], cols[:, C_MEMQ:C_MEMQ + 1], MEM_D ** -0.5, None, ALU.mult, w=[t_col])
        t_cs = v("ts", cols[0:FOX_D, C_FOXQ:C_FOXQ + 1], cols[0:FOX_D, C_FOXQ:C_FOXQ + 1], FOX_D ** -0.5, None,
                 ALU.mult)
        t_cs = v("ts", cols[0:SB_D, C_SBQ:C_SBQ + 1], cols[0:SB_D, C_SBQ:C_SBQ + 1], SB_D ** -0.5, None, ALU.mult)
        mkn_h = [[mkn[:, tb * MEM_H + hh, :] for tb in range(TB)] for hh in range(MEM_H)]
        t_mk = head_transposes(mkT, mkn_h, 0, P, cols[:, C_MEMK:C_MEMK + 1], [t, t_cs])

        wsm = carve(14336, KT, 8)
        t_ws = fetch("forget_weight_loaded", [(wsm, a["w_f"])], w=everything())
        t_wsm = split(wsm_h[:], wsm_l[:], wsm, [t_ws])
        t_bf = fetch("block1_constants_loaded", [(carve(14500, P), a["fox_mask"]), (carve(14628, P), a["upto"]),
                                                 (carve(14800, FOX_H), a["b_forget"])], w=everything())
        fox_mask, upto, bfor = carve(14500, P), carve(14628, P), carve(14800, FOX_H)
        t_xm = norm_to_x(h, cols[:, CM:CM + 8], [t_x, t_col], scr=8192, bank=0)
        wait(PE, *t_xm, t_wsm, *others())
        for tb in range(TB):
            for k in range(KT):
                ins = mm3(ps[:, 7, tb * 8:tb * 8 + 8], xh[:, k, tb * P:tb * P + P], xl[:, k, tb * P:tb * P + P],
                          wsm_h[:, k], wsm_l[:, k], k == 0, k == KT - 1)
        t_f = done(ins)
        t_q = gemm_chunk(0)
        fl, fe = carve(14816, TB, FOX_H), carve(14832, TB, FOX_H)
        cum = carve(14848, TB, FOX_H)
        t = v("tt", fl, ps[:, 7, 0:16].rearrange("p (b h) -> p b h", b=TB),
              bfor.unsqueeze(1).to_broadcast([P, TB, FOX_H]), ALU.add, w=[t_f, t_bf])
        t = log_sigmoid_pieces(v, s, ALU, ACT, fl, fe, [t])
        t = v("stt", fl, fl, 0.0, fe, ALU.min, ALU.subtract, w=[t])
        wait(PE, t)
        mm(ps[:, 7, 16:24], upto, fl[:, 0, :])
        mm(ps[:, 7, 24:32], ones[:], fl[:, 0, :], True, False)
        t_c = done(mm(ps[:, 7, 24:32], upto, fl[:, 1, :], False, True))
        t_cum = v("copy", cum, ps[:, 7, 16:32].rearrange("p (b h) -> p b h", b=TB), w=[t_c])
        t_k = gemm_chunk(2)
        qa, ka = carve(A_PT, TB, FOX_H, FOX_A), carve(A_PT + 1056, TB, FOX_H, FOX_A)
        qsq = carve(A_P + 2048, 16, FOX_D)
        qa_v = qa.rearrange("p b h d -> p (b h) d")
        ka_v = ka.rearrange("p b h d -> p (b h) d")
        t = head_norm(banks(0, 2).rearrange("p (h d) -> p h d", d=FOX_D), qa_v[:, :, 0:FOX_D], 16, FOX_D, 8, [t_q], qsq)
        cum_v = cum.rearrange("p b h -> p (b h)").unsqueeze(2)
        v("set", qa_v[:, :, FOX_D:FOX_D + 1], 1.0)
        v("copy", qa_v[:, :, FOX_D + 1:FOX_A], cum_v, w=[t_cum])
        v("set", ka_v[:, :, FOX_D + 1:FOX_A], 1.0)
        v("ts", ka_v[:, :, FOX_D:FOX_D + 1], cum_v, -1.0, None, ALU.mult)
        t_v = gemm_chunk(4, free=[t_mv])
        t = head_norm(banks(2, 2).rearrange("p (h d) -> p h d", d=FOX_D), ka_v[:, :, 0:FOX_D], 16, FOX_D, 24,
                      [t_k, dve.now], qsq)
        vt = carve(A_V, TB, 512)
        t_vt = s(vt, ps[:, 4:6, :], ACT.Copy, w=[t_v, t_mk])
        bandsT = carve(A_P, TB, 4, S)
        t_bw = fetch("pool_tables_loaded", [(bandsT, a["bands"]), (zs[:, 0:512], a["w_pool"])], w=[*everything()])
        t_p = gemm_chunk(6, free=[t_cum, t_mv])
        pin = carve(A_PIN, TB, 512)
        t_pin = s(pin, ps[:, 6:8, :], ACT.Copy, w=[t_p])
        qT, kT = carve(A_QT, FOX_H, S, parts=FOX_A), carve(A_KT, FOX_H, S, parts=FOX_A)
        t_qT = head_transposes(qT, [[qa[:, tb, hh, :] for tb in range(TB)] for hh in range(FOX_H)], 0, FOX_A,
                               cols[0:FOX_A, C_FOXQ:C_FOXQ + 1], [t, t_cs, act.now])
        t_kT = head_transposes(kT, [[ka[:, tb, hh, :] for tb in range(TB)] for hh in range(FOX_H)], 4, FOX_A,
                               cols[0:FOX_A, C_FOXK:C_FOXK + 1], [t, act.now])
        mixT = carve(A_MIX, 4, S)
        wait(PE, t_bw, t_pin, act.now, dve.now)
        for g in range(4):
            o = ps[:, g // 2, (g % 2) * S:(g % 2) * S + S]
            for sbk in range(TB):
                ins = mm(o, pin[:, sbk, g * P:g * P + P], bandsT[:, sbk, g, :], sbk == 0, sbk == 1)
        t = done(ins)
        t = s(mixT, banks(0, 2).rearrange("p (g n) -> p g n", g=4), ACT.Copy, w=[t])
        wait(PE, t)
        for g in range(4):
            ins = mm(ps[:, 2 + g // 2, (g % 2) * S:(g % 2) * S + S], zs[:, g * P:g * P + P], mixT[:, g, :])
        t = done(ins)
        t = v("tt", mixT, banks(2, 2).rearrange("p (g n) -> p g n", g=4),
              cols[:, C_PS:C_PS + 4].unsqueeze(2).to_broadcast([P, 4, S]), ALU.mult, w=[t])
        t_cat1 = split(xh[:, 4:8], xl[:, 4:8], mixT, [t, *last_use()])

        prob = carve(A_P, TB, FOX_H, S)
        for tb in range(TB):
            ns = P * (tb + 1)
            b0 = 4 * (1 - tb)
            wait(PE, t_qT, t_kT, *others())
            for hh in range(FOX_H):
                o = ps[:, b0 + hh // 2, (hh % 2) * S:(hh % 2) * S + ns]
                mm(o, qT[:, hh, tb * P:tb * P + P], kT[:, hh, 0:ns], True, False)
                ins = mm(o[:, ns - P:ns], ident[:], fox_mask, False, True)
            t = done(ins)
            sc = banks(b0, 4).rearrange("p (h n) -> p h n", h=FOX_H)[:, :, 0:ns]
            t = softmax(v, s, ALU, ACT, AX, sc, prob[:, tb, :, 0:ns], stat, FOX_H, [t, t_cat1], P)
        pT0, pT1 = carve(A_PT, FOX_H, S), carve(A_PT + 2048, FOX_H, P)
        wait(PE, *others())
        for hh in range(FOX_H):
            for tb in range(TB):
                ins = tr(ps[:, hh // 2, (hh % 2) * S + tb * P:(hh % 2) * S + tb * P + P], prob[:, tb, hh, 0:P])
            if hh % 2:
                t = done(ins)
                t = s(pT0[:, hh - 1:hh + 1, :], ps[:, hh // 2, :].rearrange("p (h n) -> p h n", h=2), ACT.Copy,
                      w=[t, pe.now])
        for hh in range(FOX_H):
            ins = tr(ps[:, 4 + hh // 4, (hh % 4) * P:(hh % 4) * P + P], prob[:, 1, hh, P:S])
        t = done(ins)
        t1 = v("copy", pT1, banks(4, 2).rearrange("p (h n) -> p h n", h=FOX_H), w=[t])
        wait(PE, t1, act.now)
        for hh in range(FOX_H):
            o = ps[(hh % 2) * FOX_D:(hh % 2) * FOX_D + FOX_D, 6 + hh // 4, (hh // 2 % 2) * S:(hh // 2 % 2) * S + S]
            mm(o, vt[:, 0, hh * FOX_D:hh * FOX_D + FOX_D], pT0[:, hh, :], True, False)
            ins = mm(o[:, P:S], vt[:, 1, hh * FOX_D:hh * FOX_D + FOX_D], pT1[:, hh, :], False, True)
        t = done(ins)
        foxT = carve(A_QT, 4, S)
        t = v("copy", foxT, banks(6, 2).rearrange("p (k n) -> p k n", k=4), w=[t])
        t_cat0 = split(xh[:, 0:4], xl[:, 0:4], foxT, [t, *last_use()])

        def transpose_to_x(src, w, bank):
            for b in range(4):
                wait(PE, *w, *others())
                for k in (2 * b, 2 * b + 1):
                    for tb in range(TB):
                        ins = tr(ps[:, bank + b, (k % 2) * S + tb * P:(k % 2) * S + tb * P + P],
                                 src[:, tb, k * P:k * P + P])
                t = done(ins)
                two = slice(2 * b, 2 * b + 2)
                t = split(xh[:, two], xl[:, two], ps[:, bank + b, :].rearrange("p (k n) -> p k n", k=2), [t, *last_use()])
            return act.now, t

        def out_proj(t_in, gate=None, w=()):
            wait(PE, *t_in, *others())
            for c in range(2):
                for half in range(2):
                    slot = take()
                    bh, bl = parts(slot, 4, 512)
                    for tb in range(TB):
                        for k in range(4):
                            kk = 4 * half + k
                            ins = mm3(ps[:, 2 * tb + c, :], xh[:, kk, tb * P:tb * P + P], xl[:, kk, tb * P:tb * P + P],
                                      bh[:, k], bl[:, k], kk == 0, kk == 7)
                    used[slot].add(ins)
                    pump_to(2 if c and half else 3)
            return add_residual([used[slot].now, *w], gate)

        def add_residual(w, gate=None):
            for tb in range(TB):
                y = banks(2 * tb, 2)
                if gate is not None:
                    t = v("tt", gate[1][:, tb], y, gate[0], ALU.mult, w=w)
                    t = v("tt", h[:, tb, :], h[:, tb, :], gate[1][:, tb], ALU.add, w=[t])
                else:
                    t = v("tt", h[:, tb, :], h[:, tb, :], y, ALU.add, w=w)
            return t

        t_h = out_proj([t_cat1, t_cat0, act.now])

        if stage == "mix":
            return finish(nc, SP, h, out, ctx, [t_h], fetch)
        t_xm = norm_to_x(h, cols[:, CQ:CQ + 8], [t_h], scr=8192, bank=4)
        wait(PE, *t_xm)
        t_q = gemm_chunk(0)
        mqn, mqsq = carve(A_V, 8, MEM_D), carve(A_PIN, 8, MEM_D)
        t = head_norm(banks(0, 2).rearrange("p (h d) -> p h d", d=MEM_D), mqn, 8, MEM_D, 8, [t_q], mqsq)
        mqT = carve(A_QT, MEM_H, S)
        t = head_transposes(mqT, [[mqn[:, tb * MEM_H + hh, :] for tb in range(TB)] for hh in range(MEM_H)], 2, P,
                            cols[:, C_MEMQ:C_MEMQ + 1], [t])
        mprob = carve(A_KT, TB, MEM_H, S)
        for tb in range(TB):
            wait(PE, t)
            for hh in range(MEM_H):
                ins = mm(ps[:, 4 + 2 * tb + hh // 2, (hh % 2) * S:(hh % 2) * S + S],
                         mqT[:, hh, tb * P:tb * P + P], mkT[:, hh, :])
            tp = done(ins)
            softmax(v, s, ALU, ACT, AX, banks(4 + 2 * tb, 2).rearrange("p (h n) -> p h n", h=MEM_H),
                    mprob[:, tb], stat, MEM_H, [tp], P)
        mpT = carve(A_P, TB, MEM_H, S)
        wait(PE, dve.now, act.now)
        for mb in range(TB):
            for hh in range(MEM_H):
                for tb in range(TB):
                    ins = tr(ps[:, 2 * mb + hh // 2, (hh % 2) * S + tb * P:(hh % 2) * S + tb * P + P],
                             mprob[:, tb, hh, mb * P:mb * P + P])
            t = done(ins)
            src = banks(2 * mb, 2).rearrange("p (h n) -> p h n", h=MEM_H)
            t = s(mpT[:, mb], src, ACT.Copy, w=[t]) if mb == 0 else v("copy", mpT[:, mb], src, w=[t])
        wait(PE, dve.now, act.now)
        for hh in range(MEM_H):
            o = ps[:, 4 + hh // 2, (hh % 2) * S:(hh % 2) * S + S]
            for mb in range(TB):
                ins = mm(o, mv[:, mb, hh * MEM_D:hh * MEM_D + MEM_D], mpT[:, mb, hh, :], mb == 0, mb == 1)
        t = done(ins)
        moT = carve(A_QT, 4, S)
        t = v("copy", moT, banks(4, 2).rearrange("p (k n) -> p k n", k=4), w=[t])
        t = split(xh[:, 0:4], xl[:, 0:4], moT, [t, *last_use()])
        wait(PE, t, act.now)
        for c in range(2):
            slot = take()
            bh, bl = parts(slot, 4, 512)
            for tb in range(TB):
                for k in range(4):
                    ins = mm3(ps[:, 2 * tb + c, :], xh[:, k, tb * P:tb * P + P], xl[:, k, tb * P:tb * P + P],
                              bh[:, k], bl[:, k], k == 0, k == 3)
            used[slot].add(ins)
        t_h = add_residual([used[slot].now])
        if stage == "mem":
            return finish(nc, SP, h, out, ctx, [t_h], fetch)
        ada_load = [Count(nc, ctx, f"ada_loaded{n}") for n in range(3)]
        ada_done = [Count(nc, ctx, f"ada_summed{n}") for n in range(3)]
        ada = carve(0, 3, SLAB)
        ada_raw = carve(6144, 3, SLAB)
        t_free = everything()
        sil, cc = cols[:, C_SC:C_SC + 8], cols[:, C_CT:C_CT + 8]
        t = s(sil, cc, ACT.Exp, w=[t_col], scale=-1.0)
        t = v("ts", sil, sil, 1.0, None, ALU.add, w=[t])
        t = v("recip", sil, sil, w=[t])
        t_sil = v("tt", sil, sil, cc, ALU.mult, w=[t])
        wait(POOL, *t_free)
        t_az = pool.add(POOL.memset(carve(0, 3 * SLAB), 0.0))
        t_y0 = pool.add(POOL.memset(wl[:, 0:2, :].bitcast(f32), 0.0))

        def load_ada(k, n, w=()):
            wait(SP, *w, ada_done[n].now)
            src = a["w_ada"].rearrange("n p m -> (n p) m")[bass.ds((k * 3 + n) * P, P), :]
            ada_load[n].add(SP.dma_start(ada_raw[:, n, :], src), 16)

        def sum_ada(k, n):
            wait(DVE, ada_load[n].now, ada_done[n].now, t_az, t_sil)
            ada_done[n].add(DVE.scalar_tensor_tensor(ada[:, n, :], ada_raw[:, n, :], cols[:, bass.ds(C_SC + k, 1)],
                                                     ada[:, n, :], ALU.mult, ALU.add))

        def clear_sums(t_y0):
            wait(PE, t_y0, *others())
            for b in range(4):
                mm(ps[:, b, :], wl[:, 0, 0:P], wl[:, 0:2, :], True, False)

        def slot_ready(slot):
            wait(PE, split_hi[slot].now, split_lo[slot].now)

        def hidden_products(refill):
            wait(PE, z_read.now)
            for half in range(2):
                slot_ready(half)
                used[half].add(gemm_tok(4, half, half, 4 * half, first=half == 0, last=half == 1))
                if half == 0:
                    refill(0)

        def add_products(slot, k0, t_w, stop=False):
            bh, bl = parts(slot, 2, D)
            slot_ready(slot)
            wait(PE, *t_w)
            for tb in range(TB):
                for k in range(2):
                    for half in range(2):
                        n = slice(half * 512, half * 512 + 512)
                        ins = mm3(ps[:, 2 * tb + half, :], wh[:, k0 + k, tb * P:tb * P + P],
                                  wl[:, k0 + k, tb * P:tb * P + P], bh[:, k, n], bl[:, k, n], False, stop and k == 1)
            used[slot].add(ins)

        def ff_step(i, refill, first=False, ada_k=None, ada_next=None):
            t_w = act.now, dve.now
            hidden_products(refill)
            sg = zs[:, 0:512].rearrange("p (b n) -> p b n", b=TB)
            hid = zs[:, 512:1024].rearrange("p (b n) -> p b n", b=TB)
            t = s(sg, ps[:, 4:6, 0:FF_C], ACT.Silu, w=[used[1].now, z_read.now])
            wait(DVE, t, pe.now)
            z_read.add(DVE.tensor_tensor(hid, sg, ps[:, 4:6, FF_C:512], ALU.mult))
            refill(1)
            if not first:
                add_products(2, 0, t_w)
            wait(PE, z_read.now, *t_w)
            for k in range(2):
                for tb in range(TB):
                    ins = tr(ps[:, 6, k * S + tb * P:k * S + tb * P + P], hid[:, tb, k * P:k * P + P])
            t = done(ins)
            if not first:
                refill(2)
            src = ps[:, 6, :].rearrange("p (k n) -> p k n", k=2)
            split(wh[:, 0:2], wl[:, 0:2], src, [t])
            if ada_k is not None:
                for n in range(3):
                    sum_ada(ada_k, n)
                    if ada_next is not None:
                        load_ada(ada_next, n)

        def later(slot):
            pass

        def pumped(slot):
            assert plan[at["use"]][2] == slot
            at["use"] += 1
            pump()

        def at_loop(n_steps, per_step):
            for k in at:
                at[k] += n_steps * per_step

        t_xm = norm_to_x(h, cols[:, CF:CF + 8], [t_h], scr=12288, bank=0)
        for n in range(3):
            load_ada(0, n, t_free)
        wait(PE, *t_xm)
        clear_sums(t_y0)
        pump()
        ff_step(0, pumped, first=True)
        FF_L = FF_N - 4
        assert at["split"] == at["use"] + 3 and at["load"] == at["use"] + 6
        steps = {act: 2, dve: 1, pe: 1, z_read: 1, **{used[n]: 1 for n in range(3)},
                 **{load[n]: 16 for n in range(3)}, **{split_hi[n]: 1 for n in range(3)},
                 **{split_lo[n]: 1 for n in range(3)}, **{c: 16 for c in ada_load}, **{c: 1 for c in ada_done}}
        with loop(nc, FF_L, steps) as j:
            def refill(slot, j=j):
                emit_split(slot)
                if slot < 2:
                    emit_load("w_gu", 2 * j + 6 + slot, slot)
                else:
                    emit_load("w_down", j + 2, slot)
            ff_step(j + 1, refill, ada_k=j, ada_next=j + 1)
        at_loop(FF_L, 3)
        for i in range(FF_N - 3, FF_N):
            ff_step(i, pumped, ada_k=i - 1 if i == FF_N - 3 else None)
        add_products(2, 0, [act.now, dve.now], stop=True)
        at["use"] += 1
        t_h = add_residual([used[2].now])
        if stage == "ffn":
            return finish(nc, SP, h, out, ctx, [t_h], fetch)

        md = cols[:, C_ADA:C_ADA + 48]
        wait(PE, *(c.now for c in ada_done), *others())
        for j in range(48):
            ins = mm(ps[:, 4, 2 * j:2 * j + 2], ada[:, j // 16, (j % 16) * P:(j % 16) * P + P], ones[:, 0:2])
        t = done(ins)
        t = v("tt", md, md, ps[:, 4, 0:96].rearrange("p (j t) -> p j t", t=2)[:, :, 0], ALU.add, w=[t])
        for c_out, c_g, m in ((C_G1, C_N1, 1), (C_G2, C_N2, 4)):
            t_g = v("stt", cols[:, c_out:c_out + 8], cols[:, C_ADA + 8 * m:C_ADA + 8 * m + 8], 1.0,
                    cols[:, c_g:c_g + 8], ALU.add, ALU.mult, w=[t])

        def spread_gate(m, dst, scr, bank, w):
            diag = carve(scr, KT, P)
            t = v("tt", diag, ident[:].unsqueeze(1).to_broadcast([P, KT, P]),
                  cols[:, C_ADA + 8 * m:C_ADA + 8 * m + 8].unsqueeze(2).to_broadcast([P, KT, P]), ALU.mult, w=w)
            wait(PE, t, *others())
            for half in range(2):
                ins = mm(ps[:, bank + half, :], ones[:], carve(scr, TB, 512)[:, half, :])
            t = done(ins)
            return s(dst, banks(bank, 2), ACT.Copy, w=[t])

        B_VSB, B_OML, B_VML, B_CV, B_PRE, B_QT, B_KT, B_QN, B_Y, B_ST = (
            0, 1024, 2048, 3088, 5136, 7208, 9256, 11304, 13352, 15400)
        t_all = everything()
        c2 = {n: wf[:, k * P:k * P + P] for k, n in enumerate(("ml_mask", "sb_keep", "sb_mask", "after"))}
        t_c2 = fetch("block2_constants_loaded", [(c2[n], a[n]) for n in c2] +
                     [(carve(B_ST, KT, 8), a["w_if"])], w=t_all)
        t_x2 = norm_to_x(h, cols[:, C_G1:C_G1 + 8], [t_h, t_g], shift=cols[:, C_ADA:C_ADA + 8], scr=B_QT, bank=0)
        t_wsm = split(wsm_h[:], wsm_l[:], carve(B_ST, KT, 8), [t_c2, *everything()])
        wait(PE, *t_x2, t_wsm, *others())
        for tb in range(TB):
            for k in range(KT):
                ins = mm3(ps[:, 7, tb * 8:tb * 8 + 8], xh[:, k, tb * P:tb * P + P], xl[:, k, tb * P:tb * P + P],
                          wsm_h[:, k], wsm_l[:, k], k == 0, k == KT - 1)
        t_if = done(ins)

        def gemm_feat(bank, free=()):
            wait(PE, *free)
            pump_to(2)
            slots = (take(), take())
            pq = [parts(sl, 4, 512) for sl in slots]
            for m in range(4):
                for k in range(KT):
                    bh, bl = pq[k // 4]
                    col = slice(m * P, m * P + P)
                    ins = mm3(ps[:, bank + m // 2, (m % 2) * S:(m % 2) * S + S], bh[:, k % 4, col], bl[:, k % 4, col],
                              xh[:, k, :], xl[:, k, :], k == 0, k == KT - 1)
                    if m == 3 and k == 3:
                        used[slots[0]].add(ins)
            return used[slots[1]].add(ins)

        pre = carve(B_PRE, 8, S + CONV - 1)
        conv = carve(B_CV, 8, S)
        t_z = v("set", pre[:, :, 0:CONV - 1], 0.0, w=t_all)
        gt = carve(B_ST + 64, TB, 8)
        t = v("copy", gt, ps[:, 7, 0:16].rearrange("p (b h) -> p b h", b=TB), w=[t_if])
        wait(PE, t)
        for m in range(2):
            for tb in range(TB):
                ins = tr(ps[0:ML_H, 6, m * S + tb * P:m * S + tb * P + P], gt[:, tb, m * ML_H:m * ML_H + ML_H])
        t_gr = done(ins)
        for c in range(2):
            t = gemm_feat(2 * c)
            t_pre = s(pre[:, 4 * c:4 * c + 4, CONV - 1:], banks(2 * c, 2).rearrange("p (k n) -> p k n", k=4),
                      ACT.Copy, w=[t, t_z])
            pump_to(2)
        t_qs = gemm_chunk(4)
        rows = lambda n: carve(B_Y + n * S, S, parts=ML_H)
        fr, le, cumA, er, cm, em, on4 = (rows(n) for n in range(7))
        t1 = v("set", on4, 1.0, w=t_all)
        t = v("ts", fr, ps[0:ML_H, 6, S:2 * S], cols[0:ML_H, C_BG + 1:C_BG + 2], None, ALU.add, w=[t_gr, *t_all])
        t = log_sigmoid_pieces(v, s, ALU, ACT, fr, le, [t, *t_all])
        t = v("stt", fr, fr, 0.0, le, ALU.min, ALU.subtract, w=[t])
        t = v("scan", cumA, on4, fr, 0.0, ALU.mult, ALU.add, w=[t, t1])
        t = v("stt", er, ps[0:ML_H, 6, 0:S], cols[0:ML_H, C_BG:C_BG + 1], cumA, ALU.add, ALU.subtract, w=[t])
        t = v("scan", cm, on4, er, 0.0, ALU.mult, ALU.max, w=[t])
        t = v("tt", le, cumA, cm, ALU.add, w=[t])
        t_em = s(em, le, ACT.Exp, w=[t], scale=-1.0)
        t_ncm = v("ts", cm, cm, -1.0, None, ALU.mult, w=[t])
        t_ks = gemm_chunk(0, free=[t_pre])
        qn, kn = carve(B_QN, 16, SB_D), carve(B_QN + 1024, 16, SB_D)
        t_qn = head_norm(banks(4, 2).rearrange("p (h d) -> p h d", d=SB_D), qn, 16, SB_D, 8, [t_qs], carve(B_QT, 16, SB_D))
        for k in range(8):
            w4 = [cols[:, C_CONV + 4 * k + j:C_CONV + 4 * k + j + 1] for j in range(CONV)]
            t = v("ts", conv[:, k], pre[:, k, 0:S], w4[0], None, ALU.mult, w=[t_pre, *t_all] if k == 0 else [])
            for j in range(1, CONV):
                t = v("stt", conv[:, k], pre[:, k, j:j + S], w4[j], conv[:, k], ALU.mult, ALU.add, w=[t])
        t_cv = s(conv, conv, ACT.Silu, w=[t])
        t_vm = gemm_chunk(2)
        t_kn = head_norm(banks(0, 2).rearrange("p (h d) -> p h d", d=SB_D), kn, 16, SB_D, 24, [t_ks, dve.now],
                         carve(B_QT, 16, SB_D))
        t_vs = gemm_chunk(6, free=[t_em, t_ncm])
        vml = carve(B_VML, TB, ML_H, ML_D + 1)
        t_vml = s(vml[:, :, :, 0:ML_D], ps[:, 2:4, :].rearrange("p b (h d) -> p b h d", d=ML_D), ACT.Copy, w=[t_vm, *t_all])
        t_one = v("set", vml[:, :, :, ML_D:ML_D + 1], 1.0)
        vsb = carve(B_VSB, TB, 512)
        t_vsb = s(vsb, ps[:, 6:8, :], ACT.Copy, w=[t_vs, *t_all])
        t_om = gemm_chunk(4, free=[t_qn])
        oml = carve(B_OML, TB, 512)
        t = s(oml, ps[:, 4:6, :], ACT.Exp, w=[t_om, *t_all], scale=-1.0)
        t = v("ts", oml, oml, 1.0, None, ALU.add, w=[t])
        t_oml = v("recip", oml, oml, w=[t])

        COLS = S + P
        sel4, esel = carve(B_QT, ML_H, P, parts=ML_H), carve(B_QT + 512, ML_H, S, parts=ML_H)
        id4 = ident[0:ML_H, 0:ML_H]
        t = v("copy", sel4, id4.unsqueeze(2).to_broadcast([ML_H, ML_H, P]), w=[t_kn])
        t = v("tt", esel, id4.unsqueeze(2).to_broadcast([ML_H, ML_H, S]),
              er.unsqueeze(1).to_broadcast([ML_H, ML_H, S]), ALU.mult)
        wait(PE, t, t_ncm, t_em, t1, t_c2, *others())
        for hh in range(ML_H):
            o = ps[:, hh, :]
            for sbk, (c0, c1, t0) in enumerate(((0, S, 0), (S, COLS, P))):
                mm(o[:, c0:c1], esel[:, hh, sbk * P:sbk * P + P], on4[:, t0:S], True, False)
                mm(o[:, c0:c1], sel4[:, hh, :], cm[:, t0:S], False, False)
                ins = mm(o[:, c0:c0 + P], ident[:], c2["ml_mask"], False, True)
            t_arg = done(ins)
            o = ps[:, 4 + hh, :]
            mm(o[:, 0:S], conv[:, 4 + hh, 0:P], conv[:, hh, :])
            t_s = done(mm(o[:, S:COLS], conv[:, 4 + hh, P:S], conv[:, hh, P:S]))
        wml = carve(B_QT + 1536, ML_H, COLS)
        heads = lambda b: banks(b, 4).rearrange("p (h n) -> p h n", h=4)[:, :, 0:COLS]
        t = s(wml, heads(0), ACT.Exp, w=[t_arg])
        t = v("stt", wml, heads(4), ML_D ** -0.5, wml, ALU.mult, ALU.mult, w=[t, t_s])
        wait(PE, t, t_one, t_vml)
        for tb in range(TB):
            ins = tr(ps[:, 7, 4 * tb:4 * tb + 4], em[:, tb * P:tb * P + P])
        for tb in range(TB):
            for hh in range(ML_H):
                o = ps[:, 2 * tb + hh // 2, (hh % 2) * 129:(hh % 2) * 129 + 129]
                mm(o, wml[:, hh, tb * P:tb * P + P], vml[:, 0, hh, :], True, tb == 0)
                if tb:
                    ins = mm(o, wml[:, hh, S:COLS], vml[:, 1, hh, :], False, True)
        t = done(ins)
        num = banks(0, 4).rearrange("p (b n) -> p b n", b=4)[:, :, 0:258].rearrange("p b (h d) -> p b h d", d=129)
        emc = carve(B_ST, 8)
        den = carve(B_ST + 8, 8)
        t1 = v("copy", emc, ps[:, 7, 0:8], w=[t])
        den4 = den.rearrange("p (b h) -> p b h", h=2)
        t2 = v("copy", den4, num[:, :, :, ML_D], w=[t])
        t2 = v("stt", den, den, -1.0, den, ALU.mult, ALU.max, w=[t2])
        t2 = v("tt", den, den, emc, ALU.max, w=[t1, t2])
        t2 = v("recip", den, den, w=[t2])
        mix = carve(B_Y, TB, D)
        yml = carve(B_QT, 8, ML_D)
        t2 = v("tt", yml.rearrange("p (b h) d -> p b h d", h=2), num[:, :, :, 0:ML_D],
               den4.unsqueeze(3).to_broadcast([P, 4, 2, ML_D]), ALU.mult, w=[t2])
        t_go = fetch("output_gains_loaded", [(zs[:], a["g_out"])], w=everything())
        t_n = head_norm(yml, yml, 8, ML_D, 8, [t2], carve(B_QT + 1024, 8, ML_D))
        yml4 = yml.rearrange("p (b h) d -> p b (h d)", b=TB)
        t = v("tt", oml, oml, zs[:, 512:1024].unsqueeze(1).to_broadcast([P, TB, 512]), ALU.mult, w=[t_go, t_oml])
        t_yml = v("tt", mix[:, :, 512:1024], yml4, oml, ALU.mult, w=[t_n, t])

        qT2, kT2 = carve(B_QT, SB_H, S, parts=SB_D), carve(B_KT, SB_H, S, parts=SB_D)
        for dst, srcn, col in ((qT2, qn, C_SBQ), (kT2, kn, C_SBK)):
            t = head_transposes(dst, [[srcn[:, tb * SB_H + hh, :] for tb in range(TB)] for hh in range(SB_H)],
                                0 if dst is qT2 else 4, SB_D, cols[0:SB_D, col:col + 1], [t_qn, t_kn, t_yml, t_cs])
        share, keep, arg = carve(B_CV, 4, COLS), carve(B_CV + 1536, 4, COLS), carve(B_QN, 4, COLS)
        for g in range(2):
            wait(PE, t, *others())
            for hh in range(4):
                k = 4 * g + hh
                mm(ps[:, hh, 0:S], kT2[:, k, 0:P], qT2[:, k, :])
                ins = mm(ps[:, hh, S:COLS], kT2[:, k, P:S], qT2[:, k, P:S])
            t = done(ins)
            z = heads(0)
            t = log_sigmoid_pieces(v, s, ALU, ACT, z, share, [t])
            t = v("stt", keep, z, 0.0, share, ALU.max, ALU.add, w=[t])
            diag = keep.rearrange("p h (m n) -> p h m n", m=3)[:, :, 0:3:2, :]
            t_keep = v("tt", diag, diag, c2["sb_keep"].unsqueeze(1).unsqueeze(1).to_broadcast([P, 4, 2, P]), ALU.mult, w=[t])
            t_argz = v("stt", arg, z, 0.0, share, ALU.min, ALU.subtract)
            wait(PE, t_keep)
            for hh in range(4):
                o = ps[:, 4 + hh, :]
                mm(o[:, 0:S], c2["after"], keep[:, hh, 0:S], True, False)
                mm(o[:, P:S], ones[:], keep[:, hh, S:COLS], False, False)
                mm(o[:, 0:P], ident[:], c2["sb_mask"], False, True)
                mm(o[:, S:COLS], c2["after"], keep[:, hh, S:COLS], True, False)
                ins = mm(o[:, S:COLS], ident[:], c2["sb_mask"], False, True)
            t = done(ins)
            t = v("tt", arg, arg, heads(4), ALU.subtract, w=[t, t_argz])
            t = s(arg, arg, ACT.Exp, w=[t])
            wait(PE, t)
            for hh in range(4):
                k = 4 * g + hh
                for tb in range(TB):
                    o = ps[:, hh, COLS + tb * SB_D:COLS + tb * SB_D + SB_D]
                    mm(o, arg[:, hh, tb * P:tb * P + P], vsb[:, 0, k * SB_D:k * SB_D + SB_D], True, tb == 0)
                    if tb:
                        ins = mm(o, arg[:, hh, S:COLS], vsb[:, 1, k * SB_D:k * SB_D + SB_D], False, True)
            t = done(ins)
            src = banks(0, 4).rearrange("p (h n) -> p h n", h=4)[:, :, COLS:512].rearrange("p h (b d) -> p b h d", b=TB)
            for tb in range(TB):
                t = v("copy", mix[:, tb, g * 256:g * 256 + 256].rearrange("p (h d) -> p h d", d=SB_D), src[:, tb], w=[t])
        for tb in range(TB):
            half = mix[:, tb, 0:512].rearrange("p (h d) -> p h d", d=SB_D)
            t = head_norm(half, half, 8, SB_D, 8 + 8 * tb, [t], carve(B_CV, 8, SB_D))
            t = v("tt", mix[:, tb, 0:512], mix[:, tb, 0:512], zs[:, 0:512], ALU.mult, w=[t])
        t_mix = transpose_to_x(mix, [t, t_yml], bank=4)
        g1 = carve(B_CV, D)
        t_g1 = spread_gate(2, g1, B_CV + 1024, 6, [*everything()])
        t_h = out_proj(t_mix, gate=(g1, carve(B_QN, TB, D)), w=[t_g1])
        if stage == "mix2":
            return finish(nc, SP, h, out, ctx, [t_h], fetch)

        R_SK, R_SC, R_QT = 0, 2048, 6144
        t_key4 = v("copy", key4[:], iota[:].unsqueeze(2).to_broadcast([P, NKEYS, 4]), w=[t_col])
        sk = carve(R_SK, PEER_H * 2, NKEYS)
        t_sk = fetch("sub_keys_loaded", [(carve(R_SK, SLAB), a["sub_keys"])], w=everything())
        t_x3 = norm_to_x(h, cols[:, C_G2:C_G2 + 8], [t_h], shift=cols[:, C_ADA + 24:C_ADA + 32], scr=8192, bank=0)
        scores = carve(R_SC, TB, 2 * PEER_H, NKEYS)
        wait(PE, *t_x3, t_sk)
        def queries(c):
            t = gemm_feat(2 * (c % 2), free=others())
            qT3 = carve(R_QT + 1024 * (c % 2), 4, S)
            t = s(qT3, banks(2 * (c % 2), 2).rearrange("p (k n) -> p k n", k=4), ACT.Copy, w=[t, *everything()])
            pump_to(3)
            return qT3, t

        ready = queries(0)
        for c in range(4):
            qT3, t = ready
            if c < 3:
                ready = queries(c + 1)
            wait(PE, t, dve.now)
            for tb in range(TB):
                for m in range(4):
                    ins = mm(ps[:, 4 + 2 * (c % 2) + tb, m * P:m * P + P], qT3[:, m, tb * P:tb * P + P],
                             sk[:, 4 * c + m, :])
            t = t_scored = done(ins)
            b = 4 + 2 * (c % 2)
            t_sc = v("copy", scores[:, :, 4 * c:4 * c + 4, :], ps[:, b:b + 2, :].rearrange("p b (m n) -> p b m n", m=4),
                     w=[t])

        wait(PE, *others())
        pump()
        hidden_products(later)
        at["use"] += 2

        NEG = -3.0e38
        U = lambda x: x.bitcast(u32)
        tv = carve(6144, TB, 2 * PEER_H, TOPK)
        ti = carve(6656, TB, 2 * PEER_H, TOPK)
        tf = carve(7168, TB, 2 * PEER_H, TOPK)
        bv = carve(7680, TB, PEER_H, TOPK)
        bp = carve(7936, TB, PEER_H, TOPK)
        pi, pj = carve(8192, TB, PEER_H, TOPK), carve(8448, TB, PEER_H, TOPK)
        sa, sbb, sg_ = carve(8704, TB, SEL), carve(8960, TB, SEL), carve(9216, TB, SEL)
        cand = carve(9728, PEER_H, TOPK * TOPK)
        oneh = carve(0, PEER_H, TOPK, TOPK)

        def top16(rows, w):
            t = w
            for values, v16, _ in rows:
                t_last = v("max", v16[:, 0:8], values, w=t)
                t = []
            for values, v16, i16 in rows:
                t_idx = v("idx", U(i16[:, 0:8]), v16[:, 0:8], values, w=[t_last])
            for values, v16, _ in rows:
                t_last = v("repl", values, v16[:, 0:8], values, NEG, w=[t_idx])
            for values, v16, _ in rows:
                t_max = v("max", v16[:, 8:16], values, w=[t_last])
            for values, v16, i16 in rows:
                t_idx = v("idx", U(i16[:, 8:16]), v16[:, 8:16], values, w=[t_max])
            return t_idx

        t_all = (t_scored, dve.now, act.now, pool.now)
        t = top16([(scores[:, tb, m, :], tv[:, tb, m, :], ti[:, tb, m, :]) for tb in range(TB)
                   for m in range(2 * PEER_H)], [t_sc, *t_all])
        t_tf = v("copy", tf, U(ti), w=[t])
        for tb in range(TB):
            tvh = tv[:, tb].rearrange("p (h m) k -> p h m k", m=2)
            shape = [P, PEER_H, TOPK, TOPK]
            t = v("tt", cand.rearrange("p h (i j) -> p h i j", i=TOPK), tvh[:, :, 0, :].unsqueeze(3).to_broadcast(shape),
                  tvh[:, :, 1, :].unsqueeze(2).to_broadcast(shape), ALU.add, w=[t, *t_all])
            t = top16([(cand[:, hh, :], bv[:, tb, hh, :], bp[:, tb, hh, :]) for hh in range(PEER_H)], [t])
        t1 = v("ts", U(pi), U(bp), 4, None, ALU.logical_shift_right, w=[t])
        t2 = v("ts", U(pj), U(bp), 15, None, ALU.bitwise_and)
        t1 = v("copy", bp, U(pi), w=[t1, t2])
        t2 = v("copy", pi, U(pj), w=[t2, t1])
        for src, m, dst in ((bp, 0, sa), (pi, 1, sbb)):
            for tb in range(TB):
                tfh = tf[:, tb].rearrange("p (h m) k -> p h m k", m=2)
                t = v("tt", oneh, iota[:, 0:TOPK].unsqueeze(1).unsqueeze(1).to_broadcast(shape),
                      src[:, tb].unsqueeze(3).to_broadcast(shape), ALU.is_equal, w=[t, t1, t2, t_tf])
                t = v("tt", oneh, oneh, tfh[:, :, m, :].unsqueeze(2).to_broadcast(shape), ALU.mult, w=[t])
                t = v("red", dst[:, tb, :].rearrange("p (h k) -> p h k", h=PEER_H), oneh, AX.X, ALU.add, w=[t])
        bvf = bv.rearrange("p b h k -> p (b h) k")
        sgf = sg_.rearrange("p b (h k) -> p (b h) k", h=PEER_H)
        t1 = v("tt", sgf, bvf, bvf[:, :, 0:1].to_broadcast([P, 16, TOPK]), ALU.subtract)
        t1 = s(sgf, sgf, ACT.Exp, w=[t1])
        t1 = v("red", stat[:, 8:24], sgf, AX.X, ALU.add, w=[t1])
        t1 = v("recip", stat[:, 8:24], stat[:, 8:24], w=[t1])
        t1 = v("tt", sgf, sgf, stat[:, 8:24].unsqueeze(2).to_broadcast([P, 16, TOPK]), ALU.mult, w=[t1])
        wait(PE, t, t1, *others())
        for n, src in enumerate((sa, sbb, sg_)):
            for tb in range(TB):
                ins = tr(ps[:, n, tb * P:tb * P + P], src[:, tb, :])
        t = done(ins)
        for n, dst in enumerate((sel_a, sel_b)):
            s(dst[:], ps[:, n, 0:S], ACT.Copy, w=[t])
        rest = ps[:, 2, 0:S]
        for n in range(3):
            t_sel = s(gate_parts[:, n, :], rest, ACT.Copy, w=[t])
            if n < 2:
                left = zs[:, n * S:n * S + S]
                t = v("tt", left, rest, gate_parts[:, n, :], ALU.subtract, w=[t_sel])
                rest = left

        G = arena[:, :].rearrange("p (a t) -> p a t", a=HALF_A)
        hit_b = zs[:].bitcast(bf16).rearrange("p (n g b t) -> p n g b t", n=2, g=2, t=4)
        first = wf[:].bitcast(bf16)
        hit_a = first[:, 0:512].rearrange("p (g a t) -> p g a t", g=2, t=4)
        gated = first[:, 512:2048].rearrange("p (g q a t) -> p g q a t", g=2, q=3, t=4)
        hits_used = [[Count(nc, ctx, f"hits_used{n}{g}") for g in range(2)] for n in range(2)]
        g_read = [Count(nc, ctx, f"gate_bank_read{n}") for n in range(2)]

        def build_gates(half):
            keys_a = key4[:, half * HALF_A:half * HALF_A + HALF_A, :]
            steps = {dve: 8, **{c: 1 for used_n in hits_used for c in used_n}, **{c: 1 for c in g_read}}
            with loop(nc, S // 16, steps) as i:
                for n in range(2):
                    t0 = i * 16 + n * 8
                    of_tokens = lambda x: x[:, bass.ds(t0, 8)].rearrange("p (g t) -> p g t", g=2).unsqueeze(2)
                    shape = [P, 2, HALF_A, 4]
                    t_a = v("tt", hit_a, keys_a.unsqueeze(1).to_broadcast(shape), of_tokens(sel_a).to_broadcast(shape),
                            ALU.is_equal, w=[dve.now])
                    shape = [P, 2, NKEYS, 4]
                    v("tt", hit_b[:, n], key4[:].unsqueeze(1).to_broadcast(shape), of_tokens(sel_b).to_broadcast(shape),
                      ALU.is_equal, w=[hits_used[n][1].now])
                    shape = [P, 3, HALF_A, 4]
                    for g in range(2):
                        t = v("tt", gated[:, g], hit_a[:, g].unsqueeze(1).to_broadcast(shape),
                              gate_parts[:, :, bass.ds(t0 + 4 * g, 4)].unsqueeze(2).to_broadcast(shape), ALU.mult,
                              w=[t_a, hits_used[1 - n][g].now])
                        wait(PE, t, g_read[n].now)
                        for j in range(4):
                            col = (4 * g + j) * HALF_A
                            for q in range(3):
                                ins = mm(ps[:, 6 + n, col:col + HALF_A], hit_b[:, n, g, :, j], gated[:, g, q, :, j],
                                         q == 0, q == 2)
                        hits_used[n][g].add(ins)
                    wait(ACTE, hits_used[n][1].now)
                    g_read[n].add(ACTE.activation(G[:, :, bass.ds(t0, 8)],
                                                  ps[:, 6 + n, :].rearrange("p (t a) -> p a t", t=8), ACT.Copy))

        def weigh_start(t_w):
            wait(PE, z_read.now, *t_w)
            for m in range(EX_A):
                for tb in range(TB):
                    ins = tr(ps[:, 6 + m // 2, (m % 2) * S + tb * P:(m % 2) * S + tb * P + P],
                             zs[:, tb * 512 + m * P:tb * 512 + m * P + P])
            return s(wf[:], banks(6, 2), ACT.Gelu, w=[done(ins), *t_w])

        def weigh_end(c_local, t):
            w4 = wf[:].rearrange("p (a t) -> p a t", a=EX_A)
            t = v("tt", w4, w4, G[:, bass.ds(c_local * EX_A, EX_A), :], ALU.mult, w=[t])
            split(wh[:], wl[:], w4, [t])

        def ex_step(c_local, refill):
            t_w = act.now, dve.now
            hidden_products(refill)
            wait(ACTE, used[1].now, pe.now)
            z_read.add(ACTE.activation(zs[:], banks(4, 2), ACT.Copy))
            refill(1)
            add_products(2, 0, t_w)
            refill(2)
            add_products(3, 2, t_w)
            t = weigh_start(t_w)
            refill(3)
            weigh_end(c_local, t)

        def ex_open():
            t_w = (*everything(), *(c.now for c in g_read))
            wait(ACTE, *t_w)
            z_read.add(ACTE.activation(zs[:], banks(4, 2), ACT.Copy))
            pump(2)
            t = weigh_start(t_w)
            weigh_end(0, t)
            pump()

        wait(POOL, *everything())
        t_y0 = pool.add(POOL.memset(wl[:, 0:2, :].bitcast(f32), 0.0))
        wait(DVE, *everything(), t_sel)
        wait(ACTE, *everything())
        wait(PE, *others())
        build_gates(0)
        clear_sums(t_y0)
        ex_open()
        steps = {act: 2, dve: 2, pe: 1, z_read: 1, **{c: 1 for c in used}, **{c: 16 for c in load},
                 **{c: 1 for c in split_hi}, **{c: 1 for c in split_lo}}

        def ex_loop(first, n, offset):
            assert at["split"] == at["use"] + 4 and at["load"] == at["use"] + 8
            with loop(nc, n, steps) as j:
                def refill(slot, j=j):
                    emit_split(slot)
                    if slot < 2:
                        emit_load("ex_u", 2 * j + (2 * (first + 2) + slot), slot)
                    else:
                        emit_load("ex_v", 2 * j + (2 * (first + 1) + slot - 2), slot)
                ex_step(j + (first - offset), refill)
            at_loop(n, 4)

        ex_loop(1, EX_N // 2 - 1, 0)
        t_w = act.now, dve.now
        add_products(2, 0, t_w)
        add_products(3, 2, t_w)
        t_rows = used[3].now
        hidden_products(later)
        at["use"] += 4
        wait(DVE, act.now, t_rows)
        wait(ACTE, dve.now, t_rows)
        wait(PE, *others())
        build_gates(1)
        ex_open()
        ex_loop(EX_N // 2 + 1, EX_N // 2 - 3, EX_N // 2)
        for c in (EX_N - 2, EX_N - 1):
            ex_step(c - EX_N // 2, pumped)
        t_w = act.now, dve.now
        add_products(2, 0, t_w)
        add_products(3, 2, t_w, stop=True)
        g2 = carve(0, D)
        t_g2 = spread_gate(5, g2, 1024, 4, everything())
        t_h = add_residual([used[3].now, t_g2], gate=(g2, carve(2048, TB, D)))
        return finish(nc, SP, h, out, ctx, [t_h], fetch)


def log_sigmoid_pieces(v, s, ALU, ACT, x, e, w):
    t = s(e, x, ACT.Abs, w=w)
    t = s(e, e, ACT.Exp, w=[t], scale=-1.0)
    return s(e, e, ACT.Ln, w=[t], bias=1.0)


def softmax(v, s, ALU, ACT, AX, sc, dst, stat, n_heads, w, P):
    t = v("red", stat[:, 40:40 + n_heads], sc, AX.X, ALU.max, w=w, negate=True)
    for hh in range(n_heads):
        t = s(dst[:, hh], sc[:, hh], ACT.Exp, w=[t, *w] if hh == 0 else [], bias=stat[:, 40 + hh:41 + hh],
              accum_out=stat[:, 48 + hh:49 + hh])
    t = v("recip", stat[:, 48:48 + n_heads], stat[:, 48:48 + n_heads], w=[t])
    return v("tt", dst, dst, stat[:, 48:48 + n_heads].unsqueeze(2).to_broadcast([P, n_heads, sc.shape[2]]),
             ALU.mult, w=[t])


def finish(nc, SP, h, out, ctx, w, fetch):
    t = fetch("stored", [(out, h[:])], w=w)
    wait(SP, t)


def layout(i):
    def w(x):
        return np.asarray(x)[0] if np.asarray(x).ndim > 2 else np.asarray(x)

    def slabs(m):
        k, n = m.shape
        m = m.reshape(k // 512, 4, P, n // 512, 512).transpose(3, 0, 2, 1, 4)
        return np.ascontiguousarray(m).reshape(-1, P, SLAB)

    def fcols(x):
        return np.asarray(x).reshape(-1, P).T

    def tok(x):
        return np.ascontiguousarray(np.asarray(x).reshape(TB, P, D).transpose(1, 0, 2))

    def rep(x):
        return np.ascontiguousarray(np.broadcast_to(np.asarray(x).reshape(1, -1), (P, np.asarray(x).size)))

    def small(m):
        return np.ascontiguousarray(m.reshape(KT, P, m.shape[1]).transpose(1, 0, 2))

    f4 = np.float32
    cols = np.zeros((P, 192), f4)
    cols[:, 0:8], cols[:, 8:16] = fcols(i["g_mix"]), fcols(i["g_mem_kv"])
    cols[:, 16:24], cols[:, 24:32] = fcols(i["g_mem_q"]), fcols(i["g_ffn"])
    cols[0:64, 32], cols[0:64, 33] = i["g_q_fox"][0], i["g_k_fox"][0]
    cols[64:66, 32:34] = 1
    cols[:, 34], cols[:, 35] = i["g_q_mem"][0], i["g_k_mem"][0]
    cols[:, 36:40] = fcols(i["pool_scale"])
    cols[:, 41:49] = fcols(i["c_2"])
    cols[:, 57:65], cols[:, 65:73] = fcols(i["g_norm1_2"]), fcols(i["g_norm2_2"])
    cols[:, 73:121] = fcols(i["b_ada_2"])
    cols[0:64, 121], cols[0:64, 122] = i["g_q_sb_2"][0], i["g_k_sb_2"][0]
    cols[:, 124:156] = np.asarray(i["conv_w_2"])[0].reshape(CONV, 8, P).transpose(2, 1, 0).reshape(P, 32)
    cols[0:ML_H, 172], cols[0:ML_H, 173] = i["b_igate_2"][0], i["b_fgate_2"][0]

    w_in, w_in2 = w(i["w_in"]), w(i["w_in_2"])
    gu = w(i["w_gate_up"]).reshape(D, 2, FF_N, FF_C).transpose(0, 2, 1, 3).reshape(D, FF_N * 512)
    ada = w(i["w_ada_2"]).reshape(KT, P, 3, SLAB).transpose(0, 2, 1, 3)
    q, k, v_, qk, vm, om = (w_in2[:, x:y] for x, y in
                            ((0, 512), (512, 1024), (1024, 1536), (1536, 2560), (2560, 3072), (3072, 3584)))
    c = constants()
    return {
        "x": tok(i["x"]), "mem": tok(i["mem"]), "cols": cols,
        "ident": c["ident"], "ones": c["ones"], "iota": c["iota"], "fox_mask": c["fox_mask"], "upto": c["upto"],
        "ml_mask": c["ml_mask"], "sb_keep": c["sb_keep"], "sb_mask": c["sb_mask"], "after": c["after"],
        "bands": np.ascontiguousarray(c["bands"]),
        "b_forget": rep(i["b_forget"]), "w_f": small(w_in[:, 2048:2056]), "w_if": small(w_in2[:, 3584:3592]),
        "w_pool": np.ascontiguousarray(w(i["w_pool"]).transpose(1, 0, 2)).reshape(P, 512),
        "g_out": rep(np.concatenate([np.asarray(i["g_out_sb_2"]).ravel(), np.asarray(i["g_out_ml_2"]).ravel()])),
        "sub_keys": np.ascontiguousarray(w(i["sub_keys_2"]).transpose(3, 0, 1, 2)).reshape(P, SLAB),
        "w_mem_kv": slabs(w(i["w_mem_kv"])), "w_in": slabs(w_in[:, 0:2048]), "w_out": slabs(w(i["w_out"])),
        "w_mem_q": slabs(w(i["w_mem_q"])), "w_mem_out": slabs(w(i["w_mem_out"])), "w_gu": slabs(gu),
        "w_down": np.ascontiguousarray(w(i["w_down"]).reshape(FF_N, 2, P, D).transpose(0, 2, 1, 3)).reshape(-1, P, SLAB),
        "w_ada": np.ascontiguousarray(ada).reshape(-1, P, SLAB),
        "w_in_2": slabs(np.concatenate([qk, q, k, vm, v_, om], axis=1)),
        "w_out_2": slabs(w(i["w_out_2"])), "w_q_peer": slabs(w(i["w_q_peer_2"])),
        "ex_u": slabs(w(i["expert_u_2"]).T),
        "ex_v": np.ascontiguousarray(w(i["expert_v_2"]).reshape(-1, 2, P, D).transpose(0, 2, 1, 3)).reshape(-1, P, SLAB),
    }


def kernel(**inputs):
    import concourse.bacc as bacc
    from concourse.bass_utils import run_bass_kernel_spmd

    arrays = layout(inputs)
    nc = bacc.Bacc("TRN2", target_bir_lowering=False, num_devices=1)
    aps = {n: nc.dram_tensor("in_" + n, x.shape, mybir.dt.from_np(x.dtype), kind="ExternalInput").ap()
           for n, x in arrays.items()}
    out = nc.dram_tensor("out", (P, TB, D), mybir.dt.float32, kind="ExternalOutput").ap()
    program(nc, aps, out)
    r = run_bass_kernel_spmd(nc, [{"in_" + n: x for n, x in arrays.items()}], core_ids=[0])
    return np.ascontiguousarray(r.results[0]["out"].transpose(1, 0, 2)).reshape(1, S, D)
```

```python
import numpy as np
from contextlib import ExitStack, contextmanager

import concourse.bass as bass
from concourse import mybir

P = 128
S = 256
TB = S // P
D = 1024
KT = D // P
SLAB = 2048
FOX_H, FOX_D = 8, 64
FOX_A = FOX_D + 2
POOL_WINDOWS = (2, 4, 8, 16)
MEM_H, MEM_D = 4, 128
D_FF = 2816
FF_C = 256
FF_N = D_FF // FF_C
SB_H, SB_D = 8, 64
ML_H, ML_D = 4, 128
CONV = 4
PEER_H, NKEYS, TOPK = 8, 128, 16
SEL = PEER_H * TOPK
EX_A = 4
EX_N = NKEYS // EX_A
HALF_A = NKEYS // 2
EPS = 1e-6
BIG = 1e30
N_MOD = 6


def constants():
    i = np.arange(P)
    row, col = i[:, None], i[None, :]
    bands = np.zeros((TB, P, len(POOL_WINDOWS), S), np.float32)
    t, s = np.arange(S)[None, :], np.arange(S)[:, None]
    for g, w in enumerate(POOL_WINDOWS):
        inside = (s <= t) & (s > t - w)
        bands[:, :, g] = (inside / np.minimum(t + 1, w) - (s == t)).reshape(TB, P, S)
    parts = {
        "ident": (row == col), "ones": np.ones((P, P)), "iota": np.broadcast_to(col, (P, P)),
        "fox_mask": np.where(col <= row, 0, -BIG),
        "ml_mask": np.where(row <= col, 0, -BIG),
        "sb_keep": (row < col),
        "sb_mask": np.where(row < col, 0, BIG),
        "upto": (row <= col),
        "after": (row > col),
        "bands": bands.transpose(1, 0, 2, 3).reshape(P, -1),
    }
    return {k: np.ascontiguousarray(v, dtype=np.float32) for k, v in parts.items()}


class Count:

    def __init__(self, nc, ctx, name):
        self.sem = ctx.enter_context(nc.semaphore(name))
        self.base, self.k = 0, 0

    @property
    def now(self):
        return self, self.base + self.k

    def add(self, ins, by=1):
        ins.then_inc(self.sem, by)
        self.k += by
        return self.now


def wait(eng, *tokens):
    for t in tokens:
        if t is not None and not (isinstance(t[1], int) and t[1] <= 0):
            eng.wait_ge(t[0].sem, t[1])


@contextmanager
def loop(nc, n, steps):
    before = {c: c.base + c.k for c in steps}
    with nc.Fori(0, n) as i:
        for c, d in steps.items():
            c.base, c.k = before[c] + i * d, 0
        yield i
        for c, d in steps.items():
            assert c.k == d, (c.sem, c.k, d)
    for c, d in steps.items():
        c.base, c.k = before[c] + n * d, 0


def program(nc, a, out, stage="all"):
    f32, f32r, bf16, u32 = mybir.dt.float32, mybir.dt.float32r, mybir.dt.bfloat16, mybir.dt.uint32
    ALU, ACT, AX = mybir.AluOpType, mybir.ActivationFunctionType, mybir.AxisListType
    PE, DVE, ACTE, POOL, SP = nc.tensor, nc.vector, nc.scalar, nc.gpsimd, nc.sync
    ctx = ExitStack()
    with ctx:
        def sb(name, shape, dt=f32):
            return ctx.enter_context(nc.sbuf_tensor(name, shape, dt))

        NSLOT = 4
        raw = sb("slab_raw", [P, NSLOT, SLAB])
        slab_hi = sb("slab_hi", [P, NSLOT, SLAB], f32r)
        slab_lo = sb("slab_lo", [P, NSLOT, SLAB], f32r)
        h = sb("residual", [P, TB, D])
        xh = sb("x_hi", [P, KT, S], f32r)
        xl = sb("x_lo", [P, KT, S], f32r)
        zs = sb("hidden", [P, 1024])
        wf = sb("weighted", [P, 1024])
        wh = sb("weighted_hi", [P, EX_A, S], f32r)
        wl = sb("weighted_lo", [P, EX_A, S], f32r)
        arena = sb("arena", [P, HALF_A * S])
        ident = sb("ident", [P, P])
        ones = sb("ones", [P, P])
        iota = sb("iota", [P, P])
        sel_a = sb("selected_first_keys", [P, S], bf16)
        sel_b = sb("selected_second_keys", [P, S], bf16)
        gate_parts = sb("selected_gates_in_parts", [P, 3, S], bf16)
        key4 = sb("key_numbers_by_4", [P, NKEYS, 4], bf16)
        cols = sb("columns", [P, 256])
        stat = sb("statistics", [P, 64])
        wsm_h = sb("small_weight_hi", [P, KT, 8], f32r)
        wsm_l = sb("small_weight_lo", [P, KT, 8], f32r)
        ps = ctx.enter_context(nc.psum_tensor("psum", [P, 8, 512], f32))

        def carve(at, *shape, parts=P):
            n = int(np.prod(shape))
            assert at + n <= HALF_A * S
            v = arena[0:parts, at:at + n]
            names = "abcd"[:len(shape)]
            if len(shape) > 1:
                v = v.rearrange(f"p ({' '.join(names)}) -> p {' '.join(names)}",
                                **{names[i]: shape[i] for i in range(len(shape))})
            return v

        def banks(b, n):
            return ps[:, b:b + n, :].rearrange("p b n -> p (b n)")

        pe, dve, act, pool = (Count(nc, ctx, n) for n in ("pe_done", "dve_done", "act_done", "pool_done"))
        z_read = Count(nc, ctx, "hidden_banks_read")
        load = [Count(nc, ctx, f"raw_loaded{s}") for s in range(NSLOT)]
        split_hi = [Count(nc, ctx, f"slab_hi_ready{s}") for s in range(NSLOT)]
        split_lo = [Count(nc, ctx, f"slab_lo_ready{s}") for s in range(NSLOT)]
        used = [Count(nc, ctx, f"slab_used{s}") for s in range(NSLOT)]

        def v(fn, *args, w=(), **kw):
            wait(DVE, *w)
            return dve.add(dve_ops[fn](*args, **kw))

        dve_ops = {"tt": DVE.tensor_tensor, "ts": DVE.tensor_scalar, "stt": DVE.scalar_tensor_tensor,
                        "copy": DVE.tensor_copy, "red": DVE.tensor_reduce, "recip": DVE.reciprocal,
                        "scan": DVE.tensor_tensor_scan, "max": DVE.max, "idx": DVE.max_index,
                        "repl": DVE.match_replace, "set": DVE.memset}

        def s(out, in_, func, w=(), **kw):
            wait(ACTE, *w)
            return act.add(ACTE.activation(out, in_, func, **kw))

        def mm(out, lhsT, rhs, start=True, stop=True):
            return PE.matmul(out, lhsT, rhs, start=start, stop=stop)

        def tr(out, in_):
            return PE.transpose(out, in_, ident[0:in_.shape[0], 0:in_.shape[0]])

        def done(ins):
            return pe.add(ins)

        def mm3(out, ah, al, bh, bl, start, stop):
            mm(out, ah, bh, start, False)
            mm(out, ah, bl, False, False)
            return mm(out, al, bh, False, stop)

        def everything():
            return pe.now, *(c.now for c in used), z_read.now, dve.now, act.now, pool.now

        def others():
            return dve.now, act.now, pool.now, z_read.now

        def fetch(name, pairs, w=()):
            c = Count(nc, ctx, name)
            wait(SP, *w)
            for dst, src in pairs:
                c.add(SP.dma_start(dst, src), 16)
            return c.now

        plan = []
        at = {"load": 0, "split": 0, "use": 0}

        def queue(entries):
            plan.extend(entries)

        def cyc(name, n):
            first = len(plan)
            queue([(name, j, (first + j) % NSLOT) for j in range(n)])

        def emit_load(name, j, slot):
            wait(SP, split_hi[slot].now, split_lo[slot].now)
            src = a[name].rearrange("n p m -> (n p) m")[bass.ds(j * P, P), :]
            load[slot].add(SP.dma_start(raw[:, slot, :], src), 16)

        def emit_split(slot):
            wait(ACTE, load[slot].now, used[slot].now)
            split_hi[slot].add(ACTE.activation(slab_hi[:, slot, :], raw[:, slot, :], ACT.Copy))
            wait(DVE, split_hi[slot].now)
            split_lo[slot].add(DVE.tensor_tensor(slab_lo[:, slot, :], raw[:, slot, :],
                                                 slab_hi[:, slot, :].bitcast(f32), ALU.subtract))

        def last_of(slot, before):
            return max((n for n in range(before) if plan[n][2] == slot), default=-1)

        def pump_loads():
            while at["load"] < len(plan) and last_of(plan[at["load"]][2], at["load"]) < at["split"]:
                emit_load(*plan[at["load"]])
                at["load"] += 1

        def pump(n=99):
            pump_loads()
            while n and at["split"] < at["load"] and last_of(plan[at["split"]][2], at["split"]) < at["use"]:
                emit_split(plan[at["split"]][2])
                at["split"] += 1
                n -= 1
                pump_loads()

        def pump_to(n):
            pump(max(0, n - (at["split"] - at["use"])))

        def take():
            while at["split"] <= at["use"]:
                pump(1)
            slot = plan[at["use"]][2]
            at["use"] += 1
            wait(PE, split_hi[slot].now, split_lo[slot].now)
            return slot

        def parts(slot, k, n):
            shape = dict(k=k, n=n)
            return tuple(t[:, slot, :].rearrange("p (k n) -> p k n", **shape) for t in (slab_hi, slab_lo))

        x_written = {0: (), 1: ()}

        def wait_x(half):
            wait(PE, *x_written[half])
            x_written[half] = ()

        def gemm_tok(bank, half, slot, k0, nk=4, last=True, first=True):
            bh, bl = parts(slot, 4, 512)
            for tb in range(TB):
                tok = slice(tb * P, tb * P + P)
                for k in range(nk):
                    ins = mm3(ps[:, bank + tb, :], xh[:, k0 + k, tok], xl[:, k0 + k, tok], bh[:, k], bl[:, k],
                              first and k == 0, last and k == nk - 1)
            return ins

        def gemm_chunk(bank, free=()):
            wait(PE, *free)
            for half in range(2):
                slot = take()
                wait_x(half)
                ins = gemm_tok(bank, half, slot, 4 * half, first=half == 0, last=half == 1)
                if half == 0:
                    used[slot].add(ins)
                    pump_to(3)
            return used[slot].add(ins)

        def small_products(w):
            wait(PE, *w)
            for tb in range(TB):
                for k in range(KT):
                    ins = mm3(ps[:, 7, tb * 8:tb * 8 + 8], xh[:, k, tb * P:tb * P + P], xl[:, k, tb * P:tb * P + P],
                              wsm_h[:, k], wsm_l[:, k], k == 0, k == KT - 1)
            return done(ins)

        cyc("w_mem_kv", 4)
        cyc("w_in", 8)
        cyc("w_out", 4)
        cyc("w_mem_q", 2)
        cyc("w_mem_out", 2)
        ff = [("w_gu", 0, 0), ("w_gu", 1, 1)]
        for c in range(1, FF_N):
            ff += [("w_gu", 2 * c, 0), ("w_gu", 2 * c + 1, 1), ("w_down", c - 1, 2)]
        queue(ff + [("w_down", FF_N - 1, 2)])
        cyc("w_in_2", 14)
        cyc("w_out_2", 4)
        cyc("w_q_peer", 8)
        ex = [("ex_u", 0, 0), ("ex_u", 1, 1)]
        for c in range(1, EX_N):
            columns = [("ex_u", 2 * c, 0), ("ex_u", 2 * c + 1, 1)]
            rows = [("ex_v", 2 * c - 2, 2), ("ex_v", 2 * c - 1, 3)]
            ex += rows + columns if c == EX_N // 2 else columns + rows
        queue(ex + [("ex_v", 2 * EX_N - 2, 2), ("ex_v", 2 * EX_N - 1, 3)])

        gm = arena[:, 14336:16384].rearrange("p (b n) -> p b n", b=TB)
        t_mem = {tb: [fetch(f"mem_loaded{tb}", [(gm[:, tb], a["mem"][:, tb])])] for tb in range(TB)}
        CM, CKV, CQ, CF = 0, 8, 16, 24
        C_FOXQ, C_FOXK, C_MEMQ, C_MEMK, C_PS, C_EPS = 32, 33, 34, 35, 36, 40
        C_CT, C_SC, C_N1, C_N2, C_ADA, C_SBQ, C_SBK, C_CONV = 41, 49, 57, 65, 73, 121, 122, 124
        C_G1, C_G2, C_BG = 156, 164, 172
        t_col = fetch("columns_loaded", [(cols[:, 0:192], a["cols"]), (ident[:], a["ident"]), (ones[:], a["ones"]),
                                         (iota[:], a["iota"])])
        pump_loads()
        t_x = fetch("x_loaded", [(h[:], a["x"])])
        nc.scalar.preload_act_table_set("natural_log_exp_and_others")

        def rstd(n, width, at0, w):
            t = v("ts", stat[:, at0:at0 + n], stat[:, at0:at0 + n], 1.0 / width, EPS, ALU.mult, ALU.add, w=w)
            wait(POOL, t)
            return pool.add(POOL.tensor_tensor(stat[:, at0:at0 + n], stat[:, at0:at0 + n],
                                               minus_half[:, 0:n], ALU.pow))

        minus_half = sb("minus_half", [P, 16])
        t_mh = pool.add(POOL.memset(minus_half[:], -0.5))

        def split(dst_h, dst_l, full, w):
            wait(DVE, *w)
            t = s(dst_h, full, ACT.Copy, w=w)
            return v("tt", dst_l, full, dst_h.bitcast(f32), ALU.subtract, w=[t])

        def norm_to_x(src, gain, t_src, t_gain=None, shift=None, scr=0, bank=0, ready=True):
            def low(high):
                two, t = high
                v("tt", xl[:, two], full[:, two], xh[:, two].bitcast(f32), ALU.subtract, w=[t, *last_use()])

            free = everything()
            xs = carve(scr, TB, D)
            full = carve(scr + TB * D, KT, S)
            for tb in range(TB):
                w = [*t_src[tb], *(f for f in free if f[0] is not dve)] if isinstance(t_src, dict) else [*t_src, *free]
                t = s(xs[:, tb, :], src[:, tb, :], ACT.Square, w=w, accum_out=stat[:, tb:tb + 1])
            t = rstd(TB, D, 0, [t, t_mh])
            if ready:
                pump_to(1)
            for tb in range(TB):
                t = v("ts", xs[:, tb, :], src[:, tb, :], stat[:, tb:tb + 1], None, ALU.mult, w=[*free, t, act.now])
            high = None
            for b in range(4):
                wait(PE, *free, t, *last_use())
                for k in (2 * b, 2 * b + 1):
                    for tb in range(TB):
                        ins = tr(ps[:, bank + b, (k % 2) * S + tb * P:(k % 2) * S + tb * P + P],
                                 xs[:, tb, k * P:k * P + P])
                tp = done(ins)
                two = slice(2 * b, 2 * b + 2)
                src_p = ps[:, bank + b, :].rearrange("p (k n) -> p k n", k=2)
                tf = v("tt", full[:, two], src_p, gain[:, two].unsqueeze(2).to_broadcast([P, 2, S]), ALU.mult, w=[tp, t_gain])
                if shift is not None:
                    tf = v("tt", full[:, two], full[:, two], shift[:, two].unsqueeze(2).to_broadcast([P, 2, S]),
                           ALU.add, w=[tf])
                if b:
                    low(high)
                high = two, s(xh[:, two], full[:, two], ACT.Copy, w=[tf, *last_use()])
                if b == 2:
                    x_written[0] = high_before, dve.now
                    if ready:
                        pump_to(2)
                high_before = high[1]
            low(high)
            x_written[1] = high[1], dve.now
            return x_written[1]

        def last_use():
            return [c.now for c in used]

        def head_norm(src, dst, n_heads, d, at0, w, scratch):
            t = s(scratch, src, ACT.Square, w=w)
            t = v("red", stat[:, at0:at0 + n_heads], scratch, AX.X, ALU.add, w=[t])
            t = rstd(n_heads, d, at0, [t])
            return v("tt", dst, src, stat[:, at0:at0 + n_heads].unsqueeze(2).to_broadcast([P, n_heads, d]),
                     ALU.mult, w=[t, *w])

        return_stage = []

        A_MKT, A_MV, A_V, A_PIN, A_QT, A_KT, A_P, A_PT, A_MIX = 0, 1024, 2048, 3072, 4096, 6144, 8192, 12288, 15360
        wait(PE, t_col)
        norm_to_x(gm, cols[:, CKV:CKV + 8], t_mem, t_col, scr=4096, bank=0, ready=False)
        t_k = gemm_chunk(4)
        t_v = gemm_chunk(6)
        mkn = carve(A_QT, 8, MEM_D)
        mksq = carve(A_KT, 8, MEM_D)
        t = head_norm(banks(4, 2).rearrange("p (h d) -> p h d", d=MEM_D), mkn, 8, MEM_D, 8, [t_k], mksq)
        mv = carve(A_MV, TB, 512)
        t_mv = s(mv, ps[:, 6:8, :], ACT.Copy, w=[t_v])
        mkT = carve(A_MKT, MEM_H, S)

        def head_transposes(dst, srcs, bank, n_rows, gain, w):
            for b in range(len(srcs) // 2):
                wait(PE, *w)
                for j in range(2):
                    for tb in range(TB):
                        o = j * S + tb * P
                        ins = tr(ps[0:n_rows, bank + b, o:o + P], srcs[2 * b + j][tb])
                tp = done(ins)
                t = s(dst[:, 2 * b:2 * b + 2, :], ps[0:n_rows, bank + b, :].rearrange("p (h n) -> p h n", h=2),
                      ACT.Copy, w=[tp, *w], scale=gain)
            return t

        t_cs = v("ts", cols[:, C_MEMQ:C_MEMQ + 1], cols[:, C_MEMQ:C_MEMQ + 1], MEM_D ** -0.5, None, ALU.mult, w=[t_col])
        t_cs = v("ts", cols[0:FOX_D, C_FOXQ:C_FOXQ + 1], cols[0:FOX_D, C_FOXQ:C_FOXQ + 1], FOX_D ** -0.5, None,
                 ALU.mult)
        t_cs = v("ts", cols[0:SB_D, C_SBQ:C_SBQ + 1], cols[0:SB_D, C_SBQ:C_SBQ + 1], SB_D ** -0.5, None, ALU.mult)
        mkn_h = [[mkn[:, tb * MEM_H + hh, :] for tb in range(TB)] for hh in range(MEM_H)]
        t_mk = head_transposes(mkT, mkn_h, 0, P, cols[:, C_MEMK:C_MEMK + 1], [t, t_cs])

        wsm = carve(14336, KT, 8)
        t_ws = fetch("forget_weight_loaded", [(wsm, a["w_f"])], w=everything())
        t_wsm = split(wsm_h[:], wsm_l[:], wsm, [t_ws])
        t_bf = fetch("block1_constants_loaded", [(carve(14500, P), a["fox_mask"]), (carve(14628, P), a["upto"]),
                                                 (carve(14800, FOX_H), a["b_forget"])], w=everything())
        fox_mask, upto, bfor = carve(14500, P), carve(14628, P), carve(14800, FOX_H)
        norm_to_x(h, cols[:, CM:CM + 8], [t_x], t_col, scr=8192, bank=0)
        t_q = gemm_chunk(0)
        t_f = small_products([t_wsm, t_mv])
        fl, fe = carve(14816, TB, FOX_H), carve(14832, TB, FOX_H)
        cum = carve(14848, TB, FOX_H)
        t = v("tt", fl, ps[:, 7, 0:16].rearrange("p (b h) -> p b h", b=TB),
              bfor.unsqueeze(1).to_broadcast([P, TB, FOX_H]), ALU.add, w=[t_f, t_bf])
        t = log_sigmoid_pieces(v, s, ALU, ACT, fl, fe, [t])
        t = v("stt", fl, fl, 0.0, fe, ALU.min, ALU.subtract, w=[t])
        wait(PE, t)
        mm(ps[:, 7, 16:24], upto, fl[:, 0, :])
        mm(ps[:, 7, 24:32], ones[:], fl[:, 0, :], True, False)
        t_c = done(mm(ps[:, 7, 24:32], upto, fl[:, 1, :], False, True))
        t_cum = v("copy", cum, ps[:, 7, 16:32].rearrange("p (b h) -> p b h", b=TB), w=[t_c])
        t_k = gemm_chunk(2)
        qa, ka = carve(A_PT, TB, FOX_H, FOX_A), carve(A_PT + 1056, TB, FOX_H, FOX_A)
        qsq = carve(A_P + 2048, 16, FOX_D)
        qa_v = qa.rearrange("p b h d -> p (b h) d")
        ka_v = ka.rearrange("p b h d -> p (b h) d")
        t = head_norm(banks(0, 2).rearrange("p (h d) -> p h d", d=FOX_D), qa_v[:, :, 0:FOX_D], 16, FOX_D, 8, [t_q], qsq)
        cum_v = cum.rearrange("p b h -> p (b h)").unsqueeze(2)
        v("set", qa_v[:, :, FOX_D:FOX_D + 1], 1.0)
        v("copy", qa_v[:, :, FOX_D + 1:FOX_A], cum_v, w=[t_cum])
        v("set", ka_v[:, :, FOX_D + 1:FOX_A], 1.0)
        v("ts", ka_v[:, :, FOX_D:FOX_D + 1], cum_v, -1.0, None, ALU.mult)
        t_v = gemm_chunk(4, free=[t_mv])
        t = head_norm(banks(2, 2).rearrange("p (h d) -> p h d", d=FOX_D), ka_v[:, :, 0:FOX_D], 16, FOX_D, 24,
                      [t_k, dve.now], qsq)
        vt = carve(A_V, TB, 512)
        t_vt = s(vt, ps[:, 4:6, :], ACT.Copy, w=[t_v, t_mk])
        bandsT = carve(A_P, TB, 4, S)
        t_bw = fetch("pool_tables_loaded", [(bandsT, a["bands"]), (zs[:, 0:512], a["w_pool"])], w=[*everything()])
        t_p = gemm_chunk(6, free=[t_cum, t_mv])
        pin = carve(A_PIN, TB, 512)
        t_pin = s(pin, ps[:, 6:8, :], ACT.Copy, w=[t_p])
        qT, kT = carve(A_QT, FOX_H, S, parts=FOX_A), carve(A_KT, FOX_H, S, parts=FOX_A)
        t_qT = head_transposes(qT, [[qa[:, tb, hh, :] for tb in range(TB)] for hh in range(FOX_H)], 0, FOX_A,
                               cols[0:FOX_A, C_FOXQ:C_FOXQ + 1], [t, t_cs, act.now])
        t_kT = head_transposes(kT, [[ka[:, tb, hh, :] for tb in range(TB)] for hh in range(FOX_H)], 4, FOX_A,
                               cols[0:FOX_A, C_FOXK:C_FOXK + 1], [t, act.now])
        mixT = carve(A_MIX, 4, S)
        wait(PE, t_bw, t_pin, act.now, dve.now)
        for g in range(4):
            o = ps[:, g // 2, (g % 2) * S:(g % 2) * S + S]
            for sbk in range(TB):
                ins = mm(o, pin[:, sbk, g * P:g * P + P], bandsT[:, sbk, g, :], sbk == 0, sbk == 1)
        t = done(ins)
        t = s(mixT, banks(0, 2).rearrange("p (g n) -> p g n", g=4), ACT.Copy, w=[t])
        wait(PE, t)
        for g in range(4):
            ins = mm(ps[:, 2 + g // 2, (g % 2) * S:(g % 2) * S + S], zs[:, g * P:g * P + P], mixT[:, g, :])
        t = done(ins)
        t = v("tt", mixT, banks(2, 2).rearrange("p (g n) -> p g n", g=4),
              cols[:, C_PS:C_PS + 4].unsqueeze(2).to_broadcast([P, 4, S]), ALU.mult, w=[t])
        t_cat1 = split(xh[:, 4:8], xl[:, 4:8], mixT, [t, *last_use()])

        prob = carve(A_P, TB, FOX_H, S)
        rows, t_exp = {}, {}
        wait(PE, t_qT, t_kT, *others())
        for tb in (1, 0):
            ns = P * (tb + 1)
            b0 = 4 * (1 - tb)
            for hh in range(FOX_H):
                o = ps[:, b0 + hh // 2, (hh % 2) * S:(hh % 2) * S + ns]
                mm(o, qT[:, hh, tb * P:tb * P + P], kT[:, hh, 0:ns], True, False)
                ins = mm(o[:, ns - P:ns], ident[:], fox_mask, False, True)
            t = done(ins)
            rows[tb] = prob[:, tb, :, 0:ns]
            sc = banks(b0, 4).rearrange("p (h n) -> p h n", h=FOX_H)[:, :, 0:ns]
            t_exp[tb] = softmax_open(v, s, ALU, ACT, AX, sc, rows[tb], stat, 24 * tb, [t, t_cat1, t_qT, t_kT])
        t_prob = {tb: softmax_close(v, ALU, rows[tb], stat, 24 * tb, t_exp[tb]) for tb in (1, 0)}
        pT0, pT1 = carve(A_PT, FOX_H, S), carve(A_PT + 2048, FOX_H, P)
        wait(PE, t_prob[1], t_exp[0])
        for hh in range(FOX_H):
            ins = tr(ps[:, 4 + hh // 4, (hh % 4) * P:(hh % 4) * P + P], prob[:, 1, hh, P:S])
        t_1 = done(ins)
        for hh in range(FOX_H):
            tr(ps[:, hh // 2, (hh % 2) * S + P:(hh % 2) * S + S], prob[:, 1, hh, 0:P])
        wait(PE, t_prob[0])
        for hh in range(FOX_H):
            ins = tr(ps[:, hh // 2, (hh % 2) * S:(hh % 2) * S + P], prob[:, 0, hh, 0:P])
            if hh % 2:
                t = done(ins)
                t = s(pT0[:, hh - 1:hh + 1, :], ps[:, hh // 2, :].rearrange("p (h n) -> p h n", h=2), ACT.Copy,
                      w=[t, pe.now])
        t = t_1
        t1 = v("copy", pT1, banks(4, 2).rearrange("p (h n) -> p h n", h=FOX_H), w=[t])
        wait(PE, t1, act.now)
        for hh in range(FOX_H):
            o = ps[(hh % 2) * FOX_D:(hh % 2) * FOX_D + FOX_D, 6 + hh // 4, (hh // 2 % 2) * S:(hh // 2 % 2) * S + S]
            mm(o, vt[:, 0, hh * FOX_D:hh * FOX_D + FOX_D], pT0[:, hh, :], True, False)
            ins = mm(o[:, P:S], vt[:, 1, hh * FOX_D:hh * FOX_D + FOX_D], pT1[:, hh, :], False, True)
        t = done(ins)
        foxT = carve(A_QT, 4, S)
        t = v("copy", foxT, banks(6, 2).rearrange("p (k n) -> p k n", k=4), w=[t])
        t_cat0 = split(xh[:, 0:4], xl[:, 0:4], foxT, [t, *last_use()])

        def transpose_to_x(src, w, bank):
            for b in range(4):
                wait(PE, *w, *others())
                for k in (2 * b, 2 * b + 1):
                    for tb in range(TB):
                        ins = tr(ps[:, bank + b, (k % 2) * S + tb * P:(k % 2) * S + tb * P + P],
                                 src[:, tb, k * P:k * P + P])
                t = done(ins)
                two = slice(2 * b, 2 * b + 2)
                t = split(xh[:, two], xl[:, two], ps[:, bank + b, :].rearrange("p (k n) -> p k n", k=2), [t, *last_use()])
            return act.now, t

        def out_proj(t_in, gate=None, w=()):
            wait(PE, *t_in, *others())
            for c in range(2):
                for half in range(2):
                    slot = take()
                    wait_x(half)
                    bh, bl = parts(slot, 4, 512)
                    for tb in range(TB):
                        for k in range(4):
                            kk = 4 * half + k
                            ins = mm3(ps[:, 2 * tb + c, :], xh[:, kk, tb * P:tb * P + P], xl[:, kk, tb * P:tb * P + P],
                                      bh[:, k], bl[:, k], kk == 0, kk == 7)
                    used[slot].add(ins)
                    pump_to(2 if c and half else 3)
            return add_residual([used[slot].now, *w], gate)

        def add_residual(w, gate=None):
            t_rows = {}
            for tb in range(TB):
                y = banks(2 * tb, 2)
                if gate is not None:
                    t = v("tt", gate[1][:, tb], y, gate[0], ALU.mult, w=w)
                    t = v("tt", h[:, tb, :], h[:, tb, :], gate[1][:, tb], ALU.add, w=[t])
                else:
                    t = v("tt", h[:, tb, :], h[:, tb, :], y, ALU.add, w=w)
                t_rows[tb] = [t]
            return t_rows

        t_h = out_proj([t_cat1, t_cat0, act.now])

        if stage == "mix":
            return finish(nc, SP, h, out, ctx, t_h[1], fetch)
        norm_to_x(h, cols[:, CQ:CQ + 8], t_h, scr=8192, bank=4)
        t_q = gemm_chunk(0)
        mqn, mqsq = carve(A_V, 8, MEM_D), carve(A_PIN, 8, MEM_D)
        t = head_norm(banks(0, 2).rearrange("p (h d) -> p h d", d=MEM_D), mqn, 8, MEM_D, 8, [t_q], mqsq)
        mqT = carve(A_QT, MEM_H, S)
        t = head_transposes(mqT, [[mqn[:, tb * MEM_H + hh, :] for tb in range(TB)] for hh in range(MEM_H)], 2, P,
                            cols[:, C_MEMQ:C_MEMQ + 1], [t])
        mprob = carve(A_KT, TB, MEM_H, S)
        wait(PE, t)
        t_exp = {}
        for tb in range(TB):
            for hh in range(MEM_H):
                ins = mm(ps[:, 4 + 2 * tb + hh // 2, (hh % 2) * S:(hh % 2) * S + S],
                         mqT[:, hh, tb * P:tb * P + P], mkT[:, hh, :])
            tp = done(ins)
            t_exp[tb] = softmax_open(v, s, ALU, ACT, AX, banks(4 + 2 * tb, 2).rearrange("p (h n) -> p h n", h=MEM_H),
                                     mprob[:, tb], stat, 24 * tb, [tp, t])
        mpT = carve(A_P, TB, MEM_H, S)
        for tb in range(TB):
            wait(PE, softmax_close(v, ALU, mprob[:, tb], stat, 24 * tb, t_exp[tb]))
            t_mp = []
            for mb in range(TB):
                for hh in range(MEM_H):
                    ins = tr(ps[:, 2 * mb + hh // 2, (hh % 2) * S + tb * P:(hh % 2) * S + tb * P + P],
                             mprob[:, tb, hh, mb * P:mb * P + P])
                t_mp.append(done(ins))
        for mb in range(TB):
            src = banks(2 * mb, 2).rearrange("p (h n) -> p h n", h=MEM_H)
            w = [t_mp[mb]]
            t = s(mpT[:, mb], src, ACT.Copy, w=w) if mb == 0 else v("copy", mpT[:, mb], src, w=w)
        wait(PE, dve.now, act.now)
        for hh in range(MEM_H):
            o = ps[:, 4 + hh // 2, (hh % 2) * S:(hh % 2) * S + S]
            for mb in range(TB):
                ins = mm(o, mv[:, mb, hh * MEM_D:hh * MEM_D + MEM_D], mpT[:, mb, hh, :], mb == 0, mb == 1)
        t = done(ins)
        moT = carve(A_QT, 4, S)
        t = v("copy", moT, banks(4, 2).rearrange("p (k n) -> p k n", k=4), w=[t])
        t = split(xh[:, 0:4], xl[:, 0:4], moT, [t, *last_use()])
        wait(PE, t, act.now)
        for c in range(2):
            slot = take()
            bh, bl = parts(slot, 4, 512)
            for tb in range(TB):
                for k in range(4):
                    ins = mm3(ps[:, 2 * tb + c, :], xh[:, k, tb * P:tb * P + P], xl[:, k, tb * P:tb * P + P],
                              bh[:, k], bl[:, k], k == 0, k == 3)
            used[slot].add(ins)
        t_h = add_residual([used[slot].now])
        if stage == "mem":
            return finish(nc, SP, h, out, ctx, t_h[1], fetch)
        ada_load = [Count(nc, ctx, f"ada_loaded{n}") for n in range(3)]
        ada_done = [Count(nc, ctx, f"ada_summed{n}") for n in range(3)]
        ada = carve(0, 3, SLAB)
        ada_raw = carve(6144, 3, SLAB)
        t_free = everything()
        sil, cc = cols[:, C_SC:C_SC + 8], cols[:, C_CT:C_CT + 8]
        t = s(sil, cc, ACT.Exp, w=[t_col], scale=-1.0)
        t = v("ts", sil, sil, 1.0, None, ALU.add, w=[t])
        t = v("recip", sil, sil, w=[t])
        t_sil = v("tt", sil, sil, cc, ALU.mult, w=[t])
        wait(POOL, *t_free)
        t_y0 = pool.add(POOL.memset(wl[:, 0:2, :].bitcast(f32), 0.0))

        def load_ada(k, n, w=()):
            wait(SP, *w, ada_done[n].now)
            src = a["w_ada"].rearrange("n p m -> (n p) m")[bass.ds((k * 3 + n) * P, P), :]
            ada_load[n].add(SP.dma_start(ada_raw[:, n, :], src), 16)

        def sum_ada(k, n):
            wait(DVE, ada_load[n].now, ada_done[n].now, t_az, t_sil)
            ada_done[n].add(DVE.scalar_tensor_tensor(ada[:, n, :], ada_raw[:, n, :], cols[:, bass.ds(C_SC + k, 1)],
                                                     ada[:, n, :], ALU.mult, ALU.add))

        def clear_sums(t_y0):
            wait(PE, t_y0, *others())
            for b in range(4):
                mm(ps[:, b, :], wl[:, 0, 0:P], wl[:, 0:2, :], True, False)

        def slot_ready(slot):
            wait(PE, split_hi[slot].now, split_lo[slot].now)

        def hidden_products(refill):
            wait(PE, z_read.now)
            for half in range(2):
                slot_ready(half)
                wait_x(half)
                used[half].add(gemm_tok(4, half, half, 4 * half, first=half == 0, last=half == 1))
                if half == 0:
                    refill(0)

        def add_products(slot, k0, t_w, stop=False):
            bh, bl = parts(slot, 2, D)
            slot_ready(slot)
            wait(PE, *t_w)
            for tb in range(TB):
                for k in range(2):
                    for half in range(2):
                        n = slice(half * 512, half * 512 + 512)
                        ins = mm3(ps[:, 2 * tb + half, :], wh[:, k0 + k, tb * P:tb * P + P],
                                  wl[:, k0 + k, tb * P:tb * P + P], bh[:, k, n], bl[:, k, n], False, stop and k == 1)
            used[slot].add(ins)

        def ff_step(i, refill, first=False, ada_k=None, ada_next=None):
            t_w = act.now, dve.now
            hidden_products(refill)
            sg = zs[:, 0:512].rearrange("p (b n) -> p b n", b=TB)
            hid = zs[:, 512:1024].rearrange("p (b n) -> p b n", b=TB)
            t = s(sg, ps[:, 4:6, 0:FF_C], ACT.Silu, w=[used[1].now, z_read.now])
            wait(DVE, t, pe.now)
            z_read.add(DVE.tensor_tensor(hid, sg, ps[:, 4:6, FF_C:512], ALU.mult))
            refill(1)
            if not first:
                add_products(2, 0, t_w)
            wait(PE, z_read.now, *t_w)
            for k in range(2):
                for tb in range(TB):
                    ins = tr(ps[:, 6, k * S + tb * P:k * S + tb * P + P], hid[:, tb, k * P:k * P + P])
            t = done(ins)
            if not first:
                refill(2)
            src = ps[:, 6, :].rearrange("p (k n) -> p k n", k=2)
            split(wh[:, 0:2], wl[:, 0:2], src, [t])
            if ada_k is not None:
                for n in range(3):
                    sum_ada(ada_k, n)
                    if ada_next is not None:
                        load_ada(ada_next, n)

        def later(slot):
            pass

        def pumped(slot):
            assert plan[at["use"]][2] == slot
            at["use"] += 1
            pump()

        def at_loop(n_steps, per_step):
            for k in at:
                at[k] += n_steps * per_step

        clear_sums(t_y0)
        norm_to_x(h, cols[:, CF:CF + 8], t_h, scr=12288, bank=4)
        t_az = pool.add(POOL.memset(carve(0, 3 * SLAB), 0.0))
        for n in range(3):
            load_ada(0, n, t_free)
        pump()
        ff_step(0, pumped, first=True)
        FF_L = FF_N - 4
        assert at["split"] == at["use"] + 3 and at["load"] == at["use"] + 6
        steps = {act: 2, dve: 1, pe: 1, z_read: 1, **{used[n]: 1 for n in range(3)},
                 **{load[n]: 16 for n in range(3)}, **{split_hi[n]: 1 for n in range(3)},
                 **{split_lo[n]: 1 for n in range(3)}, **{c: 16 for c in ada_load}, **{c: 1 for c in ada_done}}
        with loop(nc, FF_L, steps) as j:
            def refill(slot, j=j):
                emit_split(slot)
                if slot < 2:
                    emit_load("w_gu", 2 * j + 6 + slot, slot)
                else:
                    emit_load("w_down", j + 2, slot)
            ff_step(j + 1, refill, ada_k=j, ada_next=j + 1)
        at_loop(FF_L, 3)
        for i in range(FF_N - 3, FF_N):
            ff_step(i, pumped, ada_k=i - 1 if i == FF_N - 3 else None)
        add_products(2, 0, [act.now, dve.now], stop=True)
        at["use"] += 1
        t_h = add_residual([used[2].now])
        if stage == "ffn":
            return finish(nc, SP, h, out, ctx, t_h[1], fetch)

        md = cols[:, C_ADA:C_ADA + 48]
        wait(PE, *(c.now for c in ada_done), *others())
        for j in range(48):
            ins = mm(ps[:, 4, 2 * j:2 * j + 2], ada[:, j // 16, (j % 16) * P:(j % 16) * P + P], ones[:, 0:2])
        t = done(ins)
        t = v("tt", md, md, ps[:, 4, 0:96].rearrange("p (j t) -> p j t", t=2)[:, :, 0], ALU.add, w=[t])
        for c_out, c_g, m in ((C_G1, C_N1, 1), (C_G2, C_N2, 4)):
            t_g = v("stt", cols[:, c_out:c_out + 8], cols[:, C_ADA + 8 * m:C_ADA + 8 * m + 8], 1.0,
                    cols[:, c_g:c_g + 8], ALU.add, ALU.mult, w=[t])

        def spread_gate(m, dst, scr, bank, w):
            diag = carve(scr, KT, P)
            t = v("tt", diag, ident[:].unsqueeze(1).to_broadcast([P, KT, P]),
                  cols[:, C_ADA + 8 * m:C_ADA + 8 * m + 8].unsqueeze(2).to_broadcast([P, KT, P]), ALU.mult, w=w)
            wait(PE, t, *others())
            for half in range(2):
                ins = mm(ps[:, bank + half, :], ones[:], carve(scr, TB, 512)[:, half, :])
            t = done(ins)
            return s(dst, banks(bank, 2), ACT.Copy, w=[t])

        B_VSB, B_OML, B_VML, B_CV, B_PRE, B_QT, B_KT, B_QN, B_Y, B_ST = (
            0, 1024, 2048, 3088, 5136, 7208, 9256, 11304, 13352, 15400)
        t_all = everything()
        c2 = {n: wf[:, k * P:k * P + P] for k, n in enumerate(("ml_mask", "sb_keep", "sb_mask", "after"))}
        t_c2 = fetch("block2_constants_loaded", [(c2[n], a[n]) for n in c2] +
                     [(carve(B_ST, KT, 8), a["w_if"])], w=t_all)
        norm_to_x(h, cols[:, C_G1:C_G1 + 8], t_h, t_g, shift=cols[:, C_ADA:C_ADA + 8], scr=B_QT, bank=0)

        def gemm_feat(bank, free=()):
            wait(PE, *free)
            pump_to(2)
            slots = (take(), take())
            if not {slot for _, _, slot in plan[at["split"]:at["use"] + 2]} & set(slots):
                pump_to(2)
            pq = [parts(sl, 4, 512) for sl in slots]
            for m in range(4):
                for k in range(KT):
                    if k % 4 == 0:
                        wait_x(k // 4)
                    bh, bl = pq[k // 4]
                    col = slice(m * P, m * P + P)
                    ins = mm3(ps[:, bank + m // 2, (m % 2) * S:(m % 2) * S + S], bh[:, k % 4, col], bl[:, k % 4, col],
                              xh[:, k, :], xl[:, k, :], k == 0, k == KT - 1)
                    if m == 3 and k == 3:
                        used[slots[0]].add(ins)
            return used[slots[1]].add(ins)

        pre = carve(B_PRE, 8, S + CONV - 1)
        conv = carve(B_CV, 8, S)
        t_z = v("set", pre[:, :, 0:CONV - 1], 0.0, w=t_all)
        for c in range(2):
            t = gemm_feat(2 * c)
            t_pre = s(pre[:, 4 * c:4 * c + 4, CONV - 1:], banks(2 * c, 2).rearrange("p (k n) -> p k n", k=4),
                      ACT.Copy, w=[t, t_z])
            pump_to(2)
        t_if = small_products([split(wsm_h[:], wsm_l[:], carve(B_ST, KT, 8), [t_c2, *t_all])])
        gt = carve(B_ST + 64, TB, 8)
        t = v("copy", gt, ps[:, 7, 0:16].rearrange("p (b h) -> p b h", b=TB), w=[t_if])
        wait(PE, t)
        for m in range(2):
            for tb in range(TB):
                ins = tr(ps[0:ML_H, 6, m * S + tb * P:m * S + tb * P + P], gt[:, tb, m * ML_H:m * ML_H + ML_H])
        t_gr = done(ins)
        t_qs = gemm_chunk(4)
        rows = lambda n: carve(B_Y + n * S, S, parts=ML_H)
        fr, le, cumA, er, cm, em, on4 = (rows(n) for n in range(7))
        t1 = v("set", on4, 1.0, w=t_all)
        t = v("ts", fr, ps[0:ML_H, 6, S:2 * S], cols[0:ML_H, C_BG + 1:C_BG + 2], None, ALU.add, w=[t_gr, *t_all])
        t = log_sigmoid_pieces(v, s, ALU, ACT, fr, le, [t, *t_all])
        t = v("stt", fr, fr, 0.0, le, ALU.min, ALU.subtract, w=[t])
        t = v("scan", cumA, on4, fr, 0.0, ALU.mult, ALU.add, w=[t, t1])
        t = v("stt", er, ps[0:ML_H, 6, 0:S], cols[0:ML_H, C_BG:C_BG + 1], cumA, ALU.add, ALU.subtract, w=[t])
        t = v("scan", cm, on4, er, 0.0, ALU.mult, ALU.max, w=[t])
        t = v("tt", le, cumA, cm, ALU.add, w=[t])
        t_em = s(em, le, ACT.Exp, w=[t], scale=-1.0)
        t_ncm = v("ts", cm, cm, -1.0, None, ALU.mult, w=[t])
        t_ks = gemm_chunk(0, free=[t_pre])
        qn, kn = carve(B_QN, 16, SB_D), carve(B_QN + 1024, 16, SB_D)
        t_qn = head_norm(banks(4, 2).rearrange("p (h d) -> p h d", d=SB_D), qn, 16, SB_D, 8, [t_qs], carve(B_QT, 16, SB_D))
        def convolve(tiles):
            for k in tiles:
                w4 = [cols[:, C_CONV + 4 * k + j:C_CONV + 4 * k + j + 1] for j in range(CONV)]
                t = v("ts", conv[:, k], pre[:, k, 0:S], w4[0], None, ALU.mult, w=[t_pre, *t_all])
                for j in range(1, CONV):
                    t = v("stt", conv[:, k], pre[:, k, j:j + S], w4[j], conv[:, k], ALU.mult, ALU.add, w=[t])
            return t

        t_vm = gemm_chunk(2)
        convolve((0, 1, 2))
        t_kn = head_norm(banks(0, 2).rearrange("p (h d) -> p h d", d=SB_D), kn, 16, SB_D, 24, [t_ks, dve.now],
                         carve(B_QT, 16, SB_D))
        t_vs = gemm_chunk(6, free=[t_em, t_ncm])
        convolve((3, 4, 5))
        vml = carve(B_VML, TB, ML_H, ML_D + 1)
        t_vml = s(vml[:, :, :, 0:ML_D], ps[:, 2:4, :].rearrange("p b (h d) -> p b h d", d=ML_D), ACT.Copy, w=[t_vm, *t_all])
        t_one = v("set", vml[:, :, :, ML_D:ML_D + 1], 1.0)
        vsb = carve(B_VSB, TB, 512)
        t_vsb = s(vsb, ps[:, 6:8, :], ACT.Copy, w=[t_vs, *t_all])
        t_om = gemm_chunk(4, free=[t_qn])
        t_cv = s(conv, conv, ACT.Silu, w=[convolve((6, 7))])
        oml = carve(B_OML, TB, 512)
        t = s(oml, ps[:, 4:6, :], ACT.Exp, w=[t_om, *t_all], scale=-1.0)

        COLS = S + P
        sel4, esel = carve(B_QT, ML_H, P, parts=ML_H), carve(B_QT + 512, ML_H, S, parts=ML_H)
        id4 = ident[0:ML_H, 0:ML_H]
        t = v("copy", sel4, id4.unsqueeze(2).to_broadcast([ML_H, ML_H, P]), w=[t_kn])
        t = v("tt", esel, id4.unsqueeze(2).to_broadcast([ML_H, ML_H, S]),
              er.unsqueeze(1).to_broadcast([ML_H, ML_H, S]), ALU.mult)
        wait(PE, t, t_ncm, t_em, t1, t_c2, *others())
        for hh in range(ML_H):
            o = ps[:, hh, :]
            for sbk, (c0, c1, t0) in enumerate(((0, S, 0), (S, COLS, P))):
                mm(o[:, c0:c1], esel[:, hh, sbk * P:sbk * P + P], on4[:, t0:S], True, False)
                mm(o[:, c0:c1], sel4[:, hh, :], cm[:, t0:S], False, False)
                ins = mm(o[:, c0:c0 + P], ident[:], c2["ml_mask"], False, True)
            t_arg = done(ins)
            o = ps[:, 4 + hh, :]
            mm(o[:, 0:S], conv[:, 4 + hh, 0:P], conv[:, hh, :])
            t_s = done(mm(o[:, S:COLS], conv[:, 4 + hh, P:S], conv[:, hh, P:S]))
        wml = carve(B_QT + 1536, ML_H, COLS)
        heads = lambda b: banks(b, 4).rearrange("p (h n) -> p h n", h=4)[:, :, 0:COLS]
        t = s(wml, heads(0), ACT.Exp, w=[t_arg])
        t_oml = s(oml, oml, ACT.Ln, bias=1.0)
        t_oml = s(oml, oml, ACT.Exp, w=[t_oml], scale=-1.0)
        t = v("stt", wml, heads(4), ML_D ** -0.5, wml, ALU.mult, ALU.mult, w=[t, t_s])
        wait(PE, t, t_one, t_vml)
        for tb in range(TB):
            ins = tr(ps[:, 7, 4 * tb:4 * tb + 4], em[:, tb * P:tb * P + P])
        for tb in range(TB):
            for hh in range(ML_H):
                o = ps[:, 2 * tb + hh // 2, (hh % 2) * 129:(hh % 2) * 129 + 129]
                mm(o, wml[:, hh, tb * P:tb * P + P], vml[:, 0, hh, :], True, tb == 0)
                if tb:
                    ins = mm(o, wml[:, hh, S:COLS], vml[:, 1, hh, :], False, True)
        t = done(ins)
        num = banks(0, 4).rearrange("p (b n) -> p b n", b=4)[:, :, 0:258].rearrange("p b (h d) -> p b h d", d=129)
        emc = carve(B_ST, 8)
        den = carve(B_ST + 8, 8)
        t1 = v("copy", emc, ps[:, 7, 0:8], w=[t])
        den4 = den.rearrange("p (b h) -> p b h", h=2)
        t2 = v("copy", den4, num[:, :, :, ML_D], w=[t])
        t2 = v("stt", den, den, -1.0, den, ALU.mult, ALU.max, w=[t2])
        t2 = v("tt", den, den, emc, ALU.max, w=[t1, t2])
        t2 = v("recip", den, den, w=[t2])
        mix = carve(B_Y, TB, D)
        yml = carve(B_QT, 8, ML_D)
        t2 = v("tt", yml.rearrange("p (b h) d -> p b h d", h=2), num[:, :, :, 0:ML_D],
               den4.unsqueeze(3).to_broadcast([P, 4, 2, ML_D]), ALU.mult, w=[t2])
        t_go = fetch("output_gains_loaded", [(zs[:], a["g_out"])], w=everything())
        t_n = head_norm(yml, yml, 8, ML_D, 8, [t2], carve(B_QT + 1024, 8, ML_D))
        yml4 = yml.rearrange("p (b h) d -> p b (h d)", b=TB)
        t = v("tt", oml, oml, zs[:, 512:1024].unsqueeze(1).to_broadcast([P, TB, 512]), ALU.mult, w=[t_go, t_oml])
        t_yml = v("tt", mix[:, :, 512:1024], yml4, oml, ALU.mult, w=[t_n, t])

        qT2, kT2 = carve(B_QT, SB_H, S, parts=SB_D), carve(B_KT, SB_H, S, parts=SB_D)
        for dst, srcn, col in ((qT2, qn, C_SBQ), (kT2, kn, C_SBK)):
            t = head_transposes(dst, [[srcn[:, tb * SB_H + hh, :] for tb in range(TB)] for hh in range(SB_H)],
                                0 if dst is qT2 else 4, SB_D, cols[0:SB_D, col:col + 1], [t_qn, t_kn, t_yml, t_cs])
        share, keep, arg = (carve(at, 2, 2, COLS) for at in (B_CV, B_CV + 1536, B_QN))
        bank2 = lambda b: ps[:, b:b + 2, 0:COLS]

        def sb_scores(g):
            n = g % 2
            for hh in range(2):
                k = 2 * g + hh
                mm(ps[:, 2 * n + hh, 0:S], kT2[:, k, 0:P], qT2[:, k, :])
                ins = mm(ps[:, 2 * n + hh, S:COLS], kT2[:, k, P:S], qT2[:, k, P:S])
            t_z, z = done(ins), bank2(2 * n)
            t = log_sigmoid_pieces(v, s, ALU, ACT, z, share[:, n], [t_z, dve.now])
            t = v("stt", keep[:, n], z, 0.0, share[:, n], ALU.max, ALU.add, w=[t, pe.now])
            t_arg = v("stt", arg[:, n], z, 0.0, share[:, n], ALU.min, ALU.subtract)
            diag = keep[:, n].rearrange("p h (m n) -> p h m n", m=3)[:, :, 0:3:2, :]
            t = v("tt", diag, diag, c2["sb_keep"].unsqueeze(1).unsqueeze(1).to_broadcast([P, 2, 2, P]), ALU.mult, w=[t])
            return t, t_arg

        wait(PE, t, *others())
        made = sb_scores(0)
        for g in range(SB_H // 2):
            n = g % 2
            t_keep, t_arg = made
            if g + 1 < SB_H // 2:
                made = sb_scores(g + 1)
            wait(PE, t_keep)
            for hh in range(2):
                o = ps[:, 4 + 2 * n + hh, :]
                mm(o[:, 0:S], c2["after"], keep[:, n, hh, 0:S], True, False)
                mm(o[:, P:S], ones[:], keep[:, n, hh, S:COLS], False, False)
                mm(o[:, 0:P], ident[:], c2["sb_mask"], False, True)
                mm(o[:, S:COLS], c2["after"], keep[:, n, hh, S:COLS], True, False)
                ins = mm(o[:, S:COLS], ident[:], c2["sb_mask"], False, True)
            t = done(ins)
            t = v("tt", arg[:, n], arg[:, n], bank2(4 + 2 * n), ALU.subtract, w=[t, t_arg])
            t = s(arg[:, n], arg[:, n], ACT.Exp, w=[t])
            wait(PE, t)
            for hh in range(2):
                k = 2 * g + hh
                for tb in range(TB):
                    o = ps[:, 2 * n + hh, COLS + tb * SB_D:COLS + tb * SB_D + SB_D]
                    mm(o, arg[:, n, hh, tb * P:tb * P + P], vsb[:, 0, k * SB_D:k * SB_D + SB_D], True, tb == 0)
                    if tb:
                        ins = mm(o, arg[:, n, hh, S:COLS], vsb[:, 1, k * SB_D:k * SB_D + SB_D], False, True)
            t = done(ins)
            src = ps[:, 2 * n:2 * n + 2, COLS:512].rearrange("p h (b d) -> p b h d", b=TB)
            for tb in range(TB):
                t = v("copy", mix[:, tb, g * P:g * P + P].rearrange("p (h d) -> p h d", d=SB_D), src[:, tb], w=[t])
            wait(PE, t)
        for tb in range(TB):
            half = mix[:, tb, 0:512].rearrange("p (h d) -> p h d", d=SB_D)
            t = head_norm(half, half, 8, SB_D, 8 + 8 * tb, [t], carve(B_CV, 8, SB_D))
            t = v("tt", mix[:, tb, 0:512], mix[:, tb, 0:512], zs[:, 0:512], ALU.mult, w=[t])
        t_mix = transpose_to_x(mix, [t, t_yml], bank=4)
        g1 = carve(B_CV, D)
        t_g1 = spread_gate(2, g1, B_CV + 1024, 6, [*everything()])
        t_h = out_proj(t_mix, gate=(g1, carve(B_QN, TB, D)), w=[t_g1])
        if stage == "mix2":
            return finish(nc, SP, h, out, ctx, t_h[1], fetch)

        R_SK, R_SC, R_QT = 0, 2048, 6144
        t_key4 = v("copy", key4[:], iota[:].unsqueeze(2).to_broadcast([P, NKEYS, 4]), w=[t_col])
        sk = carve(R_SK, PEER_H * 2, NKEYS)
        t_sk = fetch("sub_keys_loaded", [(carve(R_SK, SLAB), a["sub_keys"])], w=everything())
        norm_to_x(h, cols[:, C_G2:C_G2 + 8], t_h, shift=cols[:, C_ADA + 24:C_ADA + 32], scr=8192, bank=0)
        scores = carve(R_SC, TB, 2 * PEER_H, NKEYS)
        wait(PE, t_sk)
        query_read = []
        def queries(c):
            t = gemm_feat(2 * (c % 2), free=query_read[c - 2:c - 1])
            qT3 = carve(R_QT + 1024 * (c % 2), 4, S)
            t = s(qT3, banks(2 * (c % 2), 2).rearrange("p (k n) -> p k n", k=4), ACT.Copy, w=[t, *everything()])
            query_read.append(t)
            pump_to(3)
            return qT3, t

        ready = queries(0)
        for c in range(4):
            qT3, t = ready
            if c < 3:
                ready = queries(c + 1)
            wait(PE, t, dve.now)
            for tb in range(TB):
                for m in range(4):
                    ins = mm(ps[:, 4 + 2 * (c % 2) + tb, m * P:m * P + P], qT3[:, m, tb * P:tb * P + P],
                             sk[:, 4 * c + m, :])
            t = t_scored = done(ins)
            b = 4 + 2 * (c % 2)
            t_sc = v("copy", scores[:, :, 4 * c:4 * c + 4, :], ps[:, b:b + 2, :].rearrange("p b (m n) -> p b m n", m=4),
                     w=[t])

        wait(PE, *others())
        pump()
        hidden_products(later)
        at["use"] += 2

        NEG = -3.0e38
        U = lambda x: x.bitcast(u32)
        tv = carve(6144, TB, 2 * PEER_H, TOPK)
        ti = carve(6656, TB, 2 * PEER_H, TOPK)
        tf = carve(7168, TB, 2 * PEER_H, TOPK)
        bv = carve(7680, TB, PEER_H, TOPK)
        bp = carve(7936, TB, PEER_H, TOPK)
        pi, pj = carve(8192, TB, PEER_H, TOPK), carve(8448, TB, PEER_H, TOPK)
        sa, sbb, sg_ = carve(8704, TB, SEL), carve(8960, TB, SEL), carve(9216, TB, SEL)
        cand = carve(9728, PEER_H, TOPK * TOPK)
        oneh = carve(0, PEER_H, TOPK, TOPK)

        def top16(rows, w):
            t = w
            for values, v16, _ in rows:
                t_last = v("max", v16[:, 0:8], values, w=t)
                t = []
            for values, v16, i16 in rows:
                t_idx = v("idx", U(i16[:, 0:8]), v16[:, 0:8], values, w=[t_last])
            for values, v16, _ in rows:
                t_last = v("repl", values, v16[:, 0:8], values, NEG, w=[t_idx])
            for values, v16, _ in rows:
                t_max = v("max", v16[:, 8:16], values, w=[t_last])
            for values, v16, i16 in rows:
                t_idx = v("idx", U(i16[:, 8:16]), v16[:, 8:16], values, w=[t_max])
            return t_idx

        t_all = (t_scored, dve.now, act.now, pool.now)
        t = top16([(scores[:, tb, m, :], tv[:, tb, m, :], ti[:, tb, m, :]) for tb in range(TB)
                   for m in range(2 * PEER_H)], [t_sc, *t_all])
        t_tf = v("copy", tf, U(ti), w=[t])
        for tb in range(TB):
            tvh = tv[:, tb].rearrange("p (h m) k -> p h m k", m=2)
            shape = [P, PEER_H, TOPK, TOPK]
            t = v("tt", cand.rearrange("p h (i j) -> p h i j", i=TOPK), tvh[:, :, 0, :].unsqueeze(3).to_broadcast(shape),
                  tvh[:, :, 1, :].unsqueeze(2).to_broadcast(shape), ALU.add, w=[t, *t_all])
            t = top16([(cand[:, hh, :], bv[:, tb, hh, :], bp[:, tb, hh, :]) for hh in range(PEER_H)], [t])
        t1 = v("ts", U(pi), U(bp), 4, None, ALU.logical_shift_right, w=[t])
        t2 = v("ts", U(pj), U(bp), 15, None, ALU.bitwise_and)
        t1 = v("copy", bp, U(pi), w=[t1, t2])
        t2 = v("copy", pi, U(pj), w=[t2, t1])
        for src, m, dst in ((bp, 0, sa), (pi, 1, sbb)):
            for tb in range(TB):
                tfh = tf[:, tb].rearrange("p (h m) k -> p h m k", m=2)
                t = v("tt", oneh, iota[:, 0:TOPK].unsqueeze(1).unsqueeze(1).to_broadcast(shape),
                      src[:, tb].unsqueeze(3).to_broadcast(shape), ALU.is_equal, w=[t, t1, t2, t_tf])
                t = v("tt", oneh, oneh, tfh[:, :, m, :].unsqueeze(2).to_broadcast(shape), ALU.mult, w=[t])
                t = v("red", dst[:, tb, :].rearrange("p (h k) -> p h k", h=PEER_H), oneh, AX.X, ALU.add, w=[t])
        bvf = bv.rearrange("p b h k -> p (b h) k")
        sgf = sg_.rearrange("p b (h k) -> p (b h) k", h=PEER_H)
        t1 = v("tt", sgf, bvf, bvf[:, :, 0:1].to_broadcast([P, 16, TOPK]), ALU.subtract)
        t1 = s(sgf, sgf, ACT.Exp, w=[t1])
        t1 = v("red", stat[:, 8:24], sgf, AX.X, ALU.add, w=[t1])
        t1 = v("recip", stat[:, 8:24], stat[:, 8:24], w=[t1])
        t1 = v("tt", sgf, sgf, stat[:, 8:24].unsqueeze(2).to_broadcast([P, 16, TOPK]), ALU.mult, w=[t1])
        wait(PE, t, t1, *others())
        for n, src in enumerate((sa, sbb, sg_)):
            for tb in range(TB):
                ins = tr(ps[:, n, tb * P:tb * P + P], src[:, tb, :])
        t = done(ins)
        for n, dst in enumerate((sel_a, sel_b)):
            s(dst[:], ps[:, n, 0:S], ACT.Copy, w=[t])
        rest = ps[:, 2, 0:S]
        for n in range(3):
            t_sel = s(gate_parts[:, n, :], rest, ACT.Copy, w=[t])
            if n < 2:
                left = zs[:, n * S:n * S + S]
                t = v("tt", left, rest, gate_parts[:, n, :], ALU.subtract, w=[t_sel])
                rest = left

        G = arena[:, :].rearrange("p (a t) -> p a t", a=HALF_A)
        hit_b = zs[:].bitcast(bf16).rearrange("p (n g b t) -> p n g b t", n=2, g=2, t=4)
        first = wf[:].bitcast(bf16)
        hit_a = first[:, 0:512].rearrange("p (g a t) -> p g a t", g=2, t=4)
        gated = first[:, 512:2048].rearrange("p (g q a t) -> p g q a t", g=2, q=3, t=4)
        hits_used = [[Count(nc, ctx, f"hits_used{n}{g}") for g in range(2)] for n in range(2)]
        g_read = [Count(nc, ctx, f"gate_bank_read{n}") for n in range(2)]
        for c in (*hits_used[0], *hits_used[1], *g_read):
            wait(POOL, pool.now)
            c.add(POOL.memset(minus_half[:, 0:1], -0.5))
            pool.add(POOL.memset(minus_half[:, 1:2], -0.5))

        def build_gates(half):
            keys_a = key4[:, half * HALF_A:half * HALF_A + HALF_A, :]
            steps = {dve: 10, **{c: 1 for used_n in hits_used for c in used_n}, **{c: 1 for c in g_read}}
            with loop(nc, S // 16, steps) as i:
                t_gated = dve.now
                for n in range(2):
                    t0 = i * 16 + n * 8
                    of_tokens = lambda x: x[:, bass.ds(t0, 8)].rearrange("p (g t) -> p g t", g=2).unsqueeze(2)
                    shape = [P, NKEYS, 4]
                    find_b = lambda g, w=(): v("tt", hit_b[:, n, g], key4[:],
                                               sel_b[:, bass.ds(t0 + 4 * g, 4)].unsqueeze(1).to_broadcast(shape),
                                               ALU.is_equal, w=w)
                    find_b(0, w=[hits_used[n][1].now])
                    t_a = v("tt", hit_a, keys_a.unsqueeze(1).to_broadcast([P, 2, HALF_A, 4]),
                            of_tokens(sel_a).to_broadcast([P, 2, HALF_A, 4]), ALU.is_equal, w=[t_gated])
                    find_b(1)
                    shape = [P, 3, HALF_A, 4]
                    for g in range(2):
                        t = v("tt", gated[:, g], hit_a[:, g].unsqueeze(1).to_broadcast(shape),
                              gate_parts[:, :, bass.ds(t0 + 4 * g, 4)].unsqueeze(2).to_broadcast(shape), ALU.mult,
                              w=[t_a, hits_used[1 - n][g].now])
                        t_gated = t
                        wait(PE, t, g_read[n].now)
                        for j in range(4):
                            col = (4 * g + j) * HALF_A
                            for q in range(3):
                                ins = mm(ps[:, 6 + n, col:col + HALF_A], hit_b[:, n, g, :, j], gated[:, g, q, :, j],
                                         q == 0, q == 2)
                        hits_used[n][g].add(ins)
                    wait(ACTE, hits_used[n][1].now)
                    g_read[n].add(ACTE.activation(G[:, :, bass.ds(t0, 8)],
                                                  ps[:, 6 + n, :].rearrange("p (t a) -> p a t", t=8), ACT.Copy))

        def weigh_start(t_w):
            wait(PE, z_read.now, *t_w)
            for m in range(EX_A):
                for tb in range(TB):
                    ins = tr(ps[:, 6 + m // 2, (m % 2) * S + tb * P:(m % 2) * S + tb * P + P],
                             zs[:, tb * 512 + m * P:tb * 512 + m * P + P])
            return s(wf[:], banks(6, 2), ACT.Gelu, w=[done(ins), *t_w])

        def weigh_end(c_local, t):
            w4 = wf[:].rearrange("p (a t) -> p a t", a=EX_A)
            t = v("tt", w4, w4, G[:, bass.ds(c_local * EX_A, EX_A), :], ALU.mult, w=[t])
            split(wh[:], wl[:], w4, [t])

        def ex_step(c_local, refill):
            t_w = act.now, dve.now
            hidden_products(refill)
            wait(ACTE, used[1].now, pe.now)
            z_read.add(ACTE.activation(zs[:], banks(4, 2), ACT.Copy))
            refill(1)
            add_products(2, 0, t_w)
            refill(2)
            add_products(3, 2, t_w)
            t = weigh_start(t_w)
            refill(3)
            weigh_end(c_local, t)

        def ex_open():
            t_w = (*everything(), *(c.now for c in g_read))
            wait(ACTE, *t_w)
            z_read.add(ACTE.activation(zs[:], banks(4, 2), ACT.Copy))
            pump(2)
            t = weigh_start(t_w)
            weigh_end(0, t)
            pump()

        wait(POOL, *everything())
        t_y0 = pool.add(POOL.memset(wl[:, 0:2, :].bitcast(f32), 0.0))
        wait(DVE, *everything(), t_sel)
        wait(ACTE, *everything())
        wait(PE, *others())
        build_gates(0)
        clear_sums(t_y0)
        ex_open()
        steps = {act: 2, dve: 2, pe: 1, z_read: 1, **{c: 1 for c in used}, **{c: 16 for c in load},
                 **{c: 1 for c in split_hi}, **{c: 1 for c in split_lo}}

        def ex_loop(first, n, offset):
            assert at["split"] == at["use"] + 4 and at["load"] == at["use"] + 8
            with loop(nc, n, steps) as j:
                def refill(slot, j=j):
                    emit_split(slot)
                    if slot < 2:
                        emit_load("ex_u", 2 * j + (2 * (first + 2) + slot), slot)
                    else:
                        emit_load("ex_v", 2 * j + (2 * (first + 1) + slot - 2), slot)
                ex_step(j + (first - offset), refill)
            at_loop(n, 4)

        ex_loop(1, EX_N // 2 - 1, 0)
        t_w = act.now, dve.now
        add_products(2, 0, t_w)
        add_products(3, 2, t_w)
        t_rows = used[3].now
        hidden_products(later)
        at["use"] += 4
        wait(DVE, act.now, t_rows)
        wait(ACTE, dve.now, t_rows)
        wait(PE, *others())
        build_gates(1)
        ex_open()
        ex_loop(EX_N // 2 + 1, EX_N // 2 - 3, EX_N // 2)
        for c in (EX_N - 2, EX_N - 1):
            ex_step(c - EX_N // 2, pumped)
        t_w = act.now, dve.now
        add_products(2, 0, t_w)
        add_products(3, 2, t_w, stop=True)
        g2 = carve(0, D)
        t_g2 = spread_gate(5, g2, 1024, 4, everything())
        t_h = add_residual([used[3].now, t_g2], gate=(g2, carve(2048, TB, D)))
        return finish(nc, SP, h, out, ctx, t_h[1], fetch)


def log_sigmoid_pieces(v, s, ALU, ACT, x, e, w):
    t = s(e, x, ACT.Abs, w=w)
    t = s(e, e, ACT.Exp, w=[t], scale=-1.0)
    return s(e, e, ACT.Ln, w=[t], bias=1.0)


def softmax_open(v, s, ALU, ACT, AX, sc, dst, stat, at0, w):
    n = dst.shape[1]
    t = v("red", stat[:, at0:at0 + n], sc, AX.X, ALU.max, w=w, negate=True)
    for hh in range(n):
        t = s(dst[:, hh], sc[:, hh], ACT.Exp, w=[t, *w] if hh == 0 else [], bias=stat[:, at0 + hh:at0 + hh + 1],
              accum_out=stat[:, at0 + n + hh:at0 + n + hh + 1])
    return t


def softmax_close(v, ALU, dst, stat, at0, t):
    n = dst.shape[1]
    sums = stat[:, at0 + n:at0 + 2 * n]
    t = v("recip", sums, sums, w=[t])
    return v("tt", dst, dst, sums.unsqueeze(2).to_broadcast(list(dst.shape)), ALU.mult, w=[t])


def finish(nc, SP, h, out, ctx, w, fetch):
    t = fetch("stored", [(out, h[:])], w=w)
    wait(SP, t)


def layout(i):
    def w(x):
        return np.asarray(x)[0] if np.asarray(x).ndim > 2 else np.asarray(x)

    def slabs(m):
        k, n = m.shape
        m = m.reshape(k // 512, 4, P, n // 512, 512).transpose(3, 0, 2, 1, 4)
        return np.ascontiguousarray(m).reshape(-1, P, SLAB)

    def fcols(x):
        return np.asarray(x).reshape(-1, P).T

    def tok(x):
        return np.ascontiguousarray(np.asarray(x).reshape(TB, P, D).transpose(1, 0, 2))

    def rep(x):
        return np.ascontiguousarray(np.broadcast_to(np.asarray(x).reshape(1, -1), (P, np.asarray(x).size)))

    def small(m):
        return np.ascontiguousarray(m.reshape(KT, P, m.shape[1]).transpose(1, 0, 2))

    f4 = np.float32
    cols = np.zeros((P, 192), f4)
    cols[:, 0:8], cols[:, 8:16] = fcols(i["g_mix"]), fcols(i["g_mem_kv"])
    cols[:, 16:24], cols[:, 24:32] = fcols(i["g_mem_q"]), fcols(i["g_ffn"])
    cols[0:64, 32], cols[0:64, 33] = i["g_q_fox"][0], i["g_k_fox"][0]
    cols[64:66, 32:34] = 1
    cols[:, 34], cols[:, 35] = i["g_q_mem"][0], i["g_k_mem"][0]
    cols[:, 36:40] = fcols(i["pool_scale"])
    cols[:, 41:49] = fcols(i["c_2"])
    cols[:, 57:65], cols[:, 65:73] = fcols(i["g_norm1_2"]), fcols(i["g_norm2_2"])
    cols[:, 73:121] = fcols(i["b_ada_2"])
    cols[0:64, 121], cols[0:64, 122] = i["g_q_sb_2"][0], i["g_k_sb_2"][0]
    cols[:, 124:156] = np.asarray(i["conv_w_2"])[0].reshape(CONV, 8, P).transpose(2, 1, 0).reshape(P, 32)
    cols[0:ML_H, 172], cols[0:ML_H, 173] = i["b_igate_2"][0], i["b_fgate_2"][0]

    w_in, w_in2 = w(i["w_in"]), w(i["w_in_2"])
    gu = w(i["w_gate_up"]).reshape(D, 2, FF_N, FF_C).transpose(0, 2, 1, 3).reshape(D, FF_N * 512)
    ada = w(i["w_ada_2"]).reshape(KT, P, 3, SLAB).transpose(0, 2, 1, 3)
    q, k, v_, qk, vm, om = (w_in2[:, x:y] for x, y in
                            ((0, 512), (512, 1024), (1024, 1536), (1536, 2560), (2560, 3072), (3072, 3584)))
    c = constants()
    return {
        "x": tok(i["x"]), "mem": tok(i["mem"]), "cols": cols,
        "ident": c["ident"], "ones": c["ones"], "iota": c["iota"], "fox_mask": c["fox_mask"], "upto": c["upto"],
        "ml_mask": c["ml_mask"], "sb_keep": c["sb_keep"], "sb_mask": c["sb_mask"], "after": c["after"],
        "bands": np.ascontiguousarray(c["bands"]),
        "b_forget": rep(i["b_forget"]), "w_f": small(w_in[:, 2048:2056]), "w_if": small(w_in2[:, 3584:3592]),
        "w_pool": np.ascontiguousarray(w(i["w_pool"]).transpose(1, 0, 2)).reshape(P, 512),
        "g_out": rep(np.concatenate([np.asarray(i["g_out_sb_2"]).ravel(), np.asarray(i["g_out_ml_2"]).ravel()])),
        "sub_keys": np.ascontiguousarray(w(i["sub_keys_2"]).transpose(3, 0, 1, 2)).reshape(P, SLAB),
        "w_mem_kv": slabs(w(i["w_mem_kv"])), "w_in": slabs(w_in[:, 0:2048]), "w_out": slabs(w(i["w_out"])),
        "w_mem_q": slabs(w(i["w_mem_q"])), "w_mem_out": slabs(w(i["w_mem_out"])), "w_gu": slabs(gu),
        "w_down": np.ascontiguousarray(w(i["w_down"]).reshape(FF_N, 2, P, D).transpose(0, 2, 1, 3)).reshape(-1, P, SLAB),
        "w_ada": np.ascontiguousarray(ada).reshape(-1, P, SLAB),
        "w_in_2": slabs(np.concatenate([qk, q, k, vm, v_, om], axis=1)),
        "w_out_2": slabs(w(i["w_out_2"])), "w_q_peer": slabs(w(i["w_q_peer_2"])),
        "ex_u": slabs(w(i["expert_u_2"]).T),
        "ex_v": np.ascontiguousarray(w(i["expert_v_2"]).reshape(-1, 2, P, D).transpose(0, 2, 1, 3)).reshape(-1, P, SLAB),
    }


def kernel(**inputs):
    import concourse.bacc as bacc
    from concourse.bass_utils import run_bass_kernel_spmd

    arrays = layout(inputs)
    nc = bacc.Bacc("TRN2", target_bir_lowering=False, num_devices=1)
    aps = {n: nc.dram_tensor("in_" + n, x.shape, mybir.dt.from_np(x.dtype), kind="ExternalInput").ap()
           for n, x in arrays.items()}
    out = nc.dram_tensor("out", (P, TB, D), mybir.dt.float32, kind="ExternalOutput").ap()
    program(nc, aps, out)
    r = run_bass_kernel_spmd(nc, [{"in_" + n: x for n, x in arrays.items()}], core_ids=[0])
    return np.ascontiguousarray(r.results[0]["out"].transpose(1, 0, 2)).reshape(1, S, D)
```

```python
import numpy as np
from contextlib import ExitStack, contextmanager

import concourse.bass as bass
from concourse import mybir

P = 128
S = 256
TB = S // P
D = 1024
KT = D // P
SLAB = 2048
FOX_H, FOX_D = 8, 64
FOX_A = FOX_D + 2
POOL_WINDOWS = (2, 4, 8, 16)
MEM_H, MEM_D = 4, 128
D_FF = 2816
FF_C = 256
FF_N = D_FF // FF_C
SB_H, SB_D = 8, 64
ML_H, ML_D = 4, 128
CONV = 4
PEER_H, NKEYS, TOPK = 8, 128, 16
SEL = PEER_H * TOPK
EX_A = 4
EX_N = NKEYS // EX_A
HALF_A = NKEYS // 2
EPS = 1e-6
BIG = 1e30


def constants():
    i = np.arange(P)
    row, col = i[:, None], i[None, :]
    bands = np.zeros((TB, P, len(POOL_WINDOWS), S), np.float32)
    t, s = np.arange(S)[None, :], np.arange(S)[:, None]
    for g, w in enumerate(POOL_WINDOWS):
        inside = (s <= t) & (s > t - w)
        bands[:, :, g] = (inside / np.minimum(t + 1, w) - (s == t)).reshape(TB, P, S)
    parts = {
        "ident": (row == col), "ones": np.ones((P, P)), "iota": np.broadcast_to(col, (P, P)),
        "fox_mask": np.where(col <= row, 0, -BIG),
        "ml_mask": np.where(row <= col, 0, -BIG),
        "sb_keep": (row < col),
        "sb_mask": np.where(row < col, 0, BIG),
        "upto": (row <= col),
        "after": (row > col),
        "bands": bands.transpose(1, 0, 2, 3).reshape(P, -1),
    }
    return {k: np.ascontiguousarray(v, dtype=np.float32) for k, v in parts.items()}


class Count:

    def __init__(self, nc, ctx, name):
        self.sem = ctx.enter_context(nc.semaphore(name))
        self.base, self.k = 0, 0

    @property
    def now(self):
        return self, self.base + self.k

    def add(self, ins, by=1):
        ins.then_inc(self.sem, by)
        self.k += by
        return self.now


def wait(eng, *tokens):
    for t in tokens:
        if t is not None and not (isinstance(t[1], int) and t[1] <= 0):
            eng.wait_ge(t[0].sem, t[1])


@contextmanager
def loop(nc, n, steps):
    before = {c: c.base + c.k for c in steps}
    with nc.Fori(0, n) as i:
        for c, d in steps.items():
            c.base, c.k = before[c] + i * d, 0
        yield i
        for c, d in steps.items():
            assert c.k == d, (c.sem, c.k, d)
    for c, d in steps.items():
        c.base, c.k = before[c] + n * d, 0


def program(nc, a, out):
    f32, f32r, bf16, u32 = mybir.dt.float32, mybir.dt.float32r, mybir.dt.bfloat16, mybir.dt.uint32
    ALU, ACT, AX = mybir.AluOpType, mybir.ActivationFunctionType, mybir.AxisListType
    PE, DVE, ACTE, POOL, SP = nc.tensor, nc.vector, nc.scalar, nc.gpsimd, nc.sync
    ctx = ExitStack()
    with ctx:
        def sb(name, shape, dt=f32):
            return ctx.enter_context(nc.sbuf_tensor(name, shape, dt))

        NSLOT = 4
        raw = sb("slab_raw", [P, NSLOT, SLAB])
        slab_hi = sb("slab_hi", [P, NSLOT, SLAB], f32r)
        slab_lo = sb("slab_lo", [P, NSLOT, SLAB], f32r)
        h = sb("residual", [P, TB, D])
        xh = sb("x_hi", [P, KT, S], f32r)
        xl = sb("x_lo", [P, KT, S], f32r)
        zs = sb("hidden", [P, 1024])
        wf = sb("weighted", [P, 1024])
        wh = sb("weighted_hi", [P, EX_A, S], f32r)
        wl = sb("weighted_lo", [P, EX_A, S], f32r)
        arena = sb("arena", [P, HALF_A * S])
        ident = sb("ident", [P, P])
        ones = sb("ones", [P, P])
        iota = sb("iota", [P, P])
        sel_a = sb("selected_first_keys", [P, S], bf16)
        sel_b = sb("selected_second_keys", [P, S], bf16)
        gate_parts = sb("selected_gates_in_parts", [P, 3, S], bf16)
        key4 = sb("key_numbers_by_4", [P, NKEYS, 4], bf16)
        cols = sb("columns", [P, 256])
        stat = sb("statistics", [P, 64])
        wsm_h = sb("small_weight_hi", [P, KT, 8], f32r)
        wsm_l = sb("small_weight_lo", [P, KT, 8], f32r)
        ps = ctx.enter_context(nc.psum_tensor("psum", [P, 8, 512], f32))

        def carve(at, *shape, parts=P):
            n = int(np.prod(shape))
            assert at + n <= HALF_A * S
            v = arena[0:parts, at:at + n]
            names = "abcd"[:len(shape)]
            if len(shape) > 1:
                v = v.rearrange(f"p ({' '.join(names)}) -> p {' '.join(names)}",
                                **{names[i]: shape[i] for i in range(len(shape))})
            return v

        def banks(b, n):
            return ps[:, b:b + n, :].rearrange("p b n -> p (b n)")

        pe, dve, act, pool = (Count(nc, ctx, n) for n in ("pe_done", "dve_done", "act_done", "pool_done"))
        z_read = Count(nc, ctx, "hidden_banks_read")
        load = [Count(nc, ctx, f"raw_loaded{s}") for s in range(NSLOT)]
        split_hi = [Count(nc, ctx, f"slab_hi_ready{s}") for s in range(NSLOT)]
        split_lo = [Count(nc, ctx, f"slab_lo_ready{s}") for s in range(NSLOT)]
        used = [Count(nc, ctx, f"slab_used{s}") for s in range(NSLOT)]

        def v(fn, *args, w=(), **kw):
            wait(DVE, *w)
            return dve.add(vector_ops[fn](*args, **kw))

        vector_ops = {"tt": DVE.tensor_tensor, "ts": DVE.tensor_scalar, "stt": DVE.scalar_tensor_tensor,
                        "copy": DVE.tensor_copy, "red": DVE.tensor_reduce, "recip": DVE.reciprocal,
                        "scan": DVE.tensor_tensor_scan, "max": DVE.max, "idx": DVE.max_index,
                        "repl": DVE.match_replace, "set": DVE.memset}

        def s(out, in_, func, w=(), **kw):
            wait(ACTE, *w)
            return act.add(ACTE.activation(out, in_, func, **kw))

        def mm(out, lhsT, rhs, start=True, stop=True):
            return PE.matmul(out, lhsT, rhs, start=start, stop=stop)

        def tr(out, in_):
            return PE.transpose(out, in_, ident[0:in_.shape[0], 0:in_.shape[0]])

        def done(ins):
            return pe.add(ins)

        def mm3(out, ah, al, bh, bl, start, stop):
            mm(out, ah, bh, start, False)
            mm(out, ah, bl, False, False)
            return mm(out, al, bh, False, stop)

        def everything():
            return pe.now, *(c.now for c in used), z_read.now, dve.now, act.now, pool.now

        def others():
            return dve.now, act.now, pool.now, z_read.now

        def fetch(name, pairs, w=()):
            c = Count(nc, ctx, name)
            wait(SP, *w)
            for dst, src in pairs:
                c.add(SP.dma_start(dst, src), 16)
            return c.now

        plan = []
        at = {"load": 0, "split": 0, "use": 0}

        def queue(entries):
            plan.extend(entries)

        def cyc(name, indices):
            first = len(plan)
            indices = range(indices) if isinstance(indices, int) else indices
            queue([(name, j, (first + n) % NSLOT) for n, j in enumerate(indices)])

        def emit_load(name, j, slot):
            wait(SP, split_hi[slot].now, split_lo[slot].now)
            src = a[name].rearrange("n p m -> (n p) m")[bass.ds(j * P, P), :]
            load[slot].add(SP.dma_start(raw[:, slot, :], src), 16)

        def emit_split(slot):
            wait(ACTE, load[slot].now, used[slot].now)
            split_hi[slot].add(ACTE.activation(slab_hi[:, slot, :], raw[:, slot, :], ACT.Copy))
            wait(DVE, split_hi[slot].now)
            split_lo[slot].add(DVE.tensor_tensor(slab_lo[:, slot, :], raw[:, slot, :],
                                                 slab_hi[:, slot, :].bitcast(f32), ALU.subtract))

        def last_of(slot, before):
            return max((n for n in range(before) if plan[n][2] == slot), default=-1)

        def pump_loads():
            while at["load"] < len(plan) and last_of(plan[at["load"]][2], at["load"]) < at["split"]:
                emit_load(*plan[at["load"]])
                at["load"] += 1

        def pump(n=99):
            pump_loads()
            while n and at["split"] < at["load"] and last_of(plan[at["split"]][2], at["split"]) < at["use"]:
                emit_split(plan[at["split"]][2])
                at["split"] += 1
                n -= 1
                pump_loads()

        def pump_to(n):
            pump(max(0, n - (at["split"] - at["use"])))

        def take():
            while at["split"] <= at["use"]:
                pump(1)
            slot = plan[at["use"]][2]
            at["use"] += 1
            wait(PE, split_hi[slot].now, split_lo[slot].now)
            return slot

        def parts(slot, k, n):
            shape = dict(k=k, n=n)
            return tuple(t[:, slot, :].rearrange("p (k n) -> p k n", **shape) for t in (slab_hi, slab_lo))

        x_written = {0: (), 1: ()}

        def wait_x(half):
            wait(PE, *x_written[half])
            x_written[half] = ()

        def gemm_tok(bank, half, slot, k0, nk=4, last=True, first=True):
            bh, bl = parts(slot, 4, 512)
            for tb in range(TB):
                tok = slice(tb * P, tb * P + P)
                for k in range(nk):
                    ins = mm3(ps[:, bank + tb, :], xh[:, k0 + k, tok], xl[:, k0 + k, tok], bh[:, k], bl[:, k],
                              first and k == 0, last and k == nk - 1)
            return ins

        def gemm_chunk(bank, free=()):
            wait(PE, *free)
            for half in range(2):
                slot = take()
                wait_x(half)
                ins = gemm_tok(bank, half, slot, 4 * half, first=half == 0, last=half == 1)
                if half == 0:
                    used[slot].add(ins)
                    pump_to(3)
            return used[slot].add(ins)

        def small_products(w):
            wait(PE, *w)
            for tb in range(TB):
                for k in range(KT):
                    ins = mm3(ps[:, 7, tb * 8:tb * 8 + 8], xh[:, k, tb * P:tb * P + P], xl[:, k, tb * P:tb * P + P],
                              wsm_h[:, k], wsm_l[:, k], k == 0, k == KT - 1)
            return done(ins)

        cyc("w_mem_kv", 4)
        cyc("w_in", 8)
        OUT_ORDER = (1, 0), (1, 1), (0, 0), (0, 1)
        cyc("w_out", [2 * c + half for half, c in OUT_ORDER])
        cyc("w_mem_q", 2)
        cyc("w_mem_out", 2)
        ff = [("w_gu", 0, 0), ("w_gu", 1, 1)]
        for c in range(1, FF_N):
            ff += [("w_gu", 2 * c, 0), ("w_gu", 2 * c + 1, 1), ("w_down", c - 1, 2)]
        queue(ff + [("w_down", FF_N - 1, 2)])
        cyc("w_in_2", 14)
        cyc("w_out_2", [2 * c + half for half, c in OUT_ORDER])
        cyc("w_q_peer", 8)
        ex = [("ex_u", 0, 0), ("ex_u", 1, 1)]
        for c in range(1, EX_N):
            ex += [("ex_u", 2 * c, 0), ("ex_u", 2 * c + 1, 1), ("ex_v", 2 * c - 2, 2), ("ex_v", 2 * c - 1, 3)]
        queue(ex + [("ex_v", 2 * EX_N - 2, 2), ("ex_v", 2 * EX_N - 1, 3)])

        gm = arena[:, 14336:16384].rearrange("p (b n) -> p b n", b=TB)
        t_mem = {tb: [fetch(f"mem_loaded{tb}", [(gm[:, tb], a["mem"][:, tb])])] for tb in range(TB)}
        CM, CKV, CQ, CF = 0, 8, 16, 24
        C_FOXQ, C_FOXK, C_MEMQ, C_MEMK, C_PS = 32, 33, 34, 35, 36
        C_CT, C_SC, C_N1, C_N2, C_ADA, C_SBQ, C_SBK, C_CONV = 41, 49, 57, 65, 73, 121, 122, 124
        C_G1, C_G2, C_BG = 156, 164, 172
        t_col = fetch("columns_loaded", [(cols[:, 0:192], a["cols"]), (ident[:], a["ident"]), (ones[:], a["ones"]),
                                         (iota[:], a["iota"])])
        pump_loads()
        t_x = fetch("x_loaded", [(h[:], a["x"])])
        nc.scalar.preload_act_table_set("natural_log_exp_and_others")

        def rstd(n, width, at0, w):
            t = v("ts", stat[:, at0:at0 + n], stat[:, at0:at0 + n], 1.0 / width, EPS, ALU.mult, ALU.add, w=w)
            wait(POOL, t)
            return pool.add(POOL.tensor_tensor(stat[:, at0:at0 + n], stat[:, at0:at0 + n],
                                               minus_half[:, 0:n], ALU.pow))

        minus_half = sb("minus_half", [P, 16])
        t_mh = pool.add(POOL.memset(minus_half[:], -0.5))

        def split(dst_h, dst_l, full, w):
            wait(DVE, *w)
            t = s(dst_h, full, ACT.Copy, w=w)
            return v("tt", dst_l, full, dst_h.bitcast(f32), ALU.subtract, w=[t])

        def norm_scale(src, t_src, scr, at0, ready):
            free = everything()
            xs = carve(scr, TB, D)
            for tb in range(TB):
                w = [*t_src[tb], *(f for f in free if f[0] is not dve)] if isinstance(t_src, dict) else [*t_src, *free]
                t = s(xs[:, tb, :], src[:, tb, :], ACT.Square, w=w, accum_out=stat[:, at0 + tb:at0 + tb + 1])
            t = rstd(TB, D, at0, [t, t_mh])
            if ready:
                pump_to(1)
            for tb in range(TB):
                t = v("ts", xs[:, tb, :], src[:, tb, :], stat[:, at0 + tb:at0 + tb + 1], None, ALU.mult, w=[*free, t, act.now])
            return t

        def norm_to_x(src, gain, t_src, t_gain=None, shift=None, scr=0, bank=0, ready=True, scaled=None):
            def low(high):
                two, t = high
                v("tt", xl[:, two], full[:, two], xh[:, two].bitcast(f32), ALU.subtract, w=[t, *last_use()])

            xs = carve(scr, TB, D)
            full = carve(scr + TB * D, KT, S)
            t = scaled or norm_scale(src, t_src, scr, 0, ready)
            free = everything()
            high = None
            for b in range(4):
                wait(PE, *free, t, *last_use())
                for k in (2 * b, 2 * b + 1):
                    for tb in range(TB):
                        ins = tr(ps[:, bank + b, (k % 2) * S + tb * P:(k % 2) * S + tb * P + P],
                                 xs[:, tb, k * P:k * P + P])
                tp = done(ins)
                two = slice(2 * b, 2 * b + 2)
                src_p = ps[:, bank + b, :].rearrange("p (k n) -> p k n", k=2)
                tf = v("tt", full[:, two], src_p, gain[:, two].unsqueeze(2).to_broadcast([P, 2, S]), ALU.mult, w=[tp, t_gain])
                if shift is not None:
                    tf = v("tt", full[:, two], full[:, two], shift[:, two].unsqueeze(2).to_broadcast([P, 2, S]),
                           ALU.add, w=[tf])
                if b:
                    low(high)
                high = two, s(xh[:, two], full[:, two], ACT.Copy, w=[tf, *last_use()])
                if b == 2:
                    x_written[0] = high_before, dve.now
                    pump_to(2 if ready else 1)
                high_before = high[1]
            low(high)
            x_written[1] = high[1], dve.now
            return x_written[1]

        def last_use():
            return [c.now for c in used]

        def head_norm(src, dst, n_heads, d, at0, w, scratch):
            t = s(scratch, src, ACT.Square, w=w)
            t = v("red", stat[:, at0:at0 + n_heads], scratch, AX.X, ALU.add, w=[t])
            t = rstd(n_heads, d, at0, [t])
            return v("tt", dst, src, stat[:, at0:at0 + n_heads].unsqueeze(2).to_broadcast([P, n_heads, d]),
                     ALU.mult, w=[t, *w])

        A_MKT, A_MV, A_V, A_PIN, A_QT, A_KT, A_P, A_PT, A_MIX = 0, 1024, 2048, 3072, 4096, 6144, 8192, 12288, 15360
        wait(PE, t_col)
        norm_to_x(gm, cols[:, CKV:CKV + 8], t_mem, t_col, scr=4096, bank=0, ready=False)
        t_k = gemm_chunk(4)
        t_xs = norm_scale(h, [t_x], 8192, 2, False)
        t_v = gemm_chunk(6)
        mkn = carve(A_QT, 8, MEM_D)
        mksq = carve(A_KT, 8, MEM_D)
        t = head_norm(banks(4, 2).rearrange("p (h d) -> p h d", d=MEM_D), mkn, 8, MEM_D, 8, [t_k], mksq)
        mv = carve(A_MV, TB, 512)
        t_mv = s(mv, ps[:, 6:8, :], ACT.Copy, w=[t_v])
        mkT = carve(A_MKT, MEM_H, S)

        def head_transposes(dst, srcs, bank, n_rows, gain, w):
            for b in range(len(srcs) // 2):
                wait(PE, *w)
                for j in range(2):
                    for tb in range(TB):
                        o = j * S + tb * P
                        ins = tr(ps[0:n_rows, bank + b, o:o + P], srcs[2 * b + j][tb])
                tp = done(ins)
                t = s(dst[:, 2 * b:2 * b + 2, :], ps[0:n_rows, bank + b, :].rearrange("p (h n) -> p h n", h=2),
                      ACT.Copy, w=[tp, *w], scale=gain)
            return t

        t_cs = v("ts", cols[:, C_MEMQ:C_MEMQ + 1], cols[:, C_MEMQ:C_MEMQ + 1], MEM_D ** -0.5, None, ALU.mult, w=[t_col])
        t_cs = v("ts", cols[0:FOX_D, C_FOXQ:C_FOXQ + 1], cols[0:FOX_D, C_FOXQ:C_FOXQ + 1], FOX_D ** -0.5, None,
                 ALU.mult)
        t_cs = v("ts", cols[0:SB_D, C_SBQ:C_SBQ + 1], cols[0:SB_D, C_SBQ:C_SBQ + 1], SB_D ** -0.5, None, ALU.mult)
        mkn_h = [[mkn[:, tb * MEM_H + hh, :] for tb in range(TB)] for hh in range(MEM_H)]
        t_mk = head_transposes(mkT, mkn_h, 0, P, cols[:, C_MEMK:C_MEMK + 1], [t, t_cs])

        wsm = carve(14336, KT, 8)
        t_ws = fetch("forget_weight_loaded", [(wsm, a["w_f"])], w=everything())
        t_bf = fetch("block1_constants_loaded", [(carve(14500, P), a["fox_mask"]), (carve(14628, P), a["upto"]),
                                                 (carve(14800, FOX_H), a["b_forget"])], w=everything())
        fox_mask, upto, bfor = carve(14500, P), carve(14628, P), carve(14800, FOX_H)
        norm_to_x(h, cols[:, CM:CM + 8], [t_x], t_col, scr=8192, bank=0, scaled=t_xs)
        t_wsm = split(wsm_h[:], wsm_l[:], wsm, [t_ws])
        t_q = gemm_chunk(0)
        t_f = small_products([t_wsm, t_mv])
        fl, fe = carve(14816, TB, FOX_H), carve(14832, TB, FOX_H)
        cum = carve(14848, TB, FOX_H)
        t = v("tt", fl, ps[:, 7, 0:16].rearrange("p (b h) -> p b h", b=TB),
              bfor.unsqueeze(1).to_broadcast([P, TB, FOX_H]), ALU.add, w=[t_f, t_bf])
        t = log_sigmoid_pieces(v, s, ALU, ACT, fl, fe, [t])
        t = v("stt", fl, fl, 0.0, fe, ALU.min, ALU.subtract, w=[t])
        wait(PE, t)
        mm(ps[:, 7, 16:24], upto, fl[:, 0, :])
        mm(ps[:, 7, 24:32], ones[:], fl[:, 0, :], True, False)
        t_c = done(mm(ps[:, 7, 24:32], upto, fl[:, 1, :], False, True))
        t_cum = v("copy", cum, ps[:, 7, 16:32].rearrange("p (b h) -> p b h", b=TB), w=[t_c])
        t_k = gemm_chunk(2)
        qa, ka = carve(A_PT, TB, FOX_H, FOX_A), carve(A_PT + 1056, TB, FOX_H, FOX_A)
        qsq = carve(A_P + 2048, 16, FOX_D)
        qa_v = qa.rearrange("p b h d -> p (b h) d")
        ka_v = ka.rearrange("p b h d -> p (b h) d")
        t = head_norm(banks(0, 2).rearrange("p (h d) -> p h d", d=FOX_D), qa_v[:, :, 0:FOX_D], 16, FOX_D, 8, [t_q], qsq)
        cum_v = cum.rearrange("p b h -> p (b h)").unsqueeze(2)
        v("set", qa_v[:, :, FOX_D:FOX_D + 1], 1.0)
        v("copy", qa_v[:, :, FOX_D + 1:FOX_A], cum_v, w=[t_cum])
        v("set", ka_v[:, :, FOX_D + 1:FOX_A], 1.0)
        v("ts", ka_v[:, :, FOX_D:FOX_D + 1], cum_v, -1.0, None, ALU.mult)
        t_v = gemm_chunk(4, free=[t_mv])
        t = head_norm(banks(2, 2).rearrange("p (h d) -> p h d", d=FOX_D), ka_v[:, :, 0:FOX_D], 16, FOX_D, 24,
                      [t_k, dve.now], qsq)
        vt = carve(A_V, TB, 512)
        t_vt = s(vt, ps[:, 4:6, :], ACT.Copy, w=[t_v, t_mk])
        bandsT = carve(A_P, TB, 4, S)
        t_bw = fetch("pool_tables_loaded", [(bandsT, a["bands"]), (zs[:, 0:512], a["w_pool"])], w=[*everything()])
        t_p = gemm_chunk(6, free=[t_cum, t_mv])
        pin = carve(A_PIN, TB, 512)
        t_pin = s(pin, ps[:, 6:8, :], ACT.Copy, w=[t_p])
        qT, kT = carve(A_QT, FOX_H, S, parts=FOX_A), carve(A_KT, FOX_H, S, parts=FOX_A)
        t_qT = head_transposes(qT, [[qa[:, tb, hh, :] for tb in range(TB)] for hh in range(FOX_H)], 0, FOX_A,
                               cols[0:FOX_A, C_FOXQ:C_FOXQ + 1], [t, t_cs, act.now])
        t_kT = head_transposes(kT, [[ka[:, tb, hh, :] for tb in range(TB)] for hh in range(FOX_H)], 4, FOX_A,
                               cols[0:FOX_A, C_FOXK:C_FOXK + 1], [t, act.now])
        mixT = carve(A_MIX, 4, S)
        wait(PE, t_bw, t_pin, act.now, dve.now)
        for g in range(4):
            o = ps[:, g // 2, (g % 2) * S:(g % 2) * S + S]
            for sbk in range(TB):
                ins = mm(o, pin[:, sbk, g * P:g * P + P], bandsT[:, sbk, g, :], sbk == 0, sbk == 1)
        t = done(ins)
        t = s(mixT, banks(0, 2).rearrange("p (g n) -> p g n", g=4), ACT.Copy, w=[t])
        wait(PE, t)
        for g in range(4):
            ins = mm(ps[:, 2 + g // 2, (g % 2) * S:(g % 2) * S + S], zs[:, g * P:g * P + P], mixT[:, g, :])
        t = done(ins)
        t = v("tt", mixT, banks(2, 2).rearrange("p (g n) -> p g n", g=4),
              cols[:, C_PS:C_PS + 4].unsqueeze(2).to_broadcast([P, 4, S]), ALU.mult, w=[t])
        t_cat1 = split(xh[:, 4:8], xl[:, 4:8], mixT, [t, *last_use()])
        x_written[1] = t_cat1, act.now

        prob = carve(A_P, TB, FOX_H, S)
        rows, t_exp = {}, {}
        wait(PE, t_qT, t_kT, *others())
        for tb in (1, 0):
            ns = P * (tb + 1)
            b0 = 4 * (1 - tb)
            for hh in range(FOX_H):
                o = ps[:, b0 + hh // 2, (hh % 2) * S:(hh % 2) * S + ns]
                mm(o, qT[:, hh, tb * P:tb * P + P], kT[:, hh, 0:ns], True, False)
                ins = mm(o[:, ns - P:ns], ident[:], fox_mask, False, True)
            t = done(ins)
            rows[tb] = prob[:, tb, :, 0:ns]
            sc = banks(b0, 4).rearrange("p (h n) -> p h n", h=FOX_H)[:, :, 0:ns]
            t_exp[tb] = softmax_open(v, s, ALU, ACT, AX, sc, rows[tb], stat, 24 * tb, [t, t_cat1, t_qT, t_kT])
        t_prob = {tb: softmax_close(v, ALU, rows[tb], stat, 24 * tb, t_exp[tb]) for tb in (1, 0)}
        pT0, pT1 = carve(A_PT, FOX_H, S), carve(A_PT + 2048, FOX_H, P)
        wait(PE, t_prob[1], t_exp[0])
        for hh in range(FOX_H):
            ins = tr(ps[:, 4 + hh // 4, (hh % 4) * P:(hh % 4) * P + P], prob[:, 1, hh, P:S])
        t_1 = done(ins)
        for hh in range(FOX_H):
            tr(ps[:, hh // 2, (hh % 2) * S + P:(hh % 2) * S + S], prob[:, 1, hh, 0:P])
        wait(PE, t_prob[0])
        for hh in range(FOX_H):
            ins = tr(ps[:, hh // 2, (hh % 2) * S:(hh % 2) * S + P], prob[:, 0, hh, 0:P])
            if hh % 2:
                t = done(ins)
                t = s(pT0[:, hh - 1:hh + 1, :], ps[:, hh // 2, :].rearrange("p (h n) -> p h n", h=2), ACT.Copy,
                      w=[t, pe.now])
        t = t_1
        t1 = v("copy", pT1, banks(4, 2).rearrange("p (h n) -> p h n", h=FOX_H), w=[t])
        wait(PE, t1, act.now)
        for hh in range(FOX_H):
            o = ps[(hh % 2) * FOX_D:(hh % 2) * FOX_D + FOX_D, 6 + hh // 4, (hh // 2 % 2) * S:(hh // 2 % 2) * S + S]
            mm(o, vt[:, 0, hh * FOX_D:hh * FOX_D + FOX_D], pT0[:, hh, :], True, False)
            ins = mm(o[:, P:S], vt[:, 1, hh * FOX_D:hh * FOX_D + FOX_D], pT1[:, hh, :], False, True)
        t = done(ins)
        foxT = carve(A_QT, 4, S)
        out_free = others()
        t = v("copy", foxT, banks(6, 2).rearrange("p (k n) -> p k n", k=4), w=[t])
        t_cat0 = split(xh[:, 0:4], xl[:, 0:4], foxT, [t, *last_use()])
        x_written[0] = t_cat0, act.now

        def transpose_to_x(src, w, bank, half):
            wait(PE, *w)
            for b in (0, 1):
                k0 = 4 * half + 2 * b
                for k in (k0, k0 + 1):
                    for tb in range(TB):
                        ins = tr(ps[:, bank + b, (k % 2) * S + tb * P:(k % 2) * S + tb * P + P],
                                 src[:, tb, k * P:k * P + P])
                t = done(ins)
                two = slice(k0, k0 + 2)
                t = split(xh[:, two], xl[:, two], ps[:, bank + b, :].rearrange("p (k n) -> p k n", k=2), [t, *last_use()])
            x_written[half] = t, act.now

        def out_proj(free, gate=None, w=()):
            wait(PE, *free)
            for n, (half, c) in enumerate(OUT_ORDER):
                slot = take()
                wait_x(half)
                bh, bl = parts(slot, 4, 512)
                for tb in range(TB):
                    for k in range(4):
                        kk = 4 * half + k
                        ins = mm3(ps[:, 2 * tb + c, :], xh[:, kk, tb * P:tb * P + P], xl[:, kk, tb * P:tb * P + P],
                                  bh[:, k], bl[:, k], half == 1 and k == 0, half == 0 and k == 3)
                used[slot].add(ins)
                pump_to(2 if n == 3 else 3)
            return add_residual([used[slot].now, *w], gate)

        def add_residual(w, gate=None):
            t_rows = {}
            for tb in range(TB):
                y = banks(2 * tb, 2)
                if gate is not None:
                    t = v("tt", gate[1][:, tb], y, gate[0], ALU.mult, w=w)
                    t = v("tt", h[:, tb, :], h[:, tb, :], gate[1][:, tb], ALU.add, w=[t])
                else:
                    t = v("tt", h[:, tb, :], h[:, tb, :], y, ALU.add, w=w)
                t_rows[tb] = [t]
            return t_rows

        t_h = out_proj(out_free)

        norm_to_x(h, cols[:, CQ:CQ + 8], t_h, scr=8192, bank=4)
        t_q = gemm_chunk(0)
        mqn, mqsq = carve(A_V, 8, MEM_D), carve(A_PIN, 8, MEM_D)
        t = head_norm(banks(0, 2).rearrange("p (h d) -> p h d", d=MEM_D), mqn, 8, MEM_D, 8, [t_q], mqsq)
        mqT = carve(A_QT, MEM_H, S)
        t = head_transposes(mqT, [[mqn[:, tb * MEM_H + hh, :] for tb in range(TB)] for hh in range(MEM_H)], 2, P,
                            cols[:, C_MEMQ:C_MEMQ + 1], [t])
        mprob = carve(A_KT, TB, MEM_H, S)
        wait(PE, t)
        t_exp = {}
        for tb in range(TB):
            for hh in range(MEM_H):
                ins = mm(ps[:, 4 + 2 * tb + hh // 2, (hh % 2) * S:(hh % 2) * S + S],
                         mqT[:, hh, tb * P:tb * P + P], mkT[:, hh, :])
            tp = done(ins)
            t_exp[tb] = softmax_open(v, s, ALU, ACT, AX, banks(4 + 2 * tb, 2).rearrange("p (h n) -> p h n", h=MEM_H),
                                     mprob[:, tb], stat, 24 * tb, [tp, t])
        mpT = carve(A_P, TB, MEM_H, S)
        for tb in range(TB):
            wait(PE, softmax_close(v, ALU, mprob[:, tb], stat, 24 * tb, t_exp[tb]))
            t_mp = []
            for mb in range(TB):
                for hh in range(MEM_H):
                    ins = tr(ps[:, 2 * mb + hh // 2, (hh % 2) * S + tb * P:(hh % 2) * S + tb * P + P],
                             mprob[:, tb, hh, mb * P:mb * P + P])
                t_mp.append(done(ins))
        for mb in range(TB):
            src = banks(2 * mb, 2).rearrange("p (h n) -> p h n", h=MEM_H)
            w = [t_mp[mb]]
            t = s(mpT[:, mb], src, ACT.Copy, w=w) if mb == 0 else v("copy", mpT[:, mb], src, w=w)
        wait(PE, dve.now, act.now)
        for hh in range(MEM_H):
            o = ps[:, 4 + hh // 2, (hh % 2) * S:(hh % 2) * S + S]
            for mb in range(TB):
                ins = mm(o, mv[:, mb, hh * MEM_D:hh * MEM_D + MEM_D], mpT[:, mb, hh, :], mb == 0, mb == 1)
        t = done(ins)
        moT = carve(A_QT, 4, S)
        t = v("copy", moT, banks(4, 2).rearrange("p (k n) -> p k n", k=4), w=[t])
        t = split(xh[:, 0:4], xl[:, 0:4], moT, [t, *last_use()])
        wait(PE, t, act.now)
        for c in range(2):
            slot = take()
            bh, bl = parts(slot, 4, 512)
            for tb in range(TB):
                for k in range(4):
                    ins = mm3(ps[:, 2 * tb + c, :], xh[:, k, tb * P:tb * P + P], xl[:, k, tb * P:tb * P + P],
                              bh[:, k], bl[:, k], k == 0, k == 3)
            used[slot].add(ins)
        t_h = add_residual([used[slot].now])
        ada_load = [Count(nc, ctx, f"ada_loaded{n}") for n in range(3)]
        ada_done = [Count(nc, ctx, f"ada_summed{n}") for n in range(3)]
        ada = carve(0, 3, SLAB)
        ada_raw = carve(6144, 3, SLAB)
        t_free = everything()
        sil, cc = cols[:, C_SC:C_SC + 8], cols[:, C_CT:C_CT + 8]
        t = s(sil, cc, ACT.Exp, w=[t_col], scale=-1.0)
        t = v("ts", sil, sil, 1.0, None, ALU.add, w=[t])
        t = v("recip", sil, sil, w=[t])
        t_sil = v("tt", sil, sil, cc, ALU.mult, w=[t])
        wait(POOL, *t_free)
        t_y0 = pool.add(POOL.memset(wl[:, 0:2, :].bitcast(f32), 0.0))

        def load_ada(k, n, w=()):
            wait(SP, *w, ada_done[n].now)
            src = a["w_ada"].rearrange("n p m -> (n p) m")[bass.ds((k * 3 + n) * P, P), :]
            ada_load[n].add(SP.dma_start(ada_raw[:, n, :], src), 16)

        def sum_ada(k, n):
            wait(DVE, ada_load[n].now, ada_done[n].now, t_sil)
            ada_done[n].add(DVE.scalar_tensor_tensor(ada[:, n, :], ada_raw[:, n, :], cols[:, bass.ds(C_SC + k, 1)],
                                                     ada[:, n, :], ALU.mult, ALU.add))

        def clear_sums(t_y0):
            wait(PE, t_y0, *others())
            for b in range(4):
                mm(ps[:, b, :], wl[:, 0, 0:P], wl[:, 0:2, :], True, False)

        def slot_ready(slot):
            wait(PE, split_hi[slot].now, split_lo[slot].now)

        def hidden_products(refill):
            wait(PE, z_read.now)
            for half in range(2):
                slot_ready(half)
                wait_x(half)
                used[half].add(gemm_tok(4, half, half, 4 * half, first=half == 0, last=half == 1))
                if half == 0:
                    refill(0)

        def add_products(slot, k0, t_w, stop=False):
            bh, bl = parts(slot, 2, D)
            slot_ready(slot)
            wait(PE, *t_w)
            for tb in range(TB):
                for k in range(2):
                    for half in range(2):
                        n = slice(half * 512, half * 512 + 512)
                        ins = mm3(ps[:, 2 * tb + half, :], wh[:, k0 + k, tb * P:tb * P + P],
                                  wl[:, k0 + k, tb * P:tb * P + P], bh[:, k, n], bl[:, k, n], False, stop and k == 1)
            used[slot].add(ins)

        def ff_step(i, refill, first=False, ada_k=None, ada_next=None):
            t_w = act.now, dve.now
            hidden_products(refill)
            sg = zs[:, 0:512].rearrange("p (b n) -> p b n", b=TB)
            hid = zs[:, 512:1024].rearrange("p (b n) -> p b n", b=TB)
            t = s(sg, ps[:, 4:6, 0:FF_C], ACT.Silu, w=[used[1].now, z_read.now])
            wait(DVE, t, pe.now)
            z_read.add(DVE.tensor_tensor(hid, sg, ps[:, 4:6, FF_C:512], ALU.mult))
            refill(1)
            if not first:
                add_products(2, 0, t_w)
            wait(PE, z_read.now, *t_w)
            for k in range(2):
                for tb in range(TB):
                    ins = tr(ps[:, 6, k * S + tb * P:k * S + tb * P + P], hid[:, tb, k * P:k * P + P])
            t = done(ins)
            if not first:
                refill(2)
            src = ps[:, 6, :].rearrange("p (k n) -> p k n", k=2)
            split(wh[:, 0:2], wl[:, 0:2], src, [t])
            if ada_k is not None:
                for n in range(3):
                    sum_ada(ada_k, n)
                    if ada_next is not None:
                        load_ada(ada_next, n)

        def later(slot):
            pass

        def pumped(slot, at_most=99):
            assert plan[at["use"]][2] == slot
            at["use"] += 1
            pump(at_most)

        def at_loop(n_steps, per_step):
            for k in at:
                at[k] += n_steps * per_step

        clear_sums(t_y0)
        norm_to_x(h, cols[:, CF:CF + 8], t_h, scr=12288, bank=4)
        for n in range(3):
            ada_done[n].add(POOL.memset(ada[:, n, :], 0.0))
        for n in range(3):
            load_ada(0, n, t_free)
        pump()
        ff_step(0, pumped, first=True)
        FF_L = FF_N - 4
        assert at["split"] == at["use"] + 3 and at["load"] == at["use"] + 6
        steps = {act: 2, dve: 1, pe: 1, z_read: 1, **{used[n]: 1 for n in range(3)},
                 **{load[n]: 16 for n in range(3)}, **{split_hi[n]: 1 for n in range(3)},
                 **{split_lo[n]: 1 for n in range(3)}, **{c: 16 for c in ada_load}, **{c: 1 for c in ada_done}}
        with loop(nc, FF_L, steps) as j:
            def refill(slot, j=j):
                emit_split(slot)
                if slot < 2:
                    emit_load("w_gu", 2 * j + 6 + slot, slot)
                else:
                    emit_load("w_down", j + 2, slot)
            ff_step(j + 1, refill, ada_k=j, ada_next=j + 1)
        at_loop(FF_L, 3)
        for i in range(FF_N - 3, FF_N):
            ff_step(i, lambda slot: pumped(slot, 1), ada_k=i - 1 if i == FF_N - 3 else None)
        add_products(2, 0, [act.now, dve.now], stop=True)
        at["use"] += 1
        t_h = add_residual([used[2].now])

        md = cols[:, C_ADA:C_ADA + 48]
        wait(PE, *(c.now for c in ada_done), *others())
        for j in range(48):
            ins = mm(ps[:, 4, 2 * j:2 * j + 2], ada[:, j // 16, (j % 16) * P:(j % 16) * P + P], ones[:, 0:2])
        t = done(ins)
        t = v("tt", md, md, ps[:, 4, 0:96].rearrange("p (j t) -> p j t", t=2)[:, :, 0], ALU.add, w=[t])
        for c_out, c_g, m in ((C_G1, C_N1, 1), (C_G2, C_N2, 4)):
            t_g = v("stt", cols[:, c_out:c_out + 8], cols[:, C_ADA + 8 * m:C_ADA + 8 * m + 8], 1.0,
                    cols[:, c_g:c_g + 8], ALU.add, ALU.mult, w=[t])

        def spread_gate(m, dst, scr, bank, w):
            diag = carve(scr, KT, P)
            t = v("tt", diag, ident[:].unsqueeze(1).to_broadcast([P, KT, P]),
                  cols[:, C_ADA + 8 * m:C_ADA + 8 * m + 8].unsqueeze(2).to_broadcast([P, KT, P]), ALU.mult, w=w)
            wait(PE, t, *others())
            for half in range(2):
                ins = mm(ps[:, bank + half, :], ones[:], carve(scr, TB, 512)[:, half, :])
            t = done(ins)
            return s(dst, banks(bank, 2), ACT.Copy, w=[t])

        B_VSB, B_OML, B_VML, B_CV, B_PRE, B_QT, B_KT, B_QN, B_Y, B_ST = (
            0, 1024, 2048, 3088, 5136, 7208, 9256, 11304, 13352, 15400)
        t_all = everything()
        c2 = {n: wf[:, k * P:k * P + P] for k, n in enumerate(("ml_mask", "sb_keep", "sb_mask", "after"))}
        t_c2 = fetch("block2_constants_loaded", [(c2[n], a[n]) for n in c2] +
                     [(carve(B_ST, KT, 8), a["w_if"])], w=t_all)
        norm_to_x(h, cols[:, C_G1:C_G1 + 8], t_h, t_g, shift=cols[:, C_ADA:C_ADA + 8], scr=B_QT, bank=0)

        def gemm_feat(bank, free=()):
            wait(PE, *free)
            pump_to(2)
            slots = (take(), take())
            if not {slot for _, _, slot in plan[at["split"]:at["use"] + 2]} & set(slots):
                pump_to(2)
            pq = [parts(sl, 4, 512) for sl in slots]
            for m in range(4):
                for k in range(KT):
                    if k % 4 == 0:
                        wait_x(k // 4)
                    bh, bl = pq[k // 4]
                    col = slice(m * P, m * P + P)
                    ins = mm3(ps[:, bank + m // 2, (m % 2) * S:(m % 2) * S + S], bh[:, k % 4, col], bl[:, k % 4, col],
                              xh[:, k, :], xl[:, k, :], k == 0, k == KT - 1)
                    if m == 3 and k == 3:
                        used[slots[0]].add(ins)
            return used[slots[1]].add(ins)

        pre = carve(B_PRE, 8, S + CONV - 1)
        conv = carve(B_CV, 8, S)
        t_z = v("set", pre[:, :, 0:CONV - 1], 0.0, w=t_all)
        for c in range(2):
            t = gemm_feat(2 * c)
            t_pre = s(pre[:, 4 * c:4 * c + 4, CONV - 1:], banks(2 * c, 2).rearrange("p (k n) -> p k n", k=4),
                      ACT.Copy, w=[t, t_z])
            pump_to(2)
        t_if = small_products([split(wsm_h[:], wsm_l[:], carve(B_ST, KT, 8), [t_c2, *t_all])])
        gt = carve(B_ST + 64, TB, 8)
        t = v("copy", gt, ps[:, 7, 0:16].rearrange("p (b h) -> p b h", b=TB), w=[t_if])
        wait(PE, t)
        for m in range(2):
            for tb in range(TB):
                ins = tr(ps[0:ML_H, 6, m * S + tb * P:m * S + tb * P + P], gt[:, tb, m * ML_H:m * ML_H + ML_H])
        t_gr = done(ins)
        t_qs = gemm_chunk(4)
        rows = lambda n: carve(B_Y + n * S, S, parts=ML_H)
        fr, le, cumA, er, cm, em, on4 = (rows(n) for n in range(7))
        t1 = v("set", on4, 1.0, w=t_all)
        t = v("ts", fr, ps[0:ML_H, 6, S:2 * S], cols[0:ML_H, C_BG + 1:C_BG + 2], None, ALU.add, w=[t_gr, *t_all])
        t = log_sigmoid_pieces(v, s, ALU, ACT, fr, le, [t, *t_all])
        t = v("stt", fr, fr, 0.0, le, ALU.min, ALU.subtract, w=[t])
        t = v("scan", cumA, on4, fr, 0.0, ALU.mult, ALU.add, w=[t, t1])
        t = v("stt", er, ps[0:ML_H, 6, 0:S], cols[0:ML_H, C_BG:C_BG + 1], cumA, ALU.add, ALU.subtract, w=[t])
        t = v("scan", cm, on4, er, 0.0, ALU.mult, ALU.max, w=[t])
        t = v("tt", le, cumA, cm, ALU.add, w=[t])
        t_em = s(em, le, ACT.Exp, w=[t], scale=-1.0)
        t_ncm = v("ts", cm, cm, -1.0, None, ALU.mult, w=[t])
        t_ks = gemm_chunk(0, free=[t_pre])
        qn, kn = carve(B_QN, 16, SB_D), carve(B_QN + 1024, 16, SB_D)
        t_qn = head_norm(banks(4, 2).rearrange("p (h d) -> p h d", d=SB_D), qn, 16, SB_D, 8, [t_qs], carve(B_QT, 16, SB_D))
        def convolve(tiles):
            for k in tiles:
                w4 = [cols[:, C_CONV + 4 * k + j:C_CONV + 4 * k + j + 1] for j in range(CONV)]
                t = v("ts", conv[:, k], pre[:, k, 0:S], w4[0], None, ALU.mult, w=[t_pre, *t_all])
                for j in range(1, CONV):
                    t = v("stt", conv[:, k], pre[:, k, j:j + S], w4[j], conv[:, k], ALU.mult, ALU.add, w=[t])
            return t

        t_vm = gemm_chunk(2)
        convolve((0, 1, 2))
        t_kn = head_norm(banks(0, 2).rearrange("p (h d) -> p h d", d=SB_D), kn, 16, SB_D, 24, [t_ks, dve.now],
                         carve(B_QT, 16, SB_D))
        t_vs = gemm_chunk(6, free=[t_em, t_ncm])
        convolve((3, 4, 5))
        vml = carve(B_VML, TB, ML_H, ML_D + 1)
        t_vml = s(vml[:, :, :, 0:ML_D], ps[:, 2:4, :].rearrange("p b (h d) -> p b h d", d=ML_D), ACT.Copy, w=[t_vm, *t_all])
        t_one = v("set", vml[:, :, :, ML_D:ML_D + 1], 1.0)
        vsb = carve(B_VSB, TB, 512)
        t_vsb = s(vsb, ps[:, 6:8, :], ACT.Copy, w=[t_vs, *t_all])
        t_om = gemm_chunk(4, free=[t_qn])
        t_cv = s(conv, conv, ACT.Silu, w=[convolve((6, 7))])
        oml = carve(B_OML, TB, 512)
        t_om_read = s(oml, ps[:, 4:6, :], ACT.Exp, w=[t_om, *t_all], scale=-1.0)

        qT2, kT2 = carve(B_QT, SB_H, S, parts=SB_D), carve(B_KT, SB_H, S, parts=SB_D)
        w = [t_qn, t_kn, t_cs, t_vml, t_vsb]
        for dst, srcn, col in ((qT2, qn, C_SBQ), (kT2, kn, C_SBK)):
            t = head_transposes(dst, [[srcn[:, tb * SB_H + hh, :] for tb in range(TB)] for hh in range(SB_H)],
                                0 if dst is qT2 else 4, SB_D, cols[0:SB_D, col:col + 1], w)
            w = [t_om_read]
        COLS = S + P
        sel4 = wf[0:ML_H, 512:1024].rearrange("p (a b) -> p a b", a=ML_H)
        esel = zs[0:ML_H, :].rearrange("p (a b) -> p a b", a=ML_H)
        id4 = ident[0:ML_H, 0:ML_H]
        t = v("copy", sel4, id4.unsqueeze(2).to_broadcast([ML_H, ML_H, P]), w=[t_kn])
        t = v("tt", esel, id4.unsqueeze(2).to_broadcast([ML_H, ML_H, S]),
              er.unsqueeze(1).to_broadcast([ML_H, ML_H, S]), ALU.mult)
        wait(PE, t, t_ncm, t_em, t1, t_c2, *others())
        for hh in range(ML_H):
            o = ps[:, hh, :]
            for sbk, (c0, c1, t0) in enumerate(((0, S, 0), (S, COLS, P))):
                mm(o[:, c0:c1], esel[:, hh, sbk * P:sbk * P + P], on4[:, t0:S], True, False)
                mm(o[:, c0:c1], sel4[:, hh, :], cm[:, t0:S], False, False)
                ins = mm(o[:, c0:c0 + P], ident[:], c2["ml_mask"], False, True)
            t_arg = done(ins)
            o = ps[:, 4 + hh, :]
            mm(o[:, 0:S], conv[:, 4 + hh, 0:P], conv[:, hh, :])
            t_s = done(mm(o[:, S:COLS], conv[:, 4 + hh, P:S], conv[:, hh, P:S]))
        wml = carve(B_PRE, ML_H, COLS)
        heads = lambda b: banks(b, 4).rearrange("p (h n) -> p h n", h=4)[:, :, 0:COLS]
        t = s(wml, heads(0), ACT.Exp, w=[t_arg])
        t_oml = s(oml, oml, ACT.Ln, bias=1.0)
        t_oml = s(oml, oml, ACT.Exp, w=[t_oml], scale=-1.0)
        t = v("stt", wml, heads(4), ML_D ** -0.5, wml, ALU.mult, ALU.mult, w=[t, t_s])
        wait(PE, t, t_one, t_vml)
        for tb in range(TB):
            ins = tr(ps[:, 7, 260 + 4 * tb:264 + 4 * tb], em[:, tb * P:tb * P + P])
        for tb in range(TB):
            for hh in range(ML_H):
                o = ps[:, 4 + 2 * tb + hh // 2, (hh % 2) * 129:(hh % 2) * 129 + 129]
                mm(o, wml[:, hh, tb * P:tb * P + P], vml[:, 0, hh, :], True, tb == 0)
                if tb:
                    ins = mm(o, wml[:, hh, S:COLS], vml[:, 1, hh, :], False, True)
        t = done(ins)
        share, keep, arg = (carve(at, 2, 2, COLS) for at in (B_CV, B_CV + 1536, B_QN))
        bank2 = lambda b: ps[:, b:b + 2, 0:COLS]

        def sb_scores(g):
            for hh in range(2):
                o, k = ps[:, 2 * (g % 2) + hh, :], 2 * g + hh
                mm(o[:, 0:S], kT2[:, k, 0:P], qT2[:, k, :])
                ins = mm(o[:, S:COLS], kT2[:, k, P:S], qT2[:, k, P:S])
            return done(ins)

        def sb_share(g, t_z, w):
            return log_sigmoid_pieces(v, s, ALU, ACT, bank2(2 * (g % 2)), share[:, g % 2], [t_z, w])

        def sb_keep(g, t):
            n, z = g % 2, bank2(2 * (g % 2))
            t = v("stt", keep[:, n], z, 0.0, share[:, n], ALU.max, ALU.add, w=[t, pe.now])
            t_arg = v("stt", arg[:, n], z, 0.0, share[:, n], ALU.min, ALU.subtract)
            diag = keep[:, n].rearrange("p h (m n) -> p h m n", m=3)[:, :, 0:3:2, :]
            t = v("tt", diag, diag, c2["sb_keep"].unsqueeze(1).unsqueeze(1).to_broadcast([P, 2, 2, P]), ALU.mult, w=[t])
            return t, t_arg

        t_num = t
        t_z = [sb_scores(0), sb_scores(1)]
        t_share = [sb_share(g, t_z[g], dve.now) for g in range(2)]
        t = t_num
        num = banks(4, 4).rearrange("p (b n) -> p b n", b=4)[:, :, 0:258].rearrange("p b (h d) -> p b h d", d=129)
        emc = carve(B_ST, 8)
        den = carve(B_ST + 8, 8)
        t1 = v("copy", emc, ps[:, 7, 260:268], w=[t])
        den4 = den.rearrange("p (b h) -> p b h", h=2)
        t2 = v("copy", den4, num[:, :, :, ML_D], w=[t])
        t2 = v("stt", den, den, -1.0, den, ALU.mult, ALU.max, w=[t2])
        t2 = v("tt", den, den, emc, ALU.max, w=[t1, t2])
        t2 = v("recip", den, den, w=[t2])
        mix = carve(B_Y, TB, D)
        yml = carve(B_CV + 3072, 8, ML_D)
        t2 = v("tt", yml.rearrange("p (b h) d -> p b h d", h=2), num[:, :, :, 0:ML_D],
               den4.unsqueeze(3).to_broadcast([P, 4, 2, ML_D]), ALU.mult, w=[t2])
        made = {0: sb_keep(0, t_share[0])}
        t_go = fetch("output_gains_loaded", [(zs[:], a["g_out"])], w=everything())
        t_n = head_norm(yml, yml, 8, ML_D, 8, [t2], carve(B_VML, 8, ML_D))
        yml4 = yml.rearrange("p (b h) d -> p b (h d)", b=TB)
        t = v("tt", oml, oml, zs[:, 512:1024].unsqueeze(1).to_broadcast([P, TB, 512]), ALU.mult, w=[t_go, t_oml])
        t_yml = v("tt", mix[:, :, 512:1024], yml4, oml, ALU.mult, w=[t_n, t])

        def norm_pair(g):
            own, n = mix[:, :, g * P:g * P + P], 4 * (g % 2)
            own4 = own.rearrange("p b (h d) -> p b h d", h=2)
            sq = carve(B_QN + 1536, TB, P)
            t = s(sq, own, ACT.Square, w=[dve.now])
            t = v("red", stat[:, 8 + n:12 + n], sq.rearrange("p b (h d) -> p (b h) d", h=2), AX.X, ALU.add, w=[t])
            t = rstd(4, SB_D, 8 + n, [t])
            t = v("tt", own4, own4, stat[:, 8 + n:12 + n].rearrange("p (b h) -> p b h", h=2).unsqueeze(3).to_broadcast(
                [P, TB, 2, SB_D]), ALU.mult, w=[t])
            return v("tt", own, own, zs[:, g * P:g * P + P].unsqueeze(1).to_broadcast([P, TB, P]), ALU.mult, w=[t, t_go])

        made[1] = sb_keep(1, t_share[1])
        wait(PE, t2)
        t_evac = {}
        for g in range(SB_H // 2):
            n = g % 2
            t_keep, t_arg = made[g]
            wait(PE, t_keep, t_evac.get(g - 2))
            for hh in range(2):
                o = ps[:, 4 + 2 * n + hh, :]
                mm(o[:, 0:S], c2["after"], keep[:, n, hh, 0:S], True, False)
                mm(o[:, P:S], ones[:], keep[:, n, hh, S:COLS], False, False)
                mm(o[:, 0:P], ident[:], c2["sb_mask"], False, True)
                mm(o[:, S:COLS], c2["after"], keep[:, n, hh, S:COLS], True, False)
                ins = mm(o[:, S:COLS], ident[:], c2["sb_mask"], False, True)
            t = done(ins)
            t = t_sums_read = v("tt", arg[:, n], arg[:, n], bank2(4 + 2 * n), ALU.subtract, w=[t, t_arg])
            t = s(arg[:, n], arg[:, n], ACT.Exp, w=[t])
            if g + 2 < SB_H // 2:
                wait(PE, t_arg)
                t_next = sb_scores(g + 2)
            wait(PE, t)
            for hh in range(2):
                k = 2 * g + hh
                for tb in range(TB):
                    o = ps[:, 4 + 2 * n + hh, COLS + tb * SB_D:COLS + tb * SB_D + SB_D]
                    mm(o, arg[:, n, hh, tb * P:tb * P + P], vsb[:, 0, k * SB_D:k * SB_D + SB_D], True, tb == 0)
                    if tb:
                        ins = mm(o, arg[:, n, hh, S:COLS], vsb[:, 1, k * SB_D:k * SB_D + SB_D], False, True)
            t_out = done(ins)
            if g + 2 < SB_H // 2:
                made[g + 2] = sb_keep(g + 2, sb_share(g + 2, t_next, dve.now))
            if g:
                norm_pair(g - 1)
            src = ps[:, 4 + 2 * n:6 + 2 * n, COLS:512].rearrange("p h (b d) -> p b h d", b=TB)
            for tb in range(TB):
                t = v("copy", mix[:, tb, g * P:g * P + P].rearrange("p (h d) -> p h d", d=SB_D), src[:, tb], w=[t_out])
            t_evac[g] = t
        transpose_to_x(mix, [t_yml, t_sums_read], 0, 1)
        t = norm_pair(SB_H // 2 - 1)
        transpose_to_x(mix, [t], 2, 0)
        banks03_read = others()
        g1 = carve(B_CV, D)
        t_g1 = spread_gate(2, g1, B_CV + 1024, 4, [*everything()])
        t_h = out_proj([*banks03_read], gate=(g1, carve(B_QN, TB, D)), w=[t_g1])

        R_SK, R_SC, R_QT = 0, 2048, 14336
        v("copy", key4[:], iota[:].unsqueeze(2).to_broadcast([P, NKEYS, 4]), w=[t_col])
        sk = carve(R_SK, PEER_H * 2, NKEYS)
        t_sk = fetch("sub_keys_loaded", [(carve(R_SK, SLAB), a["sub_keys"])], w=everything())
        norm_to_x(h, cols[:, C_G2:C_G2 + 8], t_h, shift=cols[:, C_ADA + 24:C_ADA + 32], scr=8192, bank=0)
        scores = carve(R_SC, TB, 2 * PEER_H, NKEYS)
        wait(PE, t_sk)
        query_read, score_read = [], []

        NEG = -3.0e38
        U = lambda x: x.bitcast(u32)
        tv = carve(6144, TB, 2 * PEER_H, TOPK)
        ti = carve(6656, TB, 2 * PEER_H, TOPK)
        tf = carve(7168, TB, 2 * PEER_H, TOPK)
        bv = carve(7680, TB, PEER_H, TOPK)
        bp = carve(7936, TB, PEER_H, TOPK)
        sa, sbb, sg_ = carve(8704, TB, SEL), carve(8960, TB, SEL), carve(9216, TB, SEL)
        FULL, PART = 4, 4
        CANDS = FULL * TOPK + (TOPK - FULL) * PART
        cand = carve(9728, TB, 2, CANDS)

        def top16(rows, w):
            t = w
            for values, v16, _ in rows:
                t_last = v("max", v16[:, 0:8], values, w=t)
                t = []
            for values, v16, i16 in rows:
                t_idx = v("idx", U(i16[:, 0:8]), v16[:, 0:8], values, w=[t_last])
            for values, v16, _ in rows:
                t_last = v("repl", values, v16[:, 0:8], values, NEG, w=[t_idx])
            for values, v16, _ in rows:
                t_max = v("max", v16[:, 8:16], values, w=[t_last])
            for values, v16, i16 in rows:
                t_idx = v("idx", U(i16[:, 8:16]), v16[:, 8:16], values, w=[t_max])
            return t_idx

        def choose(c, w):
            halves = range(4 * c, 4 * c + 4)
            t = top16([(scores[:, tb, m, :], tv[:, tb, m, :], ti[:, tb, m, :]) for tb in range(TB) for m in halves], w)
            for tb in range(TB):
                tvh = tv[:, tb, 4 * c:4 * c + 4].rearrange("p (h m) k -> p h m k", m=2)
                for at0, i0, i1, nj in ((0, 0, FULL, TOPK), (FULL * TOPK, FULL, TOPK, PART)):
                    shape = [P, 2, i1 - i0, nj]
                    t_cand = v("tt", cand[:, tb, :, at0:at0 + (i1 - i0) * nj].rearrange("p h (i j) -> p h i j", j=nj),
                               tvh[:, :, 0, i0:i1].unsqueeze(3).to_broadcast(shape),
                               tvh[:, :, 1, 0:nj].unsqueeze(2).to_broadcast(shape), ALU.add, w=[t])
            return top16([(cand[:, tb, hh, :], bv[:, tb, 2 * c + hh, :], bp[:, tb, 2 * c + hh, :])
                          for tb in range(TB) for hh in range(2)], [t_cand])

        def queries(c):
            t = gemm_feat(2 * (c % 2), free=query_read[c - 2:c - 1])
            qT3 = carve(R_QT + 1024 * (c % 2), 4, S)
            t = s(qT3, banks(2 * (c % 2), 2).rearrange("p (k n) -> p k n", k=4), ACT.Copy, w=[t, pe.now, *t_free])
            query_read.append(t)
            pump_to(3)
            return qT3, t

        t_free = everything()
        ready = queries(0)
        for c in range(4):
            qT3, t = ready
            if c < 3:
                ready = queries(c + 1)
            wait(PE, t, *score_read[c - 2:c - 1], *t_free)
            for tb in range(TB):
                for m in range(4):
                    ins = mm(ps[:, 4 + 2 * (c % 2) + tb, m * P:m * P + P], qT3[:, m, tb * P:tb * P + P],
                             sk[:, 4 * c + m, :])
            t = t_scored = done(ins)
            b = 4 + 2 * (c % 2)
            t_sc = v("copy", scores[:, :, 4 * c:4 * c + 4, :], ps[:, b:b + 2, :].rearrange("p b (m n) -> p b m n", m=4),
                     w=[t])
            score_read.append(t_sc)
            t_best = choose(c, [t_sc, *t_free])

        wait(PE, *others())
        pump()
        hidden_products(later)
        at["use"] += 2

        places = lambda n: carve(10240 + n * TB * SEL, TB, PEER_H, TOPK)
        for n, (op, k) in enumerate(((ALU.logical_shift_right, 4), (ALU.logical_shift_right, 2), (ALU.bitwise_and, 12),
                                     (ALU.bitwise_and, 3))):
            t = v("ts", U(places(n)), U(bp), k, None, op, w=[t_best])
        t_tf = v("copy", tf, U(ti))
        for n in range(4):
            t = v("copy", places(4 + n), U(places(n)), w=[t])
        t = v("copy", places(8), U(bp))
        by_16, by_4, mid, low_2, whole = (places(4 + n) for n in range(5))
        of_i, of_j = (carve(12544 + 128 * n, 128).bitcast(bf16).rearrange("p (b h k) -> p b h k", b=TB, h=PEER_H)
                      for n in range(2))
        t_i = v("stt", of_i, by_4, float(FULL - TOPK), by_16, ALU.add, ALU.max, w=[t])
        t_j = v("stt", mid, whole, float(FULL * TOPK), mid, ALU.is_lt, ALU.mult, w=[t])
        t_j = v("tt", of_j, mid, low_2, ALU.add, w=[t_j])
        def selection(bank, src, t, dst):
            wait(PE, t)
            for tb in range(TB):
                ins = tr(ps[:, bank, tb * P:tb * P + P], src[:, tb, :])
            return s(dst, ps[:, bank, 0:S], ACT.Copy, w=[done(ins)])

        bvf = bv.rearrange("p b h k -> p (b h) k")
        sgf = sg_.rearrange("p b (h k) -> p (b h) k", h=PEER_H)
        t1 = v("tt", sgf, bvf, bvf[:, :, 0:1].to_broadcast([P, 16, TOPK]), ALU.subtract)
        t1 = s(sgf, sgf, ACT.Exp, w=[t1])
        t1 = v("red", stat[:, 8:24], sgf, AX.X, ALU.add, w=[t1])
        t1 = v("recip", stat[:, 8:24], stat[:, 8:24], w=[t1])
        t1 = v("tt", sgf, sgf, stat[:, 8:24].unsqueeze(2).to_broadcast([P, 16, TOPK]), ALU.mult, w=[t1])
        t_g = selection(2, sg_, t1, zs[:, 0:S])

        def part_gates(t):
            rest = zs[:, 0:S]
            for n in range(3):
                t = s(gate_parts[:, n, :], rest, ACT.Copy, w=[t])
                if n < 2:
                    left = zs[:, (n + 1) * S:(n + 2) * S]
                    t = v("tt", left, rest, gate_parts[:, n, :], ALU.subtract, w=[t])
                    rest = left

        count = carve(12800, 128).bitcast(bf16).rearrange("p (i k) -> p i k", i=TOPK)
        t = v("copy", count, iota[:, 0:TOPK].unsqueeze(2).to_broadcast([P, TOPK, TOPK]), w=[t_i, t_j])
        hit = carve(13056, 1024).bitcast(bf16).rearrange("p (h i k) -> p h i k", h=PEER_H, i=TOPK)
        key = carve(R_SK, PEER_H, TOPK, TOPK)
        shape = [P, PEER_H, TOPK, TOPK]
        for src, m, dst in ((of_i, 0, sa), (of_j, 1, sbb)):
            for tb in range(TB):
                tfh = tf[:, tb].rearrange("p (h m) k -> p h m k", m=2)
                t = v("tt", hit, count.unsqueeze(1).to_broadcast(shape), src[:, tb].unsqueeze(2).to_broadcast(shape),
                      ALU.is_equal, w=[t, t_tf, t_scored])
                t = v("tt", key, hit, tfh[:, :, m, :].unsqueeze(3).to_broadcast(shape), ALU.mult, w=[t])
                t = v("red", dst[:, tb, :].rearrange("p (h k) -> p h k", h=PEER_H), key.rearrange("p h i k -> p h k i"),
                      AX.X, ALU.add, w=[t])
            t_sel = selection(m, dst, t, {0: sel_a, 1: sel_b}[m][:])
            if m == 0:
                part_gates(t_g)

        G = arena[:, :].rearrange("p (a t) -> p a t", a=HALF_A)
        hit_b = zs[:].bitcast(bf16).rearrange("p (n g b t) -> p n g b t", n=2, g=2, t=4)
        first = wf[:].bitcast(bf16)
        hit_a = first[:, 0:512].rearrange("p (g a t) -> p g a t", g=2, t=4)
        gated = first[:, 512:2048].rearrange("p (g q a t) -> p g q a t", g=2, q=3, t=4)
        hits_used = [[Count(nc, ctx, f"hits_used{n}{g}") for g in range(2)] for n in range(2)]
        g_read = [Count(nc, ctx, f"gate_bank_read{n}") for n in range(2)]
        for c in (*hits_used[0], *hits_used[1], *g_read):
            wait(POOL, pool.now)
            c.add(POOL.memset(minus_half[:, 0:1], -0.5))
            pool.add(POOL.memset(minus_half[:, 1:2], -0.5))

        def build_gates(half):
            keys_a = key4[:, half * HALF_A:half * HALF_A + HALF_A, :]
            steps = {dve: 10, **{c: 1 for used_n in hits_used for c in used_n}, **{c: 1 for c in g_read}}
            with loop(nc, S // 16, steps) as i:
                t_gated = dve.now
                for n in range(2):
                    t0 = i * 16 + n * 8
                    of_tokens = lambda x: x[:, bass.ds(t0, 8)].rearrange("p (g t) -> p g t", g=2).unsqueeze(2)
                    shape = [P, NKEYS, 4]
                    find_b = lambda g, w=(): v("tt", hit_b[:, n, g], key4[:],
                                               sel_b[:, bass.ds(t0 + 4 * g, 4)].unsqueeze(1).to_broadcast(shape),
                                               ALU.is_equal, w=w)
                    find_b(0, w=[hits_used[n][1].now])
                    t_a = v("tt", hit_a, keys_a.unsqueeze(1).to_broadcast([P, 2, HALF_A, 4]),
                            of_tokens(sel_a).to_broadcast([P, 2, HALF_A, 4]), ALU.is_equal, w=[t_gated])
                    find_b(1)
                    shape = [P, 3, HALF_A, 4]
                    for g in range(2):
                        t = v("tt", gated[:, g], hit_a[:, g].unsqueeze(1).to_broadcast(shape),
                              gate_parts[:, :, bass.ds(t0 + 4 * g, 4)].unsqueeze(2).to_broadcast(shape), ALU.mult,
                              w=[t_a, hits_used[1 - n][g].now])
                        t_gated = t
                        wait(PE, t, g_read[n].now)
                        for j in range(4):
                            col = (4 * g + j) * HALF_A
                            for q in range(3):
                                ins = mm(ps[:, 6 + n, col:col + HALF_A], hit_b[:, n, g, :, j], gated[:, g, q, :, j],
                                         q == 0, q == 2)
                        hits_used[n][g].add(ins)
                    wait(ACTE, hits_used[n][1].now)
                    g_read[n].add(ACTE.activation(G[:, :, bass.ds(t0, 8)],
                                                  ps[:, 6 + n, :].rearrange("p (t a) -> p a t", t=8), ACT.Copy))

        def weigh_start(c_local, t_w):
            wait(PE, z_read.now, *t_w)
            for m in range(EX_A):
                for tb in range(TB):
                    ins = tr(ps[:, 6 + m // 2, (m % 2) * S + tb * P:(m % 2) * S + tb * P + P],
                             zs[:, tb * 512 + m * P:tb * 512 + m * P + P])
            t = s(wf[:], banks(6, 2), ACT.Gelu, w=[done(ins), *t_w])
            w4 = wf[:].rearrange("p (a t) -> p a t", a=EX_A)
            return v("tt", w4, w4, G[:, bass.ds(c_local * EX_A, EX_A), :], ALU.mult, w=[t])

        def weigh_end(t, w=()):
            split(wh[:], wl[:], wf[:].rearrange("p (a t) -> p a t", a=EX_A), [t, *w])

        def ex_step(c_local, refill, hidden=True):
            t_w = act.now, dve.now
            if hidden:
                hidden_products(refill)
            else:
                refill(0)
            wait(ACTE, used[1].now, pe.now)
            z_read.add(ACTE.activation(zs[:], banks(4, 2), ACT.Copy))
            refill(1)
            add_products(2, 0, t_w)
            refill(2)
            t = weigh_start(c_local, t_w)
            add_products(3, 2, t_w)
            weigh_end(t, [used[3].now])
            refill(3)

        def ex_open():
            t_w = (*everything(), *(c.now for c in g_read))
            wait(ACTE, *t_w)
            z_read.add(ACTE.activation(zs[:], banks(4, 2), ACT.Copy))
            pump(2)
            weigh_end(weigh_start(0, t_w))
            pump()

        wait(POOL, *everything())
        t_y0 = pool.add(POOL.memset(wl[:, 0:2, :].bitcast(f32), 0.0))
        wait(DVE, *everything(), t_sel)
        wait(ACTE, *everything())
        wait(PE, *others())
        build_gates(0)
        clear_sums(t_y0)
        ex_open()
        steps = {act: 2, dve: 2, pe: 1, z_read: 1, **{c: 1 for c in used}, **{c: 16 for c in load},
                 **{c: 1 for c in split_hi}, **{c: 1 for c in split_lo}}

        def ex_loop(first, n, offset):
            assert at["split"] == at["use"] + 4 and at["load"] == at["use"] + 8
            with loop(nc, n, steps) as j:
                def refill(slot, j=j):
                    emit_split(slot)
                    if slot < 2:
                        emit_load("ex_u", 2 * j + (2 * (first + 2) + slot), slot)
                    else:
                        emit_load("ex_v", 2 * j + (2 * (first + 1) + slot - 2), slot)
                ex_step(j + (first - offset), refill)
            at_loop(n, 4)

        ex_loop(1, EX_N // 2 - 1, 0)
        hidden_products(later)
        wait(DVE, act.now, pe.now)
        wait(ACTE, dve.now)
        wait(PE, *others())
        build_gates(1)
        ex_step(0, pumped, hidden=False)
        ex_loop(EX_N // 2 + 1, EX_N // 2 - 3, EX_N // 2)
        for c in (EX_N - 2, EX_N - 1):
            ex_step(c - EX_N // 2, pumped)
        t_w = act.now, dve.now
        add_products(2, 0, t_w)
        add_products(3, 2, t_w, stop=True)
        g2 = carve(0, D)
        t_g2 = spread_gate(5, g2, 1024, 4, everything())
        t_h = add_residual([used[3].now, t_g2], gate=(g2, carve(2048, TB, D)))
        for t in [fetch(f"stored{tb}", [(out[:, tb], h[:, tb])], w=t_h[tb]) for tb in range(TB)]:
            wait(SP, t)


def log_sigmoid_pieces(v, s, ALU, ACT, x, e, w):
    t = s(e, x, ACT.Abs, w=w)
    t = s(e, e, ACT.Exp, w=[t], scale=-1.0)
    return s(e, e, ACT.Ln, w=[t], bias=1.0)


def softmax_open(v, s, ALU, ACT, AX, sc, dst, stat, at0, w):
    n = dst.shape[1]
    t = v("red", stat[:, at0:at0 + n], sc, AX.X, ALU.max, w=w, negate=True)
    for hh in range(n):
        t = s(dst[:, hh], sc[:, hh], ACT.Exp, w=[t, *w] if hh == 0 else [], bias=stat[:, at0 + hh:at0 + hh + 1],
              accum_out=stat[:, at0 + n + hh:at0 + n + hh + 1])
    return t


def softmax_close(v, ALU, dst, stat, at0, t):
    n = dst.shape[1]
    sums = stat[:, at0 + n:at0 + 2 * n]
    t = v("recip", sums, sums, w=[t])
    return v("tt", dst, dst, sums.unsqueeze(2).to_broadcast(list(dst.shape)), ALU.mult, w=[t])


def layout(i):
    def w(x):
        return np.asarray(x)[0] if np.asarray(x).ndim > 2 else np.asarray(x)

    def slabs(m):
        k, n = m.shape
        m = m.reshape(k // 512, 4, P, n // 512, 512).transpose(3, 0, 2, 1, 4)
        return np.ascontiguousarray(m).reshape(-1, P, SLAB)

    def fcols(x):
        return np.asarray(x).reshape(-1, P).T

    def tok(x):
        return np.ascontiguousarray(np.asarray(x).reshape(TB, P, D).transpose(1, 0, 2))

    def rep(x):
        return np.ascontiguousarray(np.broadcast_to(np.asarray(x).reshape(1, -1), (P, np.asarray(x).size)))

    def small(m):
        return np.ascontiguousarray(m.reshape(KT, P, m.shape[1]).transpose(1, 0, 2))

    f4 = np.float32
    cols = np.zeros((P, 192), f4)
    cols[:, 0:8], cols[:, 8:16] = fcols(i["g_mix"]), fcols(i["g_mem_kv"])
    cols[:, 16:24], cols[:, 24:32] = fcols(i["g_mem_q"]), fcols(i["g_ffn"])
    cols[0:64, 32], cols[0:64, 33] = i["g_q_fox"][0], i["g_k_fox"][0]
    cols[64:66, 32:34] = 1
    cols[:, 34], cols[:, 35] = i["g_q_mem"][0], i["g_k_mem"][0]
    cols[:, 36:40] = fcols(i["pool_scale"])
    cols[:, 41:49] = fcols(i["c_2"])
    cols[:, 57:65], cols[:, 65:73] = fcols(i["g_norm1_2"]), fcols(i["g_norm2_2"])
    cols[:, 73:121] = fcols(i["b_ada_2"])
    cols[0:64, 121], cols[0:64, 122] = i["g_q_sb_2"][0], i["g_k_sb_2"][0]
    cols[:, 124:156] = np.asarray(i["conv_w_2"])[0].reshape(CONV, 8, P).transpose(2, 1, 0).reshape(P, 32)
    cols[0:ML_H, 172], cols[0:ML_H, 173] = i["b_igate_2"][0], i["b_fgate_2"][0]

    w_in, w_in2 = w(i["w_in"]), w(i["w_in_2"])
    gu = w(i["w_gate_up"]).reshape(D, 2, FF_N, FF_C).transpose(0, 2, 1, 3).reshape(D, FF_N * 512)
    ada = w(i["w_ada_2"]).reshape(KT, P, 3, SLAB).transpose(0, 2, 1, 3)
    q, k, v_, qk, vm, om = (w_in2[:, x:y] for x, y in
                            ((0, 512), (512, 1024), (1024, 1536), (1536, 2560), (2560, 3072), (3072, 3584)))
    c = constants()
    return {
        "x": tok(i["x"]), "mem": tok(i["mem"]), "cols": cols,
        "ident": c["ident"], "ones": c["ones"], "iota": c["iota"], "fox_mask": c["fox_mask"], "upto": c["upto"],
        "ml_mask": c["ml_mask"], "sb_keep": c["sb_keep"], "sb_mask": c["sb_mask"], "after": c["after"],
        "bands": np.ascontiguousarray(c["bands"]),
        "b_forget": rep(i["b_forget"]), "w_f": small(w_in[:, 2048:2056]), "w_if": small(w_in2[:, 3584:3592]),
        "w_pool": np.ascontiguousarray(w(i["w_pool"]).transpose(1, 0, 2)).reshape(P, 512),
        "g_out": rep(np.concatenate([np.asarray(i["g_out_sb_2"]).ravel(), np.asarray(i["g_out_ml_2"]).ravel()])),
        "sub_keys": np.ascontiguousarray(w(i["sub_keys_2"]).transpose(3, 0, 1, 2)).reshape(P, SLAB),
        "w_mem_kv": slabs(w(i["w_mem_kv"])), "w_in": slabs(w_in[:, 0:2048]), "w_out": slabs(w(i["w_out"])),
        "w_mem_q": slabs(w(i["w_mem_q"])), "w_mem_out": slabs(w(i["w_mem_out"])), "w_gu": slabs(gu),
        "w_down": np.ascontiguousarray(w(i["w_down"]).reshape(FF_N, 2, P, D).transpose(0, 2, 1, 3)).reshape(-1, P, SLAB),
        "w_ada": np.ascontiguousarray(ada).reshape(-1, P, SLAB),
        "w_in_2": slabs(np.concatenate([qk, q, k, vm, v_, om], axis=1)),
        "w_out_2": slabs(w(i["w_out_2"])), "w_q_peer": slabs(w(i["w_q_peer_2"])),
        "ex_u": slabs(w(i["expert_u_2"]).T),
        "ex_v": np.ascontiguousarray(w(i["expert_v_2"]).reshape(-1, 2, P, D).transpose(0, 2, 1, 3)).reshape(-1, P, SLAB),
    }


def kernel(**inputs):
    import concourse.bacc as bacc
    from concourse.bass_utils import run_bass_kernel_spmd

    arrays = layout(inputs)
    nc = bacc.Bacc("TRN2", target_bir_lowering=False, num_devices=1)
    aps = {n: nc.dram_tensor("in_" + n, x.shape, mybir.dt.from_np(x.dtype), kind="ExternalInput").ap()
           for n, x in arrays.items()}
    out = nc.dram_tensor("out", (P, TB, D), mybir.dt.float32, kind="ExternalOutput").ap()
    program(nc, aps, out)
    r = run_bass_kernel_spmd(nc, [{"in_" + n: x for n, x in arrays.items()}], core_ids=[0])
    return np.ascontiguousarray(r.results[0]["out"].transpose(1, 0, 2)).reshape(1, S, D)
```
